# Optimizing a Trainium2 kernel written in Bass

```python
import math
import jax, jax.numpy as jnp
from jax import lax
import numpy as np

D_MODEL = 1024
BATCH = 1
SEQ = 512
DEPTH = 1

CHUNK = 64
D_MIX = D_MODEL
D_CONV = D_MIX // 2
CONV_WIDTH = 31
D_GLA_V = D_MIX - D_CONV
GLA_HEADS = 4
GLA_DV = D_GLA_V // GLA_HEADS
GLA_DK = GLA_DV // 2
D_GLA_K = GLA_HEADS * GLA_DK
GATE_RANK = 16
GATE_TAU = 16.0
SPLIT_SIZES = (D_CONV, D_CONV, D_GLA_K, D_GLA_K, D_GLA_V, D_GLA_V, GATE_RANK)
IN_COLS = sum(SPLIT_SIZES)
N_EXPERTS = 16
N_GROUPS = 4
EXPERTS_PER_GROUP = N_EXPERTS // N_GROUPS
TOP_K = 2
D_EXPERT = 704
EPS = 1e-6

kernel_name = 'hybrid_conv_gla_groupmoe_adaln_block'

def rmsnorm(x, g):
    xf = x.astype(jnp.float32)
    y = xf * lax.rsqrt(jnp.mean(xf * xf, axis=-1, keepdims=True) + EPS)
    return (y * g.astype(jnp.float32)).astype(x.dtype)

def layernorm(x, g, b):
    xf = x.astype(jnp.float32)
    mu = jnp.mean(xf, axis=-1, keepdims=True)
    var = jnp.mean(jnp.square(xf - mu), axis=-1, keepdims=True)
    y = (xf - mu) * lax.rsqrt(var + EPS)
    return (y * g.astype(jnp.float32) + b.astype(jnp.float32)).astype(x.dtype)

def conv_group(val, gate, w_dw, b_dw, ln_g, ln_b):
    u = val * jax.nn.sigmoid(gate)
    u = lax.conv_general_dilated(
        u, w_dw[:, None, :].astype(u.dtype), window_strides=(1,),
        padding=[(CONV_WIDTH - 1, 0)],
        dimension_numbers=('NWC', 'WIO', 'NWC'),
        feature_group_count=D_CONV) + b_dw
    u = layernorm(u, ln_g, ln_b)
    return jax.nn.silu(u)

def gla_group(q, k, v, g, lr, w_up, b_up, norm_g):
    B, S, _ = q.shape
    nc = S // CHUNK
    q = q.reshape(B, nc, CHUNK, GLA_HEADS, GLA_DK) * (GLA_DK ** -0.5)
    k = k.reshape(B, nc, CHUNK, GLA_HEADS, GLA_DK)
    v = v.reshape(B, nc, CHUNK, GLA_HEADS, GLA_DV)
    log_a = jax.nn.log_sigmoid((lr @ w_up + b_up).astype(jnp.float32)) / GATE_TAU
    log_a = log_a.reshape(B, nc, CHUNK, GLA_HEADS, GLA_DK)
    b_cum = jnp.cumsum(log_a, axis=2)
    b_end = b_cum[:, :, -1]
    k_dec = k * jnp.exp(b_end[:, :, None] - b_cum).astype(k.dtype)
    upd = jnp.einsum('bnchk,bnchv->nbhkv', k_dec, v)
    dec = jnp.exp(b_end).astype(upd.dtype).transpose(1, 0, 2, 3)[..., None]

    def step(state, inp):
        d, u = inp
        state = d * state + u
        return state, state

    _, states = lax.scan(step, jnp.zeros_like(upd[0]), (dec, upd))
    o = jnp.einsum('bnchk,nbhkv->bnchv', q, states).reshape(B, S, GLA_HEADS, GLA_DV)
    o = rmsnorm(o, norm_g)
    return o.reshape(B, S, D_GLA_V) * jax.nn.silu(g)

def grouped_moe(h, w_router, b_router, w1, w3, w2):
    B, S, D = h.shape
    hf = h.reshape(B * S, D)
    probs = jax.nn.softmax((hf @ w_router).astype(jnp.float32), axis=-1)
    sel = probs + b_router.astype(jnp.float32)
    grp = sel.reshape(-1, N_GROUPS, EXPERTS_PER_GROUP)
    grp_score = lax.top_k(grp, TOP_K)[0].sum(-1)
    best = jnp.argmax(grp_score, axis=-1)
    in_grp = jax.nn.one_hot(best, N_GROUPS, dtype=jnp.bool_)[..., None]
    masked = jnp.where(in_grp, grp, -jnp.inf).reshape(-1, N_EXPERTS)
    _, idx = lax.top_k(masked, TOP_K)
    w = jnp.take_along_axis(probs, idx, axis=-1)
    w = w / jnp.sum(w, axis=-1, keepdims=True)
    comb = jnp.einsum('tk,tke->te', w, jax.nn.one_hot(idx, N_EXPERTS, dtype=jnp.float32))
    comb = comb.astype(h.dtype)
    y = jnp.zeros_like(hf)
    for e in range(N_EXPERTS):
        he = jax.nn.silu(hf @ w1[e]) * (hf @ w3[e])
        y = y + comb[:, e:e + 1] * (he @ w2[e])
    return y.reshape(B, S, D)

def setup_inputs(seed: int = 0) -> dict:
    key = jax.random.key(seed)
    ks = jax.random.split(key, 24)
    f32 = jnp.float32
    nrm = lambda k, shape, s: jax.random.normal(k, shape, f32) * s
    return {
        'x': nrm(ks[0], (BATCH, SEQ, D_MODEL), 1.0),
        'c': nrm(ks[1], (BATCH, D_MODEL), 1.0),
        'w_ada': nrm(ks[2], (DEPTH, D_MODEL, 6 * D_MODEL), 0.3 * D_MODEL ** -0.5),
        'b_ada': nrm(ks[3], (DEPTH, 6 * D_MODEL), 0.05),
        'g_pre_mix': 1.0 + nrm(ks[4], (DEPTH, D_MODEL), 0.05),
        'g_post_mix': 1.0 + nrm(ks[5], (DEPTH, D_MODEL), 0.05),
        'g_pre_ffn': 1.0 + nrm(ks[6], (DEPTH, D_MODEL), 0.05),
        'g_post_ffn': 1.0 + nrm(ks[7], (DEPTH, D_MODEL), 0.05),
        'w_in': nrm(ks[8], (DEPTH, D_MODEL, IN_COLS), D_MODEL ** -0.5),
        'w_dw': nrm(ks[9], (DEPTH, CONV_WIDTH, D_CONV), CONV_WIDTH ** -0.5),
        'b_dw': nrm(ks[10], (DEPTH, D_CONV), 0.02),
        'conv_ln_g': 1.0 + nrm(ks[11], (DEPTH, D_CONV), 0.05),
        'conv_ln_b': nrm(ks[12], (DEPTH, D_CONV), 0.02),
        'w_gate_up': nrm(ks[13], (DEPTH, GATE_RANK, D_GLA_K), GATE_RANK ** -0.5),
        'b_gate': nrm(ks[14], (DEPTH, D_GLA_K), 0.1),
        'gla_norm_g': 1.0 + nrm(ks[15], (DEPTH, GLA_DV), 0.05),
        'w_out': nrm(ks[16], (DEPTH, D_MIX, D_MODEL), D_MIX ** -0.5),
        'w_router': nrm(ks[17], (D_MODEL, N_EXPERTS), D_MODEL ** -0.5),
        'b_router': nrm(ks[18], (N_EXPERTS,), 0.01),
        'w1': nrm(ks[19], (DEPTH, N_EXPERTS, D_MODEL, D_EXPERT), D_MODEL ** -0.5),
        'w3': nrm(ks[20], (DEPTH, N_EXPERTS, D_MODEL, D_EXPERT), D_MODEL ** -0.5),
        'w2': nrm(ks[21], (DEPTH, N_EXPERTS, D_EXPERT, D_MODEL), D_EXPERT ** -0.5),
    }

def reference(x, c, w_ada, b_ada, g_pre_mix, g_post_mix, g_pre_ffn, g_post_ffn,
              w_in, w_dw, b_dw, conv_ln_g, conv_ln_b, w_gate_up, b_gate, gla_norm_g,
              w_out, w_router, b_router, w1, w3, w2):
    split_at = [int(s) for s in np.cumsum(SPLIT_SIZES)[:-1]]
    c_act = jax.nn.silu(c)
    for l in range(DEPTH):
        mod = c_act @ w_ada[l] + b_ada[l]
        sh1, sc1, g1, sh2, sc2, g2 = [m[:, None, :] for m in jnp.split(mod, 6, axis=-1)]
        h = rmsnorm(x, g_pre_mix[l]) * (1.0 + sc1) + sh1
        proj = h @ w_in[l]
        cv, cg, q, k, v, og, lr = jnp.split(proj, split_at, axis=-1)
        y_conv = conv_group(cv, cg, w_dw[l], b_dw[l], conv_ln_g[l], conv_ln_b[l])
        y_gla = gla_group(q, k, v, og, lr, w_gate_up[l], b_gate[l], gla_norm_g[l])
        y = jnp.concatenate([y_conv, y_gla], axis=-1) @ w_out[l]
        x = x + g1 * rmsnorm(y, g_post_mix[l])
        h = rmsnorm(x, g_pre_ffn[l]) * (1.0 + sc2) + sh2
        y = grouped_moe(h, w_router, b_router, w1[l], w3[l], w2[l])
        x = x + g2 * rmsnorm(y, g_post_ffn[l])
    return x


_drawn_inputs = setup_inputs


def setup_inputs(seed=0):
    import zlib

    import numpy as np

    out = dict(_drawn_inputs(seed))
    spreads = {}
    factors = {'g_post_ffn': 6.358,
     'b_dw': 5.876,
     'conv_ln_g': 3.377,
     'conv_ln_b': 4.726,
     'b_gate': 3.09,
     'gla_norm_g': 3.901}
    for name, (base, spread) in spreads.items():
        noise = np.random.default_rng([zlib.crc32(name.encode()), seed]).standard_normal(out[name].shape)
        drawn = base * np.exp(spread * noise) if base else spread * noise
        out[name] = __import__('jax').numpy.asarray(drawn.astype(out[name].dtype))
    for name, factor in factors.items():
        out[name] = (out[name] * factor).astype(out[name].dtype)
    return out
```

```python
import concourse.bass as bass
from concourse import mybir

P = 128
BANK = 512
T, D = 512, 1024
NT, KD = T // P, D // P
CONV, WIDTH = 512, 31
NC = CONV // P
HEADS, DK, DV, CHUNK = 4, 64, 128, 64
QK = HEADS * DK
NCH = T // CHUNK
RANK, TAU = 16, 16.0
REST = 2 * QK + 2 * HEADS * DV + RANK
EXPERTS, GROUPS, F = 16, 4, 704
FULL, LAST = F // P, F % P
F2 = F // 2
BLOCK = 128
ROUNDS = T // BLOCK
EPS = 1e-6
BIG = 1e30


def build(nc, x, c, w_ada, b_ada, g_pre_mix, g_post_mix, g_pre_ffn, g_post_ffn, w_in, w_dw, b_dw,
          conv_ln_g, conv_ln_b, w_gate_up, b_gate, gla_norm_g, w_out, w_router, b_router,
          w1, w3, w2, out, threshold=BLOCK):
    f32, f32r = mybir.dt.float32, mybir.dt.float32r
    i32, u32 = mybir.dt.int32, mybir.dt.uint32
    ALU, ACT, AX = mybir.AluOpType, mybir.ActivationFunctionType, mybir.AxisListType

    base = (nc.sbuf_base + 31) // 32 * 32

    def at(name, shape, dt, offset):
        return nc.alloc_sbuf_tensor_at(name, list(shape), dt, offset=base + 4 * offset).ap()

    PIECE = 2 * F
    RAW, SPLIT = 0, KD * PIECE + 6 * D
    KEEP = 2 * SPLIT
    raw13 = at("raw13", [P, KD, PIECE], f32, RAW)
    raw2 = at("raw2", [P, 6, D], f32, RAW + KD * PIECE)
    w_rest = at("w_rest", [P, KD, REST], f32, RAW)
    o = RAW + KD * REST
    ada_sum = at("ada_sum", [P, 2, BANK], f32, o)
    soft_m = at("soft_m", [P, NT, QK], f32, o)
    ada_bias = at("ada_bias", [1, 2, BANK], f32, o + 1024)
    dw_rows = at("dw_rows", [WIDTH, CONV], f32, o + 2048)
    lrT = at("lrT", [RANK + 1, T], f32, o + 2560)
    w_up = at("w_up", [RANK + 1, QK], f32, o + 3072)
    par_rows = at("par_rows", [77, P], f32, o + 3328)
    dwT = at("dwT", [P, NC, WIDTH], f32, o + 3456)
    soft_l = at("soft_l", [P, NT, QK], f32, o + 3584)
    hi13 = at("hi13", [P, 4, PIECE], f32r, SPLIT)
    lo13 = at("lo13", [P, 4, PIECE], f32r, SPLIT + 4 * PIECE)
    hi2 = at("hi2", [P, 3, D], f32r, SPLIT + 8 * PIECE)
    lo2 = at("lo2", [P, 3, D], f32r, SPLIT + 8 * PIECE + 3 * D)
    w_conv = at("w_conv", [P, KD, 2 * CONV], f32, SPLIT)
    w_o = at("w_o", [P, KD, D], f32, SPLIT)
    o = SPLIT + 8192
    ada_w = at("ada_w", [P, 2, KD, BANK], f32, o)
    k_dec = at("k_dec", [P, NT, 2, QK], f32, o)
    state = at("state", [P, NCH, 2, DV], f32, o + 2048)
    o_sq = at("o_sq", [P, 2, BANK], f32, o + 4096)
    o_std = at("o_std", [P, 2, BANK], f32, o + 5120)
    x_again = at("x_again", [P, 2, D], f32, o + 6144)
    h2 = at("h2", [P, NT, D], f32, o)
    gate1 = at("gate1", [P, D], f32, SPLIT + 16384)
    o = KEEP
    ident = at("ident", [P, P], f32, o)
    ones = at("ones", [P, P], f32, o + 128)
    later = at("later", [P, P], f32, o + 256)
    w_r = at("w_r", [P, KD, EXPERTS], f32, o + 256)
    before = at("before", [P, P], f32, o + 384)
    o += 512
    smalls = at("smalls", [P, 264], f32, o)
    small, o = {}, 0
    for name, n in (("par", 80), ("half", 2), ("csil", 8), ("A1", 8), ("B1", 8), ("modc", 16), ("eps", 1),
                    ("xss", 4), ("xstd", 4), ("xr", 4), ("yss", 4), ("ystd", 4), ("yr", 4), ("x2ss", 4),
                    ("x2std", 4), ("x2r", 4), ("decay", 16), ("brow", 16), ("wts", 8), ("fss", 4),
                    ("fstd", 4), ("fr", 4), ("key", 16), ("gkey", 4)):
        small[name] = smalls[:, o:o + n]
        o += n
    pos = smalls[:, o:o + 8].bitcast(u32)
    count = smalls[:, o + 8:o + 9].bitcast(i32)
    assert o + 9 <= 264
    o = KEEP + 512 + 264
    gate2 = at("gate2", [P, D], f32, o)
    scale2 = at("scale2", [P, D], f32, o + 1024)
    shift2 = at("shift2", [P, D], f32, o + 2048)
    o += 3072
    hT = at("hT", [P, KD, T], f32, o)
    x2 = at("x2", [P, NT, D], f32, o)
    o += 4096
    x_rows = at("x_rows", [P, NT, D], f32, o)
    kv = at("kv", [P, NT, 3 * QK], f32, o)
    gT = at("gT", [P, HEADS, T], f32, o + 3072)
    h2T = at("h2T", [P, KD, T], f32, o)
    ZERO_MORE = o + 4096
    xe = at("xe", [P, D], f32, o)
    xeT = at("xeT", [P, KD, P], f32, o + 1024)
    x_hi = at("x_hi", [P, KD, P], f32r, o + 2048)
    x_lo = at("x_lo", [P, KD, P], f32r, o + 3072)
    o += 5120
    xhat = at("xhat", [P, NT, D], f32, o)
    conv = at("conv", [P, NC, T], f32, o)
    uT = at("uT", [P, NC, WIDTH - 1 + T], f32, o + 2048)
    rt = at("rt", [P, 1144], f32, o + 4096)
    s_act = at("s_act", [P, F], f32, o)
    he = at("he", [P, 6 * P], f32, o + 704)
    he_hi = at("he_hi", [P, 6, P], f32r, o + 1472)
    he_lo = at("he_lo", [P, 6, P], f32r, o + 2240)
    y_e = at("y_e", [P, D], f32, o + 3008)
    o += 4216
    qT = at("qT", [P, 2, T], f32, o)
    sig = at("sig", [P, 2, BANK], f32, o)
    junk = at("junk", [P, D], f32, o)
    o += 1024
    assert base + 4 * o <= nc.sbuf_usable_end, (base + 4 * o, nc.sbuf_usable_end)
    back = at("back", [P, NT, 2, D], f32, RAW)
    mixed = at("mixed", [P, NT, D], f32, SPLIT)
    result = at("result", [P, NT, D], f32, SPLIT + 4096)
    zero = at("zero", [P, 256], f32, SPLIT + 8192 + 6144)
    zero_more = at("zero_more", [P, 256], f32, ZERO_MORE)

    psum = nc.alloc_psum_tensor("psum", [P, 8 * BANK], f32).ap()

    def bank(b, n=1):
        return psum[:, b * BANK:(b + n) * BANK]

    H1 = psum[:, 0:2 * BANK].rearrange("p (b n) -> p b n", b=2)[:, :, 0:F2]
    H3 = psum[:, 2 * BANK:4 * BANK].rearrange("p (b n) -> p b n", b=2)[:, :, 0:F2]
    TB, YB = 4, 6

    table = nc.dram_tensor("table", (ROUNDS * EXPERTS, BLOCK, D), f32).ap()
    table_y = nc.dram_tensor("table_y", (ROUNDS * EXPERTS, BLOCK, D), f32).ap()
    table_rows = table.rearrange("b p d -> (b p) d")
    table_y_rows = table_y.rearrange("b p d -> (b p) d")

    w_ada_v = w_ada[0].rearrange("(k p) n -> p k n", p=P)
    w_in_v = w_in[0].rearrange("(k p) n -> p k n", p=P)
    x_v = x[0].rearrange("(t p) d -> p t d", p=P)
    out_v = out[0].rearrange("(t p) d -> p t d", p=P)
    w1_v = w1[0].rearrange("e (k p) f -> e p k f", p=P)
    w3_v = w3[0].rearrange("e (k p) f -> e p k f", p=P)
    w2_v = w2[0, :, 0:FULL * P, :].rearrange("e (k p) d -> e p k d", p=P)

    def sem(name):
        return nc.alloc_semaphore(name)

    x_in, par_in, consts, cols_up, cols_ok = map(sem, ("x_in", "par_in", "consts", "cols_up", "cols_ok"))
    ada_in = [sem(f"ada_in{i}") for i in range(2)]
    bias_in = [sem(f"bias_in{i}") for i in range(2)]
    ada_summed, ada_mm, ada_taken = map(sem, ("ada_summed", "ada_mm", "ada_taken"))
    conv_in, rest_in, w_out_in, rows_in, w_r_in = map(sem, ("conv_in", "rest_in", "w_out_in", "rows_in", "w_r_in"))
    xhat_ok, xT_up, mod1_ok, hT_a, hT_v = map(sem, ("xhat_ok", "xT_up", "mod1_ok", "hT_a", "hT_v"))
    conv_mm, sig_ok, u_ok = map(sem, ("conv_mm", "sig_ok", "u_ok"))
    unit_mm, unit_ok, z_mm, gate_parts, soft_ok, later_mm = map(
        sem, ("unit_mm", "unit_ok", "z_mm", "gate_parts", "soft_ok", "later_mm"))
    decay_ok, kdec_ok, upd_mm, state_ok, tap_ok = map(sem, ("decay_ok", "kdec_ok", "upd_mm", "state_ok", "tap_ok"))
    mean_mm, cent_ok, csq_ok, var_mm, cstd_ok, cnorm_ok, yconv_ok = map(
        sem, ("mean_mm", "cent_ok", "csq_ok", "var_mm", "cstd_ok", "cnorm_ok", "yconv_ok"))
    o_mm, osq_ok, osum_mm, ostd_ok, ygla_ok = map(sem, ("o_mm", "osq_ok", "osum_mm", "ostd_ok", "ygla_ok"))
    y_mm, yss_ok, ystd_ok, x2_ok, x2ss_ok, x2std_ok, h2_ok = map(
        sem, ("y_mm", "yss_ok", "ystd_ok", "x2_ok", "x2ss_ok", "x2std_ok", "h2_ok"))
    xag_in = [sem(f"xag_in{i}") for i in range(2)]
    h2T_up, h2T_a, h2T_v, logit_mm, exp_ok, exp_in, mask_ok, rank_mm, pos_ok = map(
        sem, ("h2T_up", "h2T_a", "h2T_v", "logit_mm", "exp_ok", "exp_in", "mask_ok", "rank_mm", "pos_ok"))
    zero_ok, cleared, cleared_more, scattered = map(sem, ("zero_ok", "cleared", "cleared_more", "scattered"))
    eps_ok, xr_ok = map(sem, ("eps_ok", "xr_ok"))
    act_step, pool_step, dve_step = map(sem, ("act_step", "pool_step", "dve_step"))
    raw13_in = [sem(f"raw13_in{i}") for i in range(4)]
    raw2_in = [sem(f"raw2_in{i}") for i in range(3)]
    hi13_ok, lo13_ok, fed13, hi2_ok, lo2_ok, fed2 = map(
        sem, ("hi13_ok", "lo13_ok", "fed13", "hi2_ok", "lo2_ok", "fed2"))
    xe_in, xeT_up, xeT_ok, xhl_ok = map(sem, ("xe_in", "xeT_up", "xeT_ok", "xhl_ok"))
    silu_ok, he_ok, heT_up, hehi_ok, helo_ok = map(
        sem, ("silu_ok", "he_ok", "heT_up", "hehi_ok", "helo_ok"))
    ye_a, ye_v, ye_out = map(sem, ("ye_a", "ye_v", "ye_out"))
    back_in = [sem(f"back_in{i}") for i in range(NT)]
    f_mix, f_ss, f_std, f_r, f_ok, stored = map(sem, ("f_mix", "f_ss", "f_std", "f_r", "f_ok", "stored"))

    def reach(eng, s, value):
        if not isinstance(value, int) or value > 0:
            eng.wait_ge(s, value)

    def chain(eng, s):
        n = [0]

        def link(ins):
            ins.then_inc(s, 1)
            n[0] += 1
            eng.wait_ge(s, n[0])
        return link

    def most(eng):
        eng.wait_ge(pos_ok, 1)
        return eng.value_load(count[0:1, 0:1], min_val=0, max_val=T)

    UNIT_BANK = [4, 5, 0, 1]
    UNITS = [("lr", 0)] + [("kv", i) for i in range(2 * NT)] + [("q", 0), ("q", 1)] + [("g", i) for i in range(HEADS)]
    KV_HALF = 3 * QK // 2
    C_K, C_V, C_G, C_LR = QK, 2 * QK, 2 * QK + HEADS * DV, 2 * QK + 2 * HEADS * DV

    R = {}
    o = 0
    for name, shape in (("sh", (NT, EXPERTS)), ("p", (NT, EXPERTS)), ("sel", (NT, EXPERTS)), ("q", (4, NT * GROUPS)),
                        ("hot0", (NT, EXPERTS)), ("hot1", (NT, EXPERTS)), ("kmax", (2, NT)), ("w", (2, NT)),
                        ("sum", (2, NT))):
        n = shape[0] * shape[1]
        part = rt[:, o:o + n].rearrange("p (a b) -> p a b", a=shape[0])
        R[name] = part
        o += n
    R["a"] = rt[:, o:o + NT]
    R["hot"] = [R["hot0"], R["hot1"]]

    block = nc.Block()
    with block:

        @block.sync
        def _(sp):
            sp.dma_start(x_rows, x_v).then_inc(x_in, 16)

            def ada(b):
                if b >= 2:
                    sp.wait_ge(ada_summed, b - 1)
                sp.dma_start(ada_w[:, b % 2], w_ada_v[:, :, b * BANK:(b + 1) * BANK]).then_inc(ada_in[b % 2], 16)
                if b >= 4:
                    if b >= 6:
                        sp.wait_ge(ada_mm, b - 1)
                    sp.dma_start(ada_bias[0:1, b % 2, :], b_ada[0:1, b * BANK:(b + 1) * BANK]).then_inc(bias_in[b % 2], 16)

            half = KD // 2
            ada(0)
            ada(1)
            sp.dma_start(w_conv[:, 0:half], w_in_v[:, 0:half, 0:2 * CONV]).then_inc(conv_in, 16)
            ada(2)
            sp.dma_start(w_conv[:, half:], w_in_v[:, half:, 0:2 * CONV]).then_inc(conv_in, 16)
            ada(3)
            sp.dma_start(w_rest[:, 0:half], w_in_v[:, 0:half, 2 * CONV:]).then_inc(rest_in, 16)
            sp.dma_start(w_rest[:, half:], w_in_v[:, half:, 2 * CONV:]).then_inc(rest_in, 16)
            for b in range(4, 12):
                ada(b)
            sp.wait_ge(conv_mm, 2 * NC)
            sp.dma_start(w_o, w_out[0].rearrange("(k p) n -> p k n", p=P)).then_inc(w_out_in, 16)

            def up(i, e):
                for g in range(4):
                    reach(sp, lo13_ok, KD * (i - 1) + 2 * (g + 1))
                    at_ = raw13[:, 2 * g:2 * g + 2]
                    sp.dma_start(at_[:, :, 0:F], w1_v[e, :, 2 * g:2 * g + 2, :]).then_inc(raw13_in[g], 16)
                    sp.dma_start(at_[:, :, F:], w3_v[e, :, 2 * g:2 * g + 2, :]).then_inc(raw13_in[g], 16)

            def down(i, e):
                for g in range(3):
                    reach(sp, lo2_ok, 6 * (i - 1) + 2 * (g + 1))
                    if g < 2:
                        sp.dma_start(raw2[:, 2 * g:2 * g + 2], w2_v[e, :, 2 * g:2 * g + 2, :]).then_inc(raw2_in[g], 32)
                    else:
                        sp.dma_start(raw2[:, 4], w2_v[e, :, 4, :]).then_inc(raw2_in[g], 16)
                        sp.dma_start(raw2[0:LAST, 5], w2[0, e, FULL * P:, :]).then_inc(raw2_in[g], 16)

            sp.wait_ge(zero_ok, 1)
            for q in range(4):
                sp.dma_start(table[0:EXPERTS, :, q * 256:(q + 1) * 256].rearrange("b p d -> p b d"),
                             zero.unsqueeze(1).broadcast_to((P, EXPERTS, 256))).then_inc(cleared, 16)
            sp.wait_ge(unit_mm, len(UNITS))
            up(0, 0)
            sp.wait_ge(later_mm, 1)
            sp.wait_ge(kdec_ok, 2)
            sp.wait_ge(tap_ok, NC * WIDTH)

            def one_pass(i0):
                up(i0 + 1, 1)
                down(i0, 0)
                with sp.Fori(2, EXPERTS) as e:
                    up(i0 + e, e)
                    down(i0 + e - 1, e - 1)
                down(i0 + EXPERTS - 1, EXPERTS - 1)

            one_pass(0)
            over = most(sp)
            with sp.If(over > threshold):
                with sp.Fori(1, ROUNDS) as r:
                    i0 = sp.snap(r * EXPERTS)
                    up(i0, 0)
                    one_pass(i0)
            for t in range(NT):
                sp.wait_ge(f_ok, t + 1)
                sp.dma_start(out_v[:, t], result[:, t]).then_inc(stored, 16)
            sp.wait_ge(stored, 16 * NT)

        @block.gpsimd
        def _(gp):
            gp.iota(small["key"], pattern=[[-1, EXPERTS]], base=EXPERTS, channel_multiplier=0,
                    allow_small_or_imprecise_dtypes=True).then_inc(consts, 1)
            gp.iota(small["gkey"], pattern=[[-1, GROUPS]], base=GROUPS, channel_multiplier=0,
                    allow_small_or_imprecise_dtypes=True).then_inc(consts, 1)
            gp.memset(ident, 0.0).then_inc(pool_step, 1)
            gp.memset(ones, 1.0).then_inc(consts, 1)
            gp.memset(small["half"], 1.0).then_inc(pool_step, 1)
            gp.memset(lrT, 1.0).then_inc(consts, 1)
            gp.wait_ge(pool_step, 2)
            gp.wait_ge(consts, 4)
            gp.affine_select(out=ident, in_=ident, compare_op=ALU.not_equal, fill=1.0, base=0,
                             pattern=[[-1, P]], channel_multiplier=1).then_inc(consts, 1)
            gp.affine_select(out=before, in_=ones, compare_op=ALU.is_gt, fill=0.0, base=0,
                             pattern=[[1, P]], channel_multiplier=-1).then_inc(consts, 1)
            gp.affine_select(out=later, in_=ones, compare_op=ALU.is_gt, fill=0.0, base=0,
                             pattern=[[-1, P]], channel_multiplier=1).then_inc(pool_step, 1)
            gp.wait_ge(pool_step, 3)
            gp.affine_select(out=later[:, 0:CHUNK], in_=later[:, 0:CHUNK], compare_op=ALU.is_gt, fill=0.0, base=CHUNK,
                             pattern=[[0, CHUNK]], channel_multiplier=-1).then_inc(consts, 1)
            gp.affine_select(out=small["half"][:, 0:1], in_=small["half"][:, 0:1], compare_op=ALU.is_gt, fill=0.0,
                             base=CHUNK, pattern=[[0, 1]], channel_multiplier=-1).then_inc(consts, 1)
            gp.affine_select(out=small["half"][:, 1:2], in_=small["half"][:, 1:2], compare_op=ALU.is_ge, fill=0.0,
                             base=-CHUNK, pattern=[[0, 1]], channel_multiplier=1).then_inc(consts, 1)
            gp.wait_ge(gate_parts, 1)
            gp.tensor_tensor(soft_l, soft_l, soft_m, ALU.add).then_inc(soft_ok, 1)
            gp.wait_ge(ada_mm, 12)
            gp.memset(zero, 0.0).then_inc(zero_ok, 1)
            gp.wait_ge(zero_ok, 1)
            gp.memset(k_dec[0:CHUNK, :, 1, :], 0.0).then_inc(pool_step, 1)
            gp.wait_ge(pool_step, 4)
            gp.memset(k_dec[CHUNK:P, :, 0, :], 0.0).then_inc(pool_step, 1)
            gp.wait_ge(pool_step, 5)
            gp.wait_ge(decay_ok, 1)
            gp.wait_ge(unit_ok, 1 + 2 * NT)
            gp.tensor_tensor(k_dec[0:CHUNK, :, 0, :], kv[0:CHUNK, :, 0:QK], soft_m[0:CHUNK], ALU.mult).then_inc(kdec_ok, 1)
            gp.wait_ge(kdec_ok, 1)
            gp.tensor_tensor(k_dec[CHUNK:P, :, 1, :], kv[CHUNK:P, :, 0:QK], soft_m[CHUNK:P], ALU.mult).then_inc(kdec_ok, 1)
            gp.wait_ge(cleared, 64)
            for t in range(NT):
                if t >= 2:
                    gp.wait_ge(x2_ok, 2 * (t - 1))
                gp.dma_start(x_again[:, t % 2], x_v[:, t]).then_inc(xag_in[t % 2], 16)
            over = most(gp)
            with gp.If(over > threshold):
                gp.memset(zero_more, 0.0).then_inc(zero_ok, 1)
                gp.wait_ge(zero_ok, 2)
                with gp.Fori(EXPERTS, ROUNDS * EXPERTS) as b:
                    gp.dma_start(table[b].rearrange("p (q d) -> p q d", q=4),
                                 zero_more.unsqueeze(1).broadcast_to((P, 4, 256))).then_inc(cleared_more, 16)
                gp.wait_ge(cleared_more, 16 * (ROUNDS - 1) * EXPERTS)
            for t in range(NT):
                for k in range(2):
                    gp.indirect_dma_start(
                        out=table_rows, out_offset=bass.IndirectOffsetOnAxis(ap=pos[:, 4 * k + t:4 * k + t + 1], axis=0),
                        in_=h2[:, t], in_offset=None).then_inc(scattered, 16)
            gp.wait_ge(scattered, 32 * NT)

            def load(i, blk):
                reach(gp, xeT_up, i)
                gp.dma_start(xe, table[blk]).then_inc(xe_in, 16)

            def split_x(i):
                gp.wait_ge(xeT_ok, i + 1)
                reach(gp, fed13, KD * i)
                gp.tensor_tensor(x_hi, xeT, ones.unsqueeze(1).broadcast_to((P, KD, P)), ALU.mult).then_inc(xhl_ok, 1)
                gp.wait_ge(xhl_ok, 2 * i + 1)
                gp.tensor_tensor(x_lo, xeT, x_hi.bitcast(f32), ALU.subtract).then_inc(xhl_ok, 1)

            def store(i, blk):
                gp.wait_ge(ye_a, i + 1)
                gp.wait_ge(ye_v, i + 1)
                gp.dma_start(table_y[blk], y_e).then_inc(ye_out, 16)

            def one_pass(i0):
                load(i0, i0)
                split_x(i0)
                load(i0 + 1, i0 + 1)
                split_x(i0 + 1)
                with gp.Fori(1, EXPERTS - 1) as e:
                    i = gp.snap(i0 + e)
                    load(i + 1, i + 1)
                    split_x(i + 1)
                    store(i - 1, i - 1)
                for e in (EXPERTS - 2, EXPERTS - 1):
                    store(i0 + e, i0 + e)

            def gather(rounds):
                rows = table_y_rows[0:rounds * EXPERTS * BLOCK]
                for t in range(NT):
                    for k in range(2):
                        gp.indirect_dma_start(
                            out=back[:, t, k], out_offset=None, in_=rows,
                            in_offset=bass.IndirectOffsetOnAxis(ap=pos[:, 4 * k + t:4 * k + t + 1], axis=0)).then_inc(back_in[t], 16)

            one_pass(0)
            over = most(gp)
            with gp.If(over > threshold):
                with gp.Fori(1, ROUNDS) as r:
                    one_pass(gp.snap(r * EXPERTS))
                gp.wait_ge(ye_out, 16 * ROUNDS * EXPERTS)
                gather(ROUNDS)
            with gp.Else():
                gp.wait_ge(ye_out, 16 * EXPERTS)
                gather(1)
            gp.wait_ge(back_in[NT - 1], 32)

        @block.scalar
        def _(act):
            link = chain(act, act_step)
            row = 0
            for src, n in ((b_ada, 48), (g_pre_mix, 8), (c, 8), (b_dw, 4), (conv_ln_g, 4), (conv_ln_b, 4), (gla_norm_g, 1)):
                act.dma_start(par_rows[row:row + n, :], src.rearrange("o (r q) -> (o r) q", q=P)).then_inc(par_in, 16)
                row += n
            act.dma_start(dw_rows, w_dw[0]).then_inc(par_in, 16)
            act.dma_start(w_up[0:RANK, :], w_gate_up[0]).then_inc(rows_in, 16)
            act.dma_start(w_up[RANK:RANK + 1, :], b_gate).then_inc(rows_in, 16)
            act.dma_start(small["brow"], b_router.rearrange("(o n) -> o n", o=1).broadcast_to((P, EXPERTS))).then_inc(rows_in, 16)
            act.dma_start(gate1, g_post_mix.broadcast_to((P, D))).then_inc(rows_in, 16)
            act.dma_start(gate2, g_post_ffn.broadcast_to((P, D))).then_inc(rows_in, 16)
            act.dma_start(scale2, g_pre_ffn.broadcast_to((P, D))).then_inc(rows_in, 16)
            act.wait_ge(cols_ok, 1)
            link(nc.scalar.activation(small["csil"], small["par"][:, 56:64], ACT.Silu))
            act.wait_ge(x_in, 16)
            for t in range(NT):
                link(nc.scalar.activation(xhat[:, t], x_rows[:, t], ACT.Square, accum_out=small["xss"][:, t:t + 1]))
            act.wait_ge(eps_ok, 1)
            link(nc.scalar.activation(small["xstd"], small["xss"], ACT.Sqrt, scale=1.0 / D, bias=small["eps"]))
            act.wait_ge(xr_ok, 1)
            for t in range(NT):
                nc.scalar.activation(xhat[:, t], x_rows[:, t], ACT.Copy, scale=small["xr"][:, t:t + 1]).then_inc(xhat_ok, 1)
            act.wait_ge(mod1_ok, 1)
            for k in range(0, KD, 2):
                act.wait_ge(xT_up, k + 1)
                nc.scalar.activation(hT[:, k], bank(k), ACT.Identity, scale=small["A1"][:, k:k + 1],
                                     bias=small["B1"][:, k:k + 1]).then_inc(hT_a, 1)
            for j in range(NC):
                act.wait_ge(conv_mm, 2 * j + 2)
                reach(act, u_ok, j - 1)
                nc.scalar.activation(sig[:, j % 2], bank(2 * (j % 2) + 1), ACT.Sigmoid).then_inc(sig_ok, 1)
            for u, (what, i) in enumerate(UNITS):
                act.wait_ge(unit_mm, u + 1)
                b = bank(UNIT_BANK[u % 4])
                if what == "lr":
                    act.wait_ge(consts, 9)
                    nc.scalar.activation(lrT[0:RANK, :], b[0:RANK, :], ACT.Copy).then_inc(unit_ok, 1)
                elif what == "kv":
                    h = i % 2
                    nc.scalar.activation(kv[:, i // 2, h * KV_HALF:(h + 1) * KV_HALF], b[:, 0:KV_HALF], ACT.Copy).then_inc(unit_ok, 1)
                elif what == "q":
                    act.wait_ge(u_ok, NC)
                    nc.scalar.activation(qT[:, i], b, ACT.Copy, scale=DK ** -0.5).then_inc(unit_ok, 1)
                else:
                    nc.scalar.activation(gT[:, i], b, ACT.Silu).then_inc(unit_ok, 1)
                if (what, i) == ("q", 1):
                    act.wait_ge(z_mm, 1)
                    z = bank(2, 2).rearrange("p (t n) -> p t n", t=NT)
                    link(nc.scalar.activation(soft_l, z, ACT.Abs))
                    link(nc.scalar.activation(soft_l, soft_l, ACT.Exp, scale=-1.0))
                    link(nc.scalar.activation(soft_l, soft_l, ACT.Ln, bias=1.0))
                    act.wait_ge(ada_mm, 12)
                    nc.scalar.activation(soft_m, z, ACT.Relu, scale=-1.0).then_inc(gate_parts, 1)
                if (what, i) == ("g", 2):
                    act.wait_ge(later_mm, 1)
                    link(nc.scalar.activation(soft_m, bank(2, 2).rearrange("p (t n) -> p t n", t=NT), ACT.Exp, scale=-1.0 / TAU))
                    nc.scalar.activation(small["decay"], bank(6)[:, 0:16], ACT.Exp, scale=-1.0 / TAU).then_inc(decay_ok, 1)
                    act.dma_start(w_r, w_router.rearrange("(k p) e -> p k e", p=P)).then_inc(w_r_in, 16)
            for j in range(NC):
                act.wait_ge(cent_ok, j + 1)
                reach(act, var_mm, j - 1)
                nc.scalar.activation(o_sq[:, j % 2], conv[:, j], ACT.Square).then_inc(csq_ok, 1)
            act.wait_ge(var_mm, NC)
            nc.scalar.activation(o_std[:, 0], bank(1), ACT.Sqrt, scale=1.0 / CONV, bias=small["eps"]).then_inc(cstd_ok, 1)
            for h in range(HEADS):
                act.wait_ge(o_mm, h + 1)
                reach(act, osum_mm, h - 1)
                nc.scalar.activation(o_sq[:, h % 2], bank(2 + h), ACT.Square).then_inc(osq_ok, 1)
            for h in range(HEADS):
                act.wait_ge(osum_mm, h + 1)
                if h == 0:
                    act.wait_ge(cnorm_ok, NC)
                reach(act, ygla_ok, h - 1)
                nc.scalar.activation(o_std[:, h % 2], bank(6 + h % 2), ACT.Sqrt, scale=1.0 / DV, bias=small["eps"]).then_inc(ostd_ok, 1)
            for j in range(NC):
                act.wait_ge(cnorm_ok, j + 1)
                nc.scalar.activation(conv[:, j], conv[:, j], ACT.Silu, scale=small["par"][:, 68 + j:69 + j],
                                     bias=small["par"][:, 72 + j:73 + j]).then_inc(yconv_ok, 1)
            for t in range(NT):
                act.wait_ge(y_mm, t + 1)
                nc.scalar.activation(junk, bank(2 * t, 2), ACT.Square, accum_out=small["yss"][:, t:t + 1]).then_inc(yss_ok, 1)
                act.wait_ge(yss_ok, t + 1)
                nc.scalar.activation(small["ystd"][:, t:t + 1], small["yss"][:, t:t + 1], ACT.Sqrt, scale=1.0 / D,
                                     bias=small["eps"]).then_inc(ystd_ok, 1)
                act.wait_ge(x2_ok, 2 * t + 2)
                nc.scalar.activation(junk, x2[:, t], ACT.Square, accum_out=small["x2ss"][:, t:t + 1]).then_inc(x2ss_ok, 1)
                act.wait_ge(x2ss_ok, t + 1)
                nc.scalar.activation(small["x2std"][:, t:t + 1], small["x2ss"][:, t:t + 1], ACT.Sqrt, scale=1.0 / D,
                                     bias=small["eps"]).then_inc(x2std_ok, 1)
            for k in range(0, KD, 2):
                act.wait_ge(h2T_up, k + 1)
                nc.scalar.activation(h2T[:, k], bank(k), ACT.Copy).then_inc(h2T_a, 1)
            act.wait_ge(exp_in, 1)
            nc.scalar.activation(R["p"], R["sh"], ACT.Exp).then_inc(exp_ok, 1)

            def split13(i, p):
                g = p // 2
                if p % 2 == 0:
                    act.wait_ge(raw13_in[g], 32 * (i + 1))
                reach(act, fed13, KD * i + p - 3)
                nc.scalar.activation(hi13[:, p % 4], raw13[:, p], ACT.Copy).then_inc(hi13_ok, 1)

            def split2(i, p):
                g = p // 2
                if p % 2 == 0:
                    act.wait_ge(raw2_in[g], 32 * (i + 1))
                reach(act, fed2, 6 * i + p - 2)
                n = P if p < FULL else LAST
                nc.scalar.activation(hi2[0:n, p % 3], raw2[0:n, p], ACT.Copy).then_inc(hi2_ok, 1)

            def silu(i):
                act.wait_ge(fed13, KD * (i + 1))
                reach(act, he_ok, i)
                nc.scalar.activation(s_act.rearrange("p (b n) -> p b n", b=2), H1, ACT.Silu).then_inc(silu_ok, 1)

            def x_out(i):
                act.wait_ge(xeT_up, i + 1)
                reach(act, xhl_ok, 2 * i)
                nc.scalar.activation(xeT.rearrange("p k n -> p (k n)"), bank(TB, 2), ACT.Copy).then_inc(xeT_ok, 1)

            def he_high(i):
                act.wait_ge(heT_up, i + 1)
                reach(act, fed2, 6 * i)
                nc.scalar.activation(he_hi.rearrange("p k n -> p (k n)"), bank(TB, 2)[:, 0:6 * P], ACT.Copy).then_inc(hehi_ok, 1)

            def y_out(i):
                act.wait_ge(fed2, 6 * (i + 1))
                reach(act, ye_out, 16 * i)
                nc.scalar.activation(y_e[:, 0:BANK], bank(YB), ACT.Copy).then_inc(ye_a, 1)

            def one_pass(i0):
                for p in range(4):
                    split13(i0, p)
                x_out(i0)
                for p in range(4, KD):
                    split13(i0, p)
                silu(i0)
                x_out(i0 + 1)
                for p in range(4):
                    split13(i0 + 1, p)
                he_high(i0)

                def body(i):
                    for p in range(4, KD):
                        split13(i, p)
                    for p in range(3):
                        split2(i - 1, p)
                    silu(i)
                    x_out(i + 1)
                    for p in range(3, 6):
                        split2(i - 1, p)
                    for p in range(4):
                        split13(i + 1, p)
                    y_out(i - 1)
                    he_high(i)

                body(i0 + 1)
                with act.Fori(2, EXPERTS - 1) as e:
                    body(act.snap(i0 + e))
                i = i0 + EXPERTS - 1
                for p in range(4, KD):
                    split13(i, p)
                for p in range(3):
                    split2(i - 1, p)
                silu(i)
                for p in range(3, 6):
                    split2(i - 1, p)
                for p in range(3):
                    split2(i, p)
                y_out(i - 1)
                he_high(i)
                for p in range(3, 6):
                    split2(i, p)
                y_out(i)

            act.wait_ge(y_mm, NT)
            act.wait_ge(x2_ok, 2 * NT)
            one_pass(0)
            over = most(act)
            with act.If(over > threshold):
                with act.Fori(1, ROUNDS) as r:
                    one_pass(act.snap(r * EXPERTS))
            for t in range(NT):
                act.wait_ge(f_mix, 2 * t + 2)
                nc.scalar.activation(result[:, t], mixed[:, t], ACT.Square, accum_out=small["fss"][:, t:t + 1]).then_inc(f_ss, 1)
                act.wait_ge(f_ss, t + 1)
                nc.scalar.activation(small["fstd"][:, t:t + 1], small["fss"][:, t:t + 1], ACT.Sqrt, scale=1.0 / D,
                                     bias=small["eps"]).then_inc(f_std, 1)

        @block.vector
        def _(dve):
            v = nc.vector
            link = chain(dve, dve_step)
            v.memset(small["eps"], EPS).then_inc(eps_ok, 1)
            dve.wait_ge(cols_up, 1)
            link(v.tensor_copy(dwT, bank(7)[:, 128:256].rearrange("p (j n) -> p j n", j=NC)[:, :, 0:WIDTH]))
            v.tensor_copy(small["par"][:, 0:77], bank(7)[:, 0:77]).then_inc(cols_ok, 1)
            dve.wait_ge(act_step, 1)

            def ada(b):
                dve.wait_ge(ada_in[b % 2], 16 * (b // 2 + 1))
                reach(dve, ada_mm, b - 1)
                s = ada_sum[:, b % 2]
                link(v.tensor_scalar(s, ada_w[:, b % 2, 0], small["csil"][:, 0:1], None, ALU.mult))
                for k in range(1, KD):
                    ins = v.scalar_tensor_tensor(out=s, in0=ada_w[:, b % 2, k], scalar=small["csil"][:, k:k + 1],
                                                 in1=s, op0=ALU.mult, op1=ALU.add)
                    if k < KD - 1:
                        link(ins)
                ins.then_inc(ada_summed, 1)

            def ada_row(r):
                dve.wait_ge(ada_mm, 5 + r)
                what, h = r // 2, slice(r % 2 * BANK, (r % 2 + 1) * BANK)
                b = bank(6 + r % 2)
                if what == 0:
                    v.tensor_tensor(gate1[:, h], b, gate1[:, h], ALU.mult).then_inc(ada_taken, 1)
                elif what == 1:
                    v.tensor_copy(shift2[:, h], b).then_inc(ada_taken, 1)
                elif what == 2:
                    v.scalar_tensor_tensor(out=scale2[:, h], in0=b, scalar=1.0, in1=scale2[:, h], op0=ALU.add,
                                           op1=ALU.mult).then_inc(ada_taken, 1)
                else:
                    v.tensor_tensor(gate2[:, h], b, gate2[:, h], ALU.mult).then_inc(ada_taken, 1)

            ada(0)
            dve.wait_ge(act_step, 1 + NT + 1)
            v.reciprocal(small["xr"], small["xstd"]).then_inc(xr_ok, 1)
            for b in range(1, 4):
                ada(b)
            dve.wait_ge(ada_mm, 4)
            link(v.tensor_tensor(small["modc"], bank(7)[:, 0:16], small["par"][:, 0:16], ALU.add))
            link(v.tensor_copy(small["B1"], small["modc"][:, 0:8]))
            v.scalar_tensor_tensor(out=small["A1"], in0=small["modc"][:, 8:16], scalar=1.0, in1=small["par"][:, 48:56],
                                   op0=ALU.add, op1=ALU.mult).then_inc(mod1_ok, 1)
            dve.wait_ge(mod1_ok, 1)
            for k in range(1, KD, 2):
                dve.wait_ge(xT_up, k + 1)
                v.tensor_scalar(hT[:, k], bank(k), small["A1"][:, k:k + 1], small["B1"][:, k:k + 1], ALU.mult,
                                ALU.add).then_inc(hT_v, 1)
            link(v.memset(uT[:, :, 0:WIDTH - 1], 0.0))
            dve.wait_ge(rows_in, 96)
            for j in range(NC):
                dve.wait_ge(sig_ok, j + 1)
                v.tensor_tensor(uT[:, j, WIDTH - 1:], bank(2 * (j % 2)), sig[:, j % 2], ALU.mult).then_inc(u_ok, 1)
                if j >= 2:
                    ada_row(j - 2)
                ada(4 + j)
            for r in range(2, 8):
                ada_row(r)
                if r < 6:
                    ada(6 + r)

            dve.wait_ge(u_ok, NC)
            for j in range(NC):
                v.tensor_scalar(conv[:, j], uT[:, j, 0:T], dwT[:, j, 0:1], small["par"][:, 64 + j:65 + j], ALU.mult,
                                ALU.add).then_inc(tap_ok, 1)
            with dve.Fori(1, WIDTH) as tap:
                for j in range(NC):
                    dve.wait_ge(tap_ok, NC * tap - NC + j + 1)
                    v.scalar_tensor_tensor(out=conv[:, j], in0=uT[:, j, bass.ds(tap, T)], scalar=dwT[:, j, bass.ds(tap, 1)],
                                           in1=conv[:, j], op0=ALU.mult, op1=ALU.add).then_inc(tap_ok, 1)
            dve.wait_ge(decay_ok, 1)
            n_state = 0
            for n in range(NCH):
                dve.wait_ge(upd_mm, n + 1)
                u = bank(6 + n % 2)
                for p in range(2):
                    for h in range(2):
                        rows = slice(h * DK, (h + 1) * DK)
                        src = u[rows, p * QK + h * DV:p * QK + (h + 1) * DV]
                        if n == 0:
                            v.tensor_copy(state[rows, n, p], src).then_inc(state_ok, 1)
                        else:
                            dve.wait_ge(state_ok, 4 * (n - 1) + 2 * p + h + 1)
                            v.scalar_tensor_tensor(out=state[rows, n, p], in0=state[rows, n - 1, p],
                                                   scalar=small["decay"][rows, p * NCH + n:p * NCH + n + 1], in1=src,
                                                   op0=ALU.mult, op1=ALU.add).then_inc(state_ok, 1)
            dve.wait_ge(mean_mm, 1)
            for j in range(NC):
                v.scalar_tensor_tensor(out=conv[:, j], in0=bank(0), scalar=-1.0 / CONV, in1=conv[:, j], op0=ALU.mult,
                                       op1=ALU.add).then_inc(cent_ok, 1)
            dve.wait_ge(cstd_ok, 1)
            link(v.reciprocal(o_std[:, 0], o_std[:, 0]))
            dve.wait_ge(cent_ok, NC)
            for j in range(NC):
                v.tensor_tensor(conv[:, j], conv[:, j], o_std[:, 0], ALU.mult).then_inc(cnorm_ok, 1)
            dve.wait_ge(unit_ok, len(UNITS))
            for h in range(HEADS):
                dve.wait_ge(ostd_ok, h + 1)
                link(v.reciprocal(o_std[:, h % 2], o_std[:, h % 2]))
                link(v.tensor_tensor(o_std[:, h % 2], bank(2 + h), o_std[:, h % 2], ALU.mult))
                v.scalar_tensor_tensor(out=gT[:, h], in0=o_std[:, h % 2], scalar=small["par"][:, 76:77], in1=gT[:, h],
                                       op0=ALU.mult, op1=ALU.mult).then_inc(ygla_ok, 1)
            for t in range(NT):
                dve.wait_ge(ystd_ok, t + 1)
                link(v.reciprocal(small["yr"][:, t:t + 1], small["ystd"][:, t:t + 1]))
                v.scalar_tensor_tensor(out=x2[:, t], in0=bank(2 * t, 2), scalar=small["yr"][:, t:t + 1], in1=gate1,
                                       op0=ALU.mult, op1=ALU.mult).then_inc(x2_ok, 1)
                dve.wait_ge(x2_ok, 2 * t + 1)
                dve.wait_ge(xag_in[t % 2], 16 * (t // 2 + 1))
                v.tensor_tensor(x2[:, t], x2[:, t], x_again[:, t % 2], ALU.add).then_inc(x2_ok, 1)
                dve.wait_ge(x2std_ok, t + 1)
                link(v.reciprocal(small["x2r"][:, t:t + 1], small["x2std"][:, t:t + 1]))
                link(v.scalar_tensor_tensor(out=h2[:, t], in0=x2[:, t], scalar=small["x2r"][:, t:t + 1], in1=scale2,
                                            op0=ALU.mult, op1=ALU.mult))
                v.tensor_tensor(h2[:, t], h2[:, t], shift2, ALU.add).then_inc(h2_ok, 1)
            for k in range(1, KD, 2):
                dve.wait_ge(h2T_up, k + 1)
                v.tensor_copy(h2T[:, k], bank(k)).then_inc(h2T_v, 1)

            dve.wait_ge(logit_mm, 1)
            E4 = (P, NT, EXPERTS)
            lg = bank(0)[:, 0:NT * EXPERTS].rearrange("p (t e) -> p t e", t=NT)
            wide = lambda a: a.unsqueeze(2).broadcast_to(E4)
            link(v.tensor_reduce(R["a"], lg, AX.X, ALU.max))
            v.tensor_tensor(R["sh"], lg, wide(R["a"]), ALU.subtract).then_inc(exp_in, 1)
            dve.wait_ge(exp_ok, 1)
            link(v.tensor_reduce(R["a"], R["p"], AX.X, ALU.add))
            link(v.reciprocal(R["a"], R["a"]))
            link(v.tensor_tensor(R["p"], R["p"], wide(R["a"]), ALU.mult))
            link(v.tensor_tensor(R["sel"], R["p"], small["brow"].unsqueeze(1).broadcast_to(E4), ALU.add))
            s4 = R["sel"].rearrange("p t (g i) -> p (t g) i", i=4)
            q = [R["q"][:, i] for i in range(4)]
            link(v.tensor_tensor(q[0], s4[:, :, 0], s4[:, :, 1], ALU.max))
            link(v.tensor_tensor(q[1], s4[:, :, 0], s4[:, :, 1], ALU.min))
            link(v.tensor_tensor(q[2], s4[:, :, 2], s4[:, :, 3], ALU.max))
            link(v.tensor_tensor(q[3], s4[:, :, 2], s4[:, :, 3], ALU.min))
            link(v.tensor_tensor(q[1], q[1], q[3], ALU.max))
            link(v.tensor_tensor(q[3], q[0], q[2], ALU.min))
            link(v.tensor_tensor(q[0], q[0], q[2], ALU.max))
            link(v.tensor_tensor(q[1], q[1], q[3], ALU.max))
            link(v.tensor_tensor(q[0], q[0], q[1], ALU.add))
            gs = q[0].rearrange("p (t g) -> p t g", g=GROUPS)
            gm = q[1].rearrange("p (t g) -> p t g", g=GROUPS)
            G4 = (P, NT, GROUPS)
            link(v.tensor_reduce(R["a"], gs, AX.X, ALU.max))
            link(v.tensor_tensor(gm, gs, R["a"].unsqueeze(2).broadcast_to(G4), ALU.is_ge))
            link(v.tensor_tensor(gm, gm, small["gkey"].unsqueeze(1).broadcast_to(G4), ALU.mult))
            link(v.tensor_reduce(R["a"], gm, AX.X, ALU.max))
            link(v.tensor_tensor(gm, gm, R["a"].unsqueeze(2).broadcast_to(G4), ALU.is_equal))
            gw = q[1].unsqueeze(2).broadcast_to((P, NT * GROUPS, 4))
            link(v.tensor_tensor(s4, s4, gw, ALU.mult))
            link(v.tensor_scalar(q[1], q[1], -1.0, BIG, ALU.add, ALU.mult))
            link(v.tensor_tensor(s4, s4, gw, ALU.add))
            for k in range(2):
                hot = R["hot"][k]
                link(v.tensor_reduce(R["a"], R["sel"], AX.X, ALU.max))
                link(v.tensor_tensor(hot, R["sel"], wide(R["a"]), ALU.is_ge))
                link(v.tensor_tensor(hot, hot, small["key"].unsqueeze(1).broadcast_to(E4), ALU.mult))
                link(v.tensor_reduce(R["kmax"][:, k], hot, AX.X, ALU.max))
                link(v.tensor_tensor(hot, hot, wide(R["kmax"][:, k]), ALU.is_equal))
                if k == 0:
                    link(v.scalar_tensor_tensor(out=R["sel"], in0=hot, scalar=-3.0 * BIG, in1=R["sel"], op0=ALU.mult, op1=ALU.add))
            v.tensor_tensor(R["sh"], R["hot"][0], R["hot"][1], ALU.add).then_inc(mask_ok, 1)
            for k in range(2):
                link(v.tensor_tensor(R["sel"], R["p"], R["hot"][k], ALU.mult))
                link(v.tensor_reduce(R["w"][:, k], R["sel"], AX.X, ALU.add))
            link(v.tensor_tensor(R["a"], R["w"][:, 0], R["w"][:, 1], ALU.add))
            link(v.reciprocal(R["a"], R["a"]))
            wts = small["wts"].rearrange("p (k t) -> p k t", k=2)
            link(v.tensor_tensor(wts, R["w"], R["a"].unsqueeze(1).broadcast_to((P, 2, NT)), ALU.mult))
            dve.wait_ge(rank_mm, 1)
            rank = bank(1)[:, 0:NT * EXPERTS].rearrange("p (t e) -> p t e", t=NT)
            for k in range(2):
                link(v.tensor_tensor(R["sel"], rank, R["hot"][k], ALU.mult))
                link(v.tensor_reduce(R["w"][:, k], R["sel"], AX.X, ALU.add))
            link(v.tensor_scalar(R["sum"], R["w"], float(BLOCK), None, ALU.is_ge))
            for m in range(2, ROUNDS):
                link(v.scalar_tensor_tensor(out=R["sum"], in0=R["w"], scalar=float(m * BLOCK), in1=R["sum"], op0=ALU.is_ge, op1=ALU.add))
            link(v.scalar_tensor_tensor(out=R["w"], in0=R["sum"], scalar=float((EXPERTS - 1) * BLOCK), in1=R["w"], op0=ALU.mult, op1=ALU.add))
            link(v.scalar_tensor_tensor(out=R["w"], in0=R["kmax"], scalar=-float(BLOCK), in1=R["w"], op0=ALU.mult, op1=ALU.add))
            link(v.tensor_scalar(pos.rearrange("p (k t) -> p k t", k=2), R["w"], float(EXPERTS * BLOCK), None, ALU.add))
            link(v.tensor_reduce(R["a"][:, 0:1], bank(1)[:, NT * EXPERTS:(NT + 1) * EXPERTS], AX.X, ALU.max))
            v.tensor_copy(count, R["a"][:, 0:1]).then_inc(pos_ok, 1)

            def split13(i, p):
                dve.wait_ge(hi13_ok, KD * i + p + 1)
                v.tensor_tensor(lo13[:, p % 4], raw13[:, p], hi13[:, p % 4].bitcast(f32), ALU.subtract).then_inc(lo13_ok, 1)

            def split2(i, p):
                dve.wait_ge(hi2_ok, 6 * i + p + 1)
                n = P if p < FULL else LAST
                v.tensor_tensor(lo2[0:n, p % 3], raw2[0:n, p], hi2[0:n, p % 3].bitcast(f32), ALU.subtract).then_inc(lo2_ok, 1)

            def gate(i):
                dve.wait_ge(silu_ok, i + 1)
                reach(dve, heT_up, i)
                v.tensor_tensor(he[:, 0:F].rearrange("p (b n) -> p b n", b=2), s_act.rearrange("p (b n) -> p b n", b=2), H3,
                                ALU.mult).then_inc(he_ok, 1)

            def he_low(i):
                dve.wait_ge(hehi_ok, i + 1)
                v.tensor_tensor(he_lo.rearrange("p k n -> p (k n)"), bank(TB, 2)[:, 0:6 * P],
                                he_hi.rearrange("p k n -> p (k n)").bitcast(f32), ALU.subtract).then_inc(helo_ok, 1)

            def y_out(i):
                dve.wait_ge(fed2, 6 * (i + 1))
                reach(dve, ye_out, 16 * i)
                v.tensor_copy(y_e[:, BANK:], bank(YB + 1)).then_inc(ye_v, 1)

            def one_pass(i0):
                for p in range(KD):
                    split13(i0, p)
                gate(i0)
                for p in range(4):
                    split13(i0 + 1, p)
                he_low(i0)

                def body(i):
                    for p in range(4, KD):
                        split13(i, p)
                    for p in range(3):
                        split2(i - 1, p)
                    gate(i)
                    for p in range(3, 6):
                        split2(i - 1, p)
                    for p in range(4):
                        split13(i + 1, p)
                    y_out(i - 1)
                    he_low(i)

                body(i0 + 1)
                with dve.Fori(2, EXPERTS - 1) as e:
                    body(dve.snap(i0 + e))
                i = i0 + EXPERTS - 1
                for p in range(4, KD):
                    split13(i, p)
                for p in range(3):
                    split2(i - 1, p)
                gate(i)
                for p in range(3, 6):
                    split2(i - 1, p)
                for p in range(3):
                    split2(i, p)
                y_out(i - 1)
                he_low(i)
                for p in range(3, 6):
                    split2(i, p)
                y_out(i)

            dve.wait_ge(scattered, 32 * NT)
            link(v.memset(he[:, F:], 0.0))
            one_pass(0)
            over = most(dve)
            with dve.If(over > threshold):
                with dve.Fori(1, ROUNDS) as r:
                    one_pass(dve.snap(r * EXPERTS))
            for t in range(NT):
                dve.wait_ge(back_in[t], 32)
                v.tensor_scalar(mixed[:, t], back[:, t, 0], small["wts"][:, t:t + 1], None, ALU.mult).then_inc(f_mix, 1)
                dve.wait_ge(f_mix, 2 * t + 1)
                v.scalar_tensor_tensor(out=mixed[:, t], in0=back[:, t, 1], scalar=small["wts"][:, NT + t:NT + t + 1],
                                       in1=mixed[:, t], op0=ALU.mult, op1=ALU.add).then_inc(f_mix, 1)
                dve.wait_ge(f_std, t + 1)
                v.reciprocal(small["fr"][:, t:t + 1], small["fstd"][:, t:t + 1]).then_inc(f_r, 1)
                dve.wait_ge(f_r, 2 * t + 1)
                v.scalar_tensor_tensor(out=result[:, t], in0=mixed[:, t], scalar=small["fr"][:, t:t + 1], in1=gate2,
                                       op0=ALU.mult, op1=ALU.mult).then_inc(f_r, 1)
                dve.wait_ge(f_r, 2 * t + 2)
                v.tensor_tensor(result[:, t], result[:, t], x2[:, t], ALU.add).then_inc(f_ok, 1)

        @block.tensor
        def _(pe):
            mm = nc.tensor.matmul
            pe.wait_ge(consts, 9)
            pe.wait_ge(par_in, 16 * 8)
            nc.tensor.transpose(bank(7)[:, 0:77], par_rows, ident[0:77, 0:77])
            for j in range(NC):
                last = nc.tensor.transpose(bank(7)[:, 128 + 32 * j:128 + 32 * j + WIDTH], dw_rows[:, j * P:(j + 1) * P],
                                           ident[0:WIDTH, 0:WIDTH])
            last.then_inc(cols_up, 1)

            def x_up(k):
                for t in range(NT):
                    if k == 0:
                        pe.wait_ge(xhat_ok, t + 1)
                    last = nc.tensor.transpose(bank(k)[:, t * P:(t + 1) * P], xhat[:, t, k * P:(k + 1) * P], ident)
                last.then_inc(xT_up, 1)

            for k in range(KD - 1):
                x_up(k)
            pe.wait_ge(cols_ok, 1)
            for b in range(4):
                pe.wait_ge(ada_summed, b + 1)
                for j in range(4):
                    last = mm(bank(7)[:, 4 * b + j:4 * b + j + 1], ada_sum[:, b % 2, j * P:(j + 1) * P], ones[:, 0:1],
                              start=True, stop=True)
                last.then_inc(ada_mm, 1)
            pe.wait_ge(mod1_ok, 1)
            x_up(KD - 1)

            def ada_row(r):
                b = 4 + r
                pe.wait_ge(ada_summed, b + 1)
                pe.wait_ge(bias_in[b % 2], 16 * (r // 2 + 1))
                reach(pe, ada_taken, r - 1)
                dst = bank(6 + r % 2)
                mm(dst, ones, ada_sum[:, b % 2], start=True, stop=False)
                mm(dst, ones[0:1, :], ada_bias[0:1, b % 2], start=False, stop=True).then_inc(ada_mm, 1)

            pe.wait_ge(hT_a, KD // 2)
            pe.wait_ge(hT_v, KD // 2)
            pe.wait_ge(conv_in, 32)
            for j in range(NC):
                reach(pe, u_ok, j - 1)
                for h in range(2):
                    for k in range(KD):
                        last = mm(bank(2 * (j % 2) + h), w_conv[:, k, h * CONV + j * P:h * CONV + (j + 1) * P], hT[:, k],
                                  start=k == 0, stop=k == KD - 1)
                    last.then_inc(conv_mm, 1)
                if j >= 1:
                    ada_row(j - 1)
            pe.wait_ge(rest_in, 32)
            for u, (what, i) in enumerate(UNITS):
                if u < 2:
                    pass
                elif u < 4:
                    pe.wait_ge(u_ok, NC)
                else:
                    pe.wait_ge(unit_ok, u - 3)
                b = bank(UNIT_BANK[u % 4])
                for k in range(KD):
                    w = w_rest[:, k]
                    se = dict(start=k == 0, stop=k == KD - 1)
                    if what == "lr":
                        last = mm(b[0:RANK, :], w[:, C_LR:C_LR + RANK], hT[:, k], **se)
                    elif what == "kv":
                        t, h = i // 2, i % 2
                        last = mm(b[:, 0:KV_HALF], hT[:, k, t * P:(t + 1) * P], w[:, C_K + h * KV_HALF:C_K + (h + 1) * KV_HALF], **se)
                    elif what == "q":
                        last = mm(b, w[:, i * P:(i + 1) * P], hT[:, k], **se)
                    else:
                        last = mm(b, w[:, C_G + i * P:C_G + (i + 1) * P], hT[:, k], **se)
                last.then_inc(unit_mm, 1)
                if u < 5:
                    ada_row(3 + u)
                if (what, i) == ("q", 0):
                    pe.wait_ge(unit_ok, 1)
                    pe.wait_ge(rows_in, 96)
                    pe.wait_ge(u_ok, NC)
                    for t in range(NT):
                        last = mm(bank(2, 2)[:, t * QK:(t + 1) * QK], lrT[:, t * P:(t + 1) * P], w_up, start=True, stop=True)
                    last.then_inc(z_mm, 1)
                if (what, i) == ("g", 1):
                    pe.wait_ge(soft_ok, 1)
                    pe.wait_ge(ada_taken, 8)
                    for t in range(NT):
                        for p in range(2):
                            mm(bank(6)[:, p * NCH + 2 * t:p * NCH + 2 * t + 2], soft_l[:, t, p * P:(p + 1) * P], small["half"],
                               start=True, stop=True)
                    for t in range(NT):
                        last = mm(bank(2, 2)[:, t * QK:(t + 1) * QK], later, soft_l[:, t], start=True, stop=True)
                    last.then_inc(later_mm, 1)
            pe.wait_ge(kdec_ok, 2)
            for n in range(NCH):
                reach(pe, state_ok, 4 * (n - 1))
                for p in range(2):
                    last = mm(bank(6 + n % 2)[:, p * QK:(p + 1) * QK], k_dec[:, n // 2, n % 2, p * P:(p + 1) * P],
                              kv[:, n // 2, QK + p * QK:QK + (p + 1) * QK], start=True, stop=True)
                last.then_inc(upd_mm, 1)
            pe.wait_ge(unit_ok, len(UNITS))
            pe.wait_ge(tap_ok, NC * WIDTH)
            for j in range(NC):
                last = mm(bank(0), ones, conv[:, j], start=j == 0, stop=j == NC - 1)
            last.then_inc(mean_mm, 1)
            for h in range(HEADS):
                rows = slice(h % 2 * DK, (h % 2 + 1) * DK)
                for n in range(NCH):
                    pe.wait_ge(state_ok, 4 * n + 4)
                    last = mm(bank(2 + h)[:, n * CHUNK:(n + 1) * CHUNK], state[rows, n, h // 2],
                              qT[rows, h // 2, n * CHUNK:(n + 1) * CHUNK], start=True, stop=True)
                last.then_inc(o_mm, 1)
            for j in range(NC):
                pe.wait_ge(csq_ok, j + 1)
                mm(bank(1), ones, o_sq[:, j % 2], start=j == 0, stop=j == NC - 1).then_inc(var_mm, 1)
            for h in range(HEADS):
                pe.wait_ge(osq_ok, h + 1)
                reach(pe, ostd_ok, h - 1)
                mm(bank(6 + h % 2), ones, o_sq[:, h % 2], start=True, stop=True).then_inc(osum_mm, 1)
            pe.wait_ge(w_out_in, 16)
            pe.wait_ge(cstd_ok, 1)
            pe.wait_ge(yconv_ok, NC)
            pe.wait_ge(ygla_ok, HEADS)
            for t in range(NT):
                for k in range(KD):
                    src = conv[:, k] if k < NC else gT[:, k - NC]
                    for h in range(2):
                        last = mm(bank(2 * t + h), src[:, t * P:(t + 1) * P], w_o[:, k, h * BANK:(h + 1) * BANK],
                                  start=k == 0, stop=k == KD - 1)
                last.then_inc(y_mm, 1)
            for k in range(KD):
                for t in range(NT):
                    if k == 0:
                        pe.wait_ge(h2_ok, t + 1)
                    last = nc.tensor.transpose(bank(k)[:, t * P:(t + 1) * P], h2[:, t, k * P:(k + 1) * P], ident)
                last.then_inc(h2T_up, 1)
            pe.wait_ge(w_r_in, 16)
            pe.wait_ge(h2T_a, KD // 2)
            pe.wait_ge(h2T_v, KD // 2)
            for t in range(NT):
                for k in range(KD):
                    last = mm(bank(0)[:, t * EXPERTS:(t + 1) * EXPERTS], h2T[:, k, t * P:(t + 1) * P], w_r[:, k],
                              start=k == 0, stop=k == KD - 1)
            last.then_inc(logit_mm, 1)
            pe.wait_ge(mask_ok, 1)
            for t in range(NT):
                dst = bank(1)[:, t * EXPERTS:(t + 1) * EXPERTS]
                mm(dst, before, R["sh"][:, t], start=True, stop=t == 0)
                for s in range(t):
                    mm(dst, ones, R["sh"][:, s], start=False, stop=s == t - 1)
            for s in range(NT):
                last = mm(bank(1)[:, NT * EXPERTS:(NT + 1) * EXPERTS], ones, R["sh"][:, s], start=s == 0, stop=s == NT - 1)
            last.then_inc(rank_mm, 1)

            def turn_x(i):
                pe.wait_ge(xe_in, 16 * (i + 1))
                reach(pe, helo_ok, i - 1)
                for k in range(KD):
                    last = nc.tensor.transpose(bank(TB, 2)[:, k * P:(k + 1) * P], xe[:, k * P:(k + 1) * P], ident)
                last.then_inc(xeT_up, 1)

            def first(i):
                pe.wait_ge(xhl_ok, 2 * i + 2)
                reach(pe, he_ok, i)
                for p in range(KD):
                    pe.wait_ge(lo13_ok, KD * i + p + 1)
                    for n, (s, w) in enumerate(((x_hi, hi13), (x_hi, lo13), (x_lo, hi13))):
                        for b in range(4):
                            last = mm(bank(b)[:, 0:F2], s[:, p], w[:, p % 4, b * F2:(b + 1) * F2],
                                      start=p == 0 and n == 0, stop=p == KD - 1 and n == 2)
                    last.then_inc(fed13, 1)

            def second(i):
                reach(pe, helo_ok, i + 1)
                reach(pe, ye_a, i)
                reach(pe, ye_v, i)
                for p in range(6):
                    pe.wait_ge(lo2_ok, 6 * i + p + 1)
                    n_ = P if p < FULL else LAST
                    for n, (s, w) in enumerate(((he_hi, hi2), (he_hi, lo2), (he_lo, hi2))):
                        for b in range(2):
                            last = mm(bank(YB + b), s[0:n_, p], w[0:n_, p % 3, b * BANK:(b + 1) * BANK],
                                      start=p == 0 and n == 0, stop=p == 5 and n == 2)
                    last.then_inc(fed2, 1)

            def turn_he(i):
                pe.wait_ge(he_ok, i + 1)
                pe.wait_ge(xeT_ok, i + 2) if not last_of_pass[0] else pe.wait_ge(xeT_ok, i + 1)
                for k in range(6):
                    last = nc.tensor.transpose(bank(TB, 2)[:, k * P:(k + 1) * P], he[:, k * P:(k + 1) * P], ident)
                last.then_inc(heT_up, 1)

            last_of_pass = [False]

            def one_pass(i0):
                last_of_pass[0] = False
                turn_x(i0)
                first(i0)
                turn_x(i0 + 1)
                turn_he(i0)
                with pe.Fori(1, EXPERTS - 1) as e:
                    i = pe.snap(i0 + e)
                    first(i)
                    turn_x(i + 1)
                    second(i - 1)
                    turn_he(i)
                i = i0 + EXPERTS - 1
                first(i)
                second(i - 1)
                last_of_pass[0] = True
                turn_he(i)
                second(i)

            one_pass(0)
            over = most(pe)
            with pe.If(over > threshold):
                with pe.Fori(1, ROUNDS) as r:
                    one_pass(pe.snap(r * EXPERTS))


def kernel(**inputs):
    import numpy as np
    import concourse.bacc as bacc
    from concourse.bass_utils import run_bass_kernel_spmd

    nc = bacc.Bacc("TRN2", target_bir_lowering=False, num_devices=1)
    arrays, args = {}, {}
    for name in ("x", "c", "w_ada", "b_ada", "g_pre_mix", "g_post_mix", "g_pre_ffn", "g_post_ffn", "w_in", "w_dw",
                 "b_dw", "conv_ln_g", "conv_ln_b", "w_gate_up", "b_gate", "gla_norm_g", "w_out", "w_router",
                 "b_router", "w1", "w3", "w2"):
        a = np.ascontiguousarray(inputs[name])
        arrays[f"in_{name}"] = a
        args[name] = nc.dram_tensor(f"in_{name}", a.shape, mybir.dt.from_np(a.dtype), kind="ExternalInput").ap()
    out = nc.dram_tensor("out", (1, T, D), mybir.dt.float32, kind="ExternalOutput").ap()
    build(nc, out=out, **args)
    result = run_bass_kernel_spmd(nc, [arrays], core_ids=[0])
    return result.results[0]["out"]
```

```python
import concourse.bass as bass
from concourse import mybir

P = 128
BANK = 512
T, D = 512, 1024
NT, KD = T // P, D // P
CONV, WIDTH = 512, 31
SHARED = 19
NC = CONV // P
HEADS, DK, DV, CHUNK = 4, 64, 128, 64
QK = HEADS * DK
NCH = T // CHUNK
RANK, TAU = 16, 16.0
SUMS = 4
UNIT = 256
EXPERTS, GROUPS, F = 16, 4, 704
FULL, LAST = F // P, F % P
F2 = F // 2
BLOCK = 128
ROUNDS = T // BLOCK
EPS = 1e-6
BIG = 1e30


def build(nc, x, c, w_ada, b_ada, g_pre_mix, g_post_mix, g_pre_ffn, g_post_ffn, w_in, w_dw, b_dw,
          conv_ln_g, conv_ln_b, w_gate_up, b_gate, gla_norm_g, w_out, w_router, b_router,
          w1, w3, w2, out, threshold=BLOCK):
    f32, f32r = mybir.dt.float32, mybir.dt.float32r
    i32, u32, bf16 = mybir.dt.int32, mybir.dt.uint32, mybir.dt.bfloat16
    ALU, ACT, AX = mybir.AluOpType, mybir.ActivationFunctionType, mybir.AxisListType

    base = (nc.sbuf_base + 31) // 32 * 32

    def at(name, shape, dt, offset):
        return nc.alloc_sbuf_tensor_at(name, list(shape), dt, offset=base + 4 * offset).ap()

    PIECE = 2 * F
    RAW, SPLIT = 0, KD * PIECE + 6 * D
    KEEP = 2 * SPLIT
    raw13 = at("raw13", [P, KD, PIECE], f32, RAW)
    raw2 = at("raw2", [P, 6, D], f32, RAW + KD * PIECE)
    ada_w = at("ada_w", [P, 2, KD, BANK], f32, RAW)
    w_o = at("w_o", [P, KD, D], f32, RAW)
    w_i = at("w_i", [P, 2, KD, UNIT], f32, RAW + 8192)
    o = RAW + 12288
    ada_sum = at("ada_sum", [P, SUMS, BANK], f32, o)
    ada_bias = at("ada_bias", [P, 2, BANK], f32, o + 2048)
    lrT = at("lrT", [RANK + 1, T], f32, o + 3072)
    w_up = at("w_up", [RANK + 1, QK], f32, o + 3584)
    k_dec = at("k_dec", [P, NT, 2, QK], f32, o)
    state = at("state", [P, NCH, 2, DV], f32, o + 2048)
    h2 = at("h2", [P, NT, D], f32, o)
    o += 4096
    dw_rows = at("dw_rows", [WIDTH, CONV], f32, o)
    zero = at("zero", [P, 256], f32, o)
    par_rows = at("par_rows", [77, P], f32, o + 512)
    dwT = at("dwT", [P, NC, WIDTH], f32, o + 640)
    hi13 = at("hi13", [P, 4, PIECE], f32r, SPLIT)
    lo13 = at("lo13", [P, 4, PIECE], f32r, SPLIT + 4 * PIECE)
    hi2 = at("hi2", [P, 3, D], f32r, SPLIT + 8 * PIECE)
    lo2 = at("lo2", [P, 3, D], f32r, SPLIT + 8 * PIECE + 3 * D)
    wi_hi = at("wi_hi", [P, 2, KD, UNIT], f32r, SPLIT)
    wi_lo = at("wi_lo", [P, 2, KD, UNIT], f32r, SPLIT + 4096)
    hT_hi = at("hT_hi", [P, KD, T], f32r, SPLIT + 8192)
    hT_lo = at("hT_lo", [P, KD, T], f32r, SPLIT + 12288)
    wo_hi = at("wo_hi", [P, KD, D], f32r, SPLIT)
    wo_lo = at("wo_lo", [P, KD, D], f32r, SPLIT + 8192)
    gate1 = at("gate1", [P, D], f32, SPLIT + 16384)
    o = KEEP
    ident = at("ident", [P, P], f32, o)
    ones = at("ones", [P, P], f32, o + 128)
    later = at("later", [P, P], f32, o + 256)
    w_r = at("w_r", [P, KD, EXPERTS], f32, o + 256)
    before = at("before", [P, P], bf16, o + 384)
    ones_b = at("ones_b", [P, P], bf16, o + 448)
    o += 512
    SMALLS = 296
    smalls = at("smalls", [P, SMALLS], f32, o)
    small, o = {}, 0
    for name, n in (("par", 80), ("half", 2), ("csil", 8), ("A1", 8), ("B1", 8), ("modc", 16), ("eps", 1),
                    ("xss", 4), ("xstd", 4), ("xr", 4), ("yss", 4), ("ystd", 4), ("yr", 4), ("x2ss", 4),
                    ("x2std", 4), ("x2r", 4), ("decay", 16), ("brow", 16), ("wts", 8), ("fss", 4),
                    ("fstd", 4), ("fr", 4), ("key", 16), ("gkey", 4), ("ostd", 16), ("or", 16)):
        small[name] = smalls[:, o:o + n]
        o += n
    pos = smalls[:, o:o + 8].bitcast(u32)
    count = smalls[:, o + 8:o + 9].bitcast(i32)
    assert o + 9 <= SMALLS
    o = KEEP + 512 + SMALLS
    gate2 = at("gate2", [P, D], f32, o)
    scale2 = at("scale2", [P, D], f32, o + 1024)
    shift2 = at("shift2", [P, D], f32, o + 2048)
    o += 3072
    x2 = at("x2", [P, NT, D], f32, o)
    soft_l = at("soft_l", [P, NT, QK], f32, o)
    w_lr = at("w_lr", [P, KD, P], f32, o)
    soft_m = at("soft_m", [P, NT, QK], f32, o + 1024)
    o_sq = at("o_sq", [P, 2, BANK], f32, o + 2048)
    sig = at("sig", [P, 2, BANK], f32, o + 2048)
    o_std = at("o_std", [P, 2, BANK], f32, o + 3072)
    h_tmp = at("h_tmp", [P, 2, BANK], f32, o + 3072)
    term = at("term", [P, 2, BANK], f32, o + 3072)
    o += 4096
    x_rows = at("x_rows", [P, NT, D], f32, o)
    lr_hi = at("lr_hi", [P, KD, P], f32r, o)
    lr_lo = at("lr_lo", [P, KD, P], f32r, o + 1024)
    kv = at("kv", [P, NT, 3 * QK], f32, o)
    g_hi = at("g_hi", [P, HEADS, T], f32r, o)
    gT = at("gT", [P, HEADS, T], f32, o + 3072)
    g_lo = at("g_lo", [P, HEADS, T], f32r, o + 3072)
    h2T = at("h2T", [P, NT + 1, KD, P], f32, o)
    y_tmp = at("y_tmp", [P, D], f32, o + 2048)
    zero_more = at("zero_more", [P, 256], f32, o + 4096)
    xe = at("xe", [P, D], f32, o)
    xeT = at("xeT", [P, KD, P], f32, o + 1024)
    x_hi = at("x_hi", [P, KD, P], f32r, o + 2048)
    x_lo = at("x_lo", [P, KD, P], f32r, o + 3072)
    o += 5120
    xhat = at("xhat", [P, NT, D], f32, o)
    conv = at("conv", [P, NC, T], f32, o)
    conv_lo = at("conv_lo", [P, NC, T], f32r, o)
    uT = at("uT", [P, NC, WIDTH - 1 + T], f32, o + 2048)
    conv_hi = at("conv_hi", [P, NC, T], f32r, o + 2048)
    rt = at("rt", [P, 1024], f32, o + 2048)
    s_act = at("s_act", [P, F], f32, o)
    he = at("he", [P, 6 * P], f32, o + 704)
    he_hi = at("he_hi", [P, 6, P], f32r, o + 1472)
    he_lo = at("he_lo", [P, 6, P], f32r, o + 2240)
    y_e = at("y_e", [P, D], f32, o + 3008)
    o += 4216
    qT = at("qT", [P, 2, T], f32, o)
    junk = at("junk", [P, D], f32, o)
    o += 1024
    assert base + 4 * o <= nc.sbuf_usable_end, (base + 4 * o, nc.sbuf_usable_end)
    back = at("back", [P, NT, 2, D], f32, RAW)
    mixed = at("mixed", [P, NT, D], f32, SPLIT)
    result = at("result", [P, NT, D], f32, SPLIT + 4096)

    psum = nc.alloc_psum_tensor("psum", [P, 8 * BANK], f32).ap()

    def bank(b, n=1):
        return psum[:, b * BANK:(b + n) * BANK]

    H1 = psum[:, 0:2 * BANK].rearrange("p (b n) -> p b n", b=2)[:, :, 0:F2]
    H3 = psum[:, 2 * BANK:4 * BANK].rearrange("p (b n) -> p b n", b=2)[:, :, 0:F2]
    TB, YB = 4, 6

    table = nc.dram_tensor("table", (ROUNDS * EXPERTS, BLOCK, D), f32).ap()
    table_y = nc.dram_tensor("table_y", (ROUNDS * EXPERTS, BLOCK, D), f32).ap()
    table_rows = table.rearrange("b p d -> (b p) d")
    table_y_rows = table_y.rearrange("b p d -> (b p) d")

    w_ada_v = w_ada[0].rearrange("(k p) n -> p k n", p=P)
    w_in_v = w_in[0].rearrange("(k p) n -> p k n", p=P)
    x_v = x[0].rearrange("(t p) d -> p t d", p=P)
    out_v = out[0].rearrange("(t p) d -> p t d", p=P)
    w1_v = w1[0].rearrange("e (k p) f -> e p k f", p=P)
    w3_v = w3[0].rearrange("e (k p) f -> e p k f", p=P)
    w2_v = w2[0, :, 0:FULL * P, :].rearrange("e (k p) d -> e p k d", p=P)

    def sem(name):
        return nc.alloc_semaphore(name)

    par_in, consts, cols_up, cols_ok = map(sem, ("par_in", "consts", "cols_up", "cols_ok"))
    x_in = [sem(f"x_in{t}") for t in range(NT)]
    ada_in = [sem(f"ada_in{i}") for i in range(2)]
    bias_in, lr_zero, diag_ok, spread_mm = map(sem, ("bias_in", "lr_zero", "diag_ok", "spread_mm"))
    ada_summed, ada_mm, ada_taken = map(sem, ("ada_summed", "ada_mm", "ada_taken"))
    w_out_in, rows_in, w_r_in, lr_in = map(sem, ("w_out_in", "rows_in", "w_r_in", "lr_in"))
    wi_in = [sem(f"wi_in{i}") for i in range(2)]
    wi_hi_ok, wi_lo_ok, wo_hi_ok, wo_lo_ok, lrw_ok, biased = map(
        sem, ("wi_hi_ok", "wi_lo_ok", "wo_hi_ok", "wo_lo_ok", "lrw_ok", "biased"))
    yhi_ok, ylo_ok, tmp_ok, lr_mm = map(sem, ("yhi_ok", "ylo_ok", "tmp_ok", "lr_mm"))
    x_again = [sem(f"x_again{i}") for i in range(2)]
    xhat_ok, xT_up, mod1_ok, hT_a, hT_v = map(sem, ("xhat_ok", "xT_up", "mod1_ok", "hT_a", "hT_v"))
    conv_mm, sig_ok, u_ok = map(sem, ("conv_mm", "sig_ok", "u_ok"))
    unit_mm, unit_ok, z_mm, gate_parts, soft_ok, later_mm = map(
        sem, ("unit_mm", "unit_ok", "z_mm", "gate_parts", "soft_ok", "later_mm"))
    decay_ok, kdec_ok, upd_mm, state_ok, tap_ok = map(sem, ("decay_ok", "kdec_ok", "upd_mm", "state_ok", "tap_ok"))
    mean_mm, cent_ok, csq_ok, var_mm, cstd_ok, cnorm_ok, yconv_ok = map(
        sem, ("mean_mm", "cent_ok", "csq_ok", "var_mm", "cstd_ok", "cnorm_ok", "yconv_ok"))
    o_mm, osq_ok, osum_mm, ostd_ok, ygla_ok = map(sem, ("o_mm", "osq_ok", "osum_mm", "ostd_ok", "ygla_ok"))
    y_mm, yss_ok, ystd_ok, x2_ok, x2ss_ok, x2std_ok, h2_ok = map(
        sem, ("y_mm", "yss_ok", "ystd_ok", "x2_ok", "x2ss_ok", "x2std_ok", "h2_ok"))
    h2T_up, h2T_a, h2T_v, logit_mm, exp_ok, exp_in, mask_ok, rank_mm, pos_ok = map(
        sem, ("h2T_up", "h2T_a", "h2T_v", "logit_mm", "exp_ok", "exp_in", "mask_ok", "rank_mm", "pos_ok"))
    zero_ok, cleared, cleared_more, scattered = map(sem, ("zero_ok", "cleared", "cleared_more", "scattered"))
    first_tap, term_ok, term_added = map(sem, ("first_tap", "term_ok", "term_added"))
    eps_ok, xr_ok = map(sem, ("eps_ok", "xr_ok"))
    act_step, pool_step, dve_step = map(sem, ("act_step", "pool_step", "dve_step"))
    raw13_in = [sem(f"raw13_in{i}") for i in range(4)]
    raw2_in = [sem(f"raw2_in{i}") for i in range(3)]
    hi13_ok, lo13_ok, fed13, hi2_ok, lo2_ok, fed2 = map(
        sem, ("hi13_ok", "lo13_ok", "fed13", "hi2_ok", "lo2_ok", "fed2"))
    xe_in, xeT_up, xeT_ok, xhl_ok = map(sem, ("xe_in", "xeT_up", "xeT_ok", "xhl_ok"))
    silu_ok, he_ok, heT_up, hehi_ok, helo_ok = map(
        sem, ("silu_ok", "he_ok", "heT_up", "hehi_ok", "helo_ok"))
    ye_a, ye_v, ye_out = map(sem, ("ye_a", "ye_v", "ye_out"))
    back_in = [sem(f"back_in{i}") for i in range(NT)]
    f_okp, f_m1, f_mix, f_ss, f_std, f_r, f_ok, stored = map(sem, ("f_okp", "f_m1", "f_mix", "f_ss", "f_std", "f_r", "f_ok", "stored"))

    def reach(eng, s, value):
        if not isinstance(value, int) or value > 0:
            eng.wait_ge(s, value)

    def chain(eng, s):
        n = [0]

        def link(ins):
            ins.then_inc(s, 1)
            n[0] += 1
            eng.wait_ge(s, n[0])
        return link

    def most(eng):
        eng.wait_ge(pos_ok, 1)
        return eng.value_load(count[0:1, 0:1], min_val=0, max_val=T)

    V0 = 2 * CONV + 2 * QK
    G0 = V0 + HEADS * DV
    UNITS = ([("conv", j, (j * P, CONV + j * P)) for j in range(NC)]
             + [("kv", 0, (2 * CONV + QK,)), ("kv", 1, (V0,)), ("kv", 2, (V0 + UNIT,)), ("q", 0, (2 * CONV,)),
                ("g", 0, (G0,)), ("g", 1, (G0 + UNIT,))])
    NU = len(UNITS)
    LR0 = G0 + HEADS * DV
    PAIR = {("conv", 0): 0, ("conv", 1): 1, ("conv", 2): 2, ("conv", 3): 0, "lr": 1, ("kv", 0): 2, ("kv", 1): 0,
            ("kv", 2): 1, "z": 2, ("q", 0): 0, ("g", 0): 1, "later": 2, ("g", 1): 0}
    O_BANK = [4, 5, 0, 1]
    TILE = [0, 1, 3, 4]
    TERMS = {4: range(1, 4), 5: range(4, 7), 6: range(7, 11), 7: range(11, 15), 8: range(15, SHARED)}
    GLA_FIRST = [*range(NC, KD), *range(NC)]

    R = {}
    o = 0
    for name, shape in (("sh", (NT, EXPERTS)), ("p", (NT, EXPERTS)), ("sel", (NT, EXPERTS)), ("q", (4, NT * GROUPS)),
                        ("hot0", (NT, EXPERTS)), ("hot1", (NT, EXPERTS)), ("kmax", (2, NT)), ("w", (2, NT)),
                        ("sum", (2, NT)), ("m32", (NT, EXPERTS // 2))):
        n = shape[0] * shape[1]
        part = rt[:, o:o + n].rearrange("p (a b) -> p a b", a=shape[0])
        R[name] = part
        o += n
    R["a"] = rt[:, o:o + NT]
    R["mask"] = rt[:, o - NT * EXPERTS // 2:o].bitcast(bf16).rearrange("p (a b) -> p a b", a=NT)
    R["hot"] = [R["hot0"], R["hot1"]]

    block = nc.Block()
    with block:

        @block.sync
        def _(sp):
            row = 0
            for src, n in ((b_ada, 48), (g_pre_mix, 8)):
                sp.dma_start(par_rows[row:row + n, :], src.rearrange("o (r q) -> (o r) q", q=P)).then_inc(par_in, 16)
                row += n

            def ada(b):
                if b >= 2:
                    sp.wait_ge(ada_summed, b - 1)
                sp.dma_start(ada_w[:, b % 2], w_ada_v[:, :, b * BANK:(b + 1) * BANK]).then_inc(ada_in[b % 2], 16)

            def unit(u):
                starts = UNITS[u][2]
                n = UNIT // len(starts)
                if u >= 2:
                    sp.wait_ge(wi_lo_ok, u - 1)
                for m, c0 in enumerate(starts):
                    sp.dma_start(w_i[:, u % 2, :, m * n:(m + 1) * n], w_in_v[:, :, c0:c0 + n]).then_inc(
                        wi_in[u % 2], 32 // len(starts))

            for t in range(NT):
                sp.dma_start(x_rows[:, t], x_v[:, t]).then_inc(x_in[t], 16)
            for b in range(4):
                ada(b)
            unit(0)
            sp.wait_ge(lr_zero, 1)
            sp.dma_start(w_lr[:, :, 0:RANK], w_in_v[:, :, LR0:LR0 + RANK]).then_inc(lr_in, 16)
            unit(1)
            ada(4)
            ada(5)
            for u, blocks in ((2, (6,)), (3, (7,)), (4, (8, 9)), (5, (10,)), (6, (11,))):
                unit(u)
                for b in blocks:
                    ada(b)
            for q in range(4):
                if q < 3:
                    unit(7 + q)
                else:
                    sp.wait_ge(ada_summed, 12)
                    sp.dma_start(w_o, w_out[0].rearrange("(k p) n -> p k n", p=P)).then_inc(w_out_in, 16)
                sp.wait_ge(zero_ok, 1)
                sp.dma_start(table[0:EXPERTS, :, q * 256:(q + 1) * 256].rearrange("b p d -> p b d"),
                             zero.unsqueeze(1).broadcast_to((P, EXPERTS, 256))).then_inc(cleared, 16)

            def up(i, e):
                for g in range(4):
                    reach(sp, lo13_ok, KD * (i - 1) + 2 * (g + 1))
                    at_ = raw13[:, 2 * g:2 * g + 2]
                    sp.dma_start(at_[:, :, 0:F], w1_v[e, :, 2 * g:2 * g + 2, :]).then_inc(raw13_in[g], 16)
                    sp.dma_start(at_[:, :, F:], w3_v[e, :, 2 * g:2 * g + 2, :]).then_inc(raw13_in[g], 16)

            def down(i, e):
                for g in range(3):
                    reach(sp, lo2_ok, 6 * (i - 1) + 2 * (g + 1))
                    if g < 2:
                        sp.dma_start(raw2[:, 2 * g:2 * g + 2], w2_v[e, :, 2 * g:2 * g + 2, :]).then_inc(raw2_in[g], 32)
                    else:
                        sp.dma_start(raw2[:, 4], w2_v[e, :, 4, :]).then_inc(raw2_in[g], 16)
                        sp.dma_start(raw2[0:LAST, 5], w2[0, e, FULL * P:, :]).then_inc(raw2_in[g], 16)

            sp.wait_ge(kdec_ok, 2)
            sp.dma_start(x2[:, 0:2], x_v[:, 0:2]).then_inc(x_again[0], 16)
            sp.wait_ge(wo_lo_ok, KD)
            up(0, 0)
            sp.wait_ge(ygla_ok, HEADS)
            sp.wait_ge(cnorm_ok, NC)
            sp.dma_start(x2[:, 2:4], x_v[:, 2:4]).then_inc(x_again[1], 16)
            sp.wait_ge(scattered, 32 * NT)
            sp.wait_ge(cleared, 64)
            sp.wait_ge(tap_ok, NC * WIDTH - SHARED)

            def one_pass(i0):
                up(i0 + 1, 1)
                down(i0, 0)
                with sp.Fori(2, EXPERTS) as e:
                    up(i0 + e, e)
                    down(i0 + e - 1, e - 1)
                down(i0 + EXPERTS - 1, EXPERTS - 1)

            one_pass(0)
            over = most(sp)
            with sp.If(over > threshold):
                with sp.Fori(1, ROUNDS) as r:
                    i0 = sp.snap(r * EXPERTS)
                    up(i0, 0)
                    one_pass(i0)
            for t in range(NT):
                sp.wait_ge(*((f_okp, t + 1) if t < 2 else (f_ok, t - 1)))
                sp.dma_start(out_v[:, t], result[:, t]).then_inc(stored, 16)
            sp.wait_ge(stored, 16 * NT)

        @block.gpsimd
        def _(gp):
            gp.iota(small["key"], pattern=[[-1, EXPERTS]], base=EXPERTS, channel_multiplier=0,
                    allow_small_or_imprecise_dtypes=True).then_inc(consts, 1)
            gp.iota(small["gkey"], pattern=[[-1, GROUPS]], base=GROUPS, channel_multiplier=0,
                    allow_small_or_imprecise_dtypes=True).then_inc(consts, 1)
            gp.memset(ident, 0.0).then_inc(pool_step, 1)
            gp.memset(ones, 1.0).then_inc(consts, 1)
            gp.memset(small["half"], 1.0).then_inc(pool_step, 1)
            gp.memset(w_lr, 0.0).then_inc(lr_zero, 1)
            gp.memset(lrT, 1.0).then_inc(consts, 1)
            gp.wait_ge(pool_step, 2)
            gp.wait_ge(consts, 4)
            gp.affine_select(out=ident, in_=ident, compare_op=ALU.not_equal, fill=1.0, base=0,
                             pattern=[[-1, P]], channel_multiplier=1).then_inc(consts, 1)
            gp.memset(ones_b, 1.0).then_inc(consts, 1)
            gp.wait_ge(consts, 6)
            gp.affine_select(out=before, in_=ones, compare_op=ALU.is_gt, fill=0.0, base=0,
                             pattern=[[1, P]], channel_multiplier=-1).then_inc(consts, 1)
            gp.affine_select(out=later, in_=ones, compare_op=ALU.is_gt, fill=0.0, base=0,
                             pattern=[[-1, P]], channel_multiplier=1).then_inc(pool_step, 1)
            gp.wait_ge(pool_step, 3)
            gp.affine_select(out=later[:, 0:CHUNK], in_=later[:, 0:CHUNK], compare_op=ALU.is_gt, fill=0.0, base=CHUNK,
                             pattern=[[0, CHUNK]], channel_multiplier=-1).then_inc(consts, 1)
            gp.affine_select(out=small["half"][:, 0:1], in_=small["half"][:, 0:1], compare_op=ALU.is_gt, fill=0.0,
                             base=CHUNK, pattern=[[0, 1]], channel_multiplier=-1).then_inc(consts, 1)
            gp.affine_select(out=small["half"][:, 1:2], in_=small["half"][:, 1:2], compare_op=ALU.is_ge, fill=0.0,
                             base=-CHUNK, pattern=[[0, 1]], channel_multiplier=1).then_inc(consts, 1)
            gp.wait_ge(cols_ok, 1)
            gp.memset(zero, 0.0).then_inc(zero_ok, 1)
            gp.wait_ge(zero_ok, 1)

            def low(u):
                gp.wait_ge(wi_hi_ok, u + 1)
                gp.tensor_tensor(wi_lo[:, u % 2], w_i[:, u % 2], wi_hi[:, u % 2].bitcast(f32), ALU.subtract).then_inc(wi_lo_ok, 1)
                gp.wait_ge(wi_lo_ok, u + 1)

            def bias(r):
                gp.wait_ge(ada_summed, 5 + r)
                gp.wait_ge(bias_in, 32)
                row, s = slice(32 * (r % 4), 32 * (r % 4) + 1), r % SUMS
                gp.tensor_tensor(ada_sum[row, s], ada_sum[row, s], ada_bias[row, r // 4], ALU.add).then_inc(biased, 1)
                gp.wait_ge(biased, r + 1)

            low(0)
            gp.wait_ge(lrw_ok, 1)
            gp.tensor_tensor(lr_lo, w_lr, lr_hi.bitcast(f32), ALU.subtract).then_inc(lrw_ok, 1)
            gp.wait_ge(lrw_ok, 2)
            low(1)
            def added(tap):
                gp.wait_ge(*((first_tap, 1) if tap == 1 else (term_added, tap - 1)))
                gp.wait_ge(term_ok, tap)
                gp.tensor_tensor(conv[:, NC - 1], conv[:, NC - 1], term[:, tap % 2], ALU.add).then_inc(term_added, 1)

            for u in range(2, NU):
                low(u)
                for r in {2: (0, 1), 3: (2, 3), 4: (4,), 5: (5, 6), 6: (7,)}.get(u, ()):
                    bias(r)
                if u == 7:
                    gp.wait_ge(gate_parts, 1)
                    gp.tensor_tensor(soft_l, soft_l, soft_m, ALU.add).then_inc(soft_ok, 1)
                    gp.wait_ge(soft_ok, 1)
                if u == NU - 1:
                    gp.wait_ge(ada_mm, 12)
                    gp.memset(k_dec[0:CHUNK, :, 1, :], 0.0).then_inc(pool_step, 1)
                    gp.wait_ge(pool_step, 4)
                    gp.memset(k_dec[CHUNK:P, :, 0, :], 0.0).then_inc(pool_step, 1)
                    gp.wait_ge(pool_step, 5)
                    gp.wait_ge(decay_ok, 1)
                    gp.tensor_tensor(k_dec[0:CHUNK, :, 0, :], kv[0:CHUNK, :, 0:QK], soft_m[0:CHUNK], ALU.mult).then_inc(kdec_ok, 1)
                    gp.wait_ge(kdec_ok, 1)
                    gp.tensor_tensor(k_dec[CHUNK:P, :, 1, :], kv[CHUNK:P, :, 0:QK], soft_m[CHUNK:P], ALU.mult).then_inc(kdec_ok, 1)
                    gp.wait_ge(kdec_ok, 2)
                for tap in TERMS.get(u - 2, ()):
                    added(tap)
            for tap in TERMS[NU - 2]:
                added(tap)
            for n, k in enumerate(GLA_FIRST):
                gp.wait_ge(wo_hi_ok, n + 1)
                gp.tensor_tensor(wo_lo[:, k], w_o[:, k], wo_hi[:, k].bitcast(f32), ALU.subtract).then_inc(wo_lo_ok, 1)
                gp.wait_ge(wo_lo_ok, n + 1)
            over = most(gp)
            with gp.If(over > threshold):
                gp.memset(zero_more, 0.0).then_inc(zero_ok, 1)
                gp.wait_ge(zero_ok, 2)
                with gp.Fori(EXPERTS, ROUNDS * EXPERTS) as b:
                    gp.dma_start(table[b].rearrange("p (q d) -> p q d", q=4),
                                 zero_more.unsqueeze(1).broadcast_to((P, 4, 256))).then_inc(cleared_more, 16)
                gp.wait_ge(cleared_more, 16 * (ROUNDS - 1) * EXPERTS)
            for t in range(NT):
                for k in range(2):
                    gp.indirect_dma_start(
                        out=table_rows, out_offset=bass.IndirectOffsetOnAxis(ap=pos[:, 4 * k + t:4 * k + t + 1], axis=0),
                        in_=h2[:, t], in_offset=None).then_inc(scattered, 16)
            gp.wait_ge(scattered, 32 * NT)

            def load(i, blk):
                reach(gp, xeT_up, i)
                gp.dma_start(xe, table[blk]).then_inc(xe_in, 16)

            def split_x(i):
                gp.wait_ge(xeT_ok, i + 1)
                reach(gp, fed13, KD * i)
                gp.tensor_tensor(x_hi, xeT, ones.unsqueeze(1).broadcast_to((P, KD, P)), ALU.mult).then_inc(xhl_ok, 1)
                gp.wait_ge(xhl_ok, 2 * i + 1)
                gp.tensor_tensor(x_lo, xeT, x_hi.bitcast(f32), ALU.subtract).then_inc(xhl_ok, 1)

            def store(i, blk):
                gp.wait_ge(ye_a, i + 1)
                gp.wait_ge(ye_v, i + 1)
                gp.dma_start(table_y[blk], y_e).then_inc(ye_out, 16)

            def one_pass(i0):
                load(i0, i0)
                split_x(i0)
                load(i0 + 1, i0 + 1)
                split_x(i0 + 1)
                with gp.Fori(1, EXPERTS - 1) as e:
                    i = gp.snap(i0 + e)
                    load(i + 1, i + 1)
                    split_x(i + 1)
                    store(i - 1, i - 1)
                for e in (EXPERTS - 2, EXPERTS - 1):
                    store(i0 + e, i0 + e)

            def gather(rounds):
                rows = table_y_rows[0:rounds * EXPERTS * BLOCK]
                for t in range(NT):
                    for k in range(2):
                        gp.indirect_dma_start(
                            out=back[:, t, k], out_offset=None, in_=rows,
                            in_offset=bass.IndirectOffsetOnAxis(ap=pos[:, 4 * k + t:4 * k + t + 1], axis=0)).then_inc(back_in[t], 16)

            one_pass(0)
            over = most(gp)
            with gp.If(over > threshold):
                with gp.Fori(1, ROUNDS) as r:
                    one_pass(gp.snap(r * EXPERTS))
                gp.wait_ge(ye_out, 16 * ROUNDS * EXPERTS)
                gather(ROUNDS)
            with gp.Else():
                gp.wait_ge(ye_out, 16 * EXPERTS)
                gather(1)
            for t in range(2):
                gp.wait_ge(f_r, 2 * t + 2)
                gp.tensor_tensor(result[:, t], result[:, t], x2[:, t], ALU.add).then_inc(f_okp, 1)
                gp.wait_ge(f_okp, t + 1)
            gp.wait_ge(back_in[NT - 1], 32)

        @block.scalar
        def _(act):
            link = chain(act, act_step)
            row = 56
            for src, n in ((c, 8), (b_dw, 4), (conv_ln_g, 4), (conv_ln_b, 4), (gla_norm_g, 1)):
                act.dma_start(par_rows[row:row + n, :], src.rearrange("o (r q) -> (o r) q", q=P)).then_inc(par_in, 16)
                row += n
            act.dma_start(dw_rows, w_dw[0]).then_inc(par_in, 16)
            b_rows = b_ada[0, 2 * D:].rearrange("(s r n) -> s r n", s=2, r=4)
            for i in range(2):
                act.dma_start(ada_bias[0:P:32, i], b_rows[i]).then_inc(bias_in, 16)
            act.dma_start(w_up[0:RANK, :], w_gate_up[0]).then_inc(rows_in, 16)
            act.dma_start(w_up[RANK:RANK + 1, :], b_gate).then_inc(rows_in, 16)
            act.dma_start(small["brow"], b_router.rearrange("(o n) -> o n", o=1).broadcast_to((P, EXPERTS))).then_inc(rows_in, 16)
            act.dma_start(gate1, g_post_mix.broadcast_to((P, D))).then_inc(rows_in, 16)
            act.dma_start(gate2, g_post_ffn.broadcast_to((P, D))).then_inc(rows_in, 16)
            act.dma_start(scale2, g_pre_ffn.broadcast_to((P, D))).then_inc(rows_in, 16)
            act.wait_ge(cols_ok, 1)
            link(nc.scalar.activation(small["csil"], small["par"][:, 56:64], ACT.Silu))
            for t in range(NT):
                act.wait_ge(x_in[t], 16)
                link(nc.scalar.activation(xhat[:, t], x_rows[:, t], ACT.Square, accum_out=small["xss"][:, t:t + 1]))
            act.wait_ge(eps_ok, 1)
            link(nc.scalar.activation(small["xstd"], small["xss"], ACT.Sqrt, scale=1.0 / D, bias=small["eps"]))
            act.wait_ge(xr_ok, 1)
            for t in range(NT):
                nc.scalar.activation(xhat[:, t], x_rows[:, t], ACT.Copy, scale=small["xr"][:, t:t + 1]).then_inc(xhat_ok, 1)
            def high(u):
                act.wait_ge(wi_in[u % 2], 32 * (u // 2 + 1))
                if u >= 2:
                    act.wait_ge(unit_mm, u - 1)
                nc.scalar.activation(wi_hi[:, u % 2], w_i[:, u % 2], ACT.Copy).then_inc(wi_hi_ok, 1)

            high(0)
            act.wait_ge(lr_in, 16)
            act.wait_ge(xhat_ok, NT)
            nc.scalar.activation(lr_hi, w_lr, ACT.Copy).then_inc(lrw_ok, 1)
            for k in range(KD):
                act.wait_ge(tmp_ok, k + 1)
                nc.scalar.activation(hT_hi[:, k], h_tmp[:, k % 2], ACT.Copy).then_inc(hT_a, 1)
            high(1)
            def term_of(tap):
                reach(act, term_added, tap - 2)
                nc.scalar.activation(term[:, tap % 2], uT[:, NC - 1, tap:tap + T], ACT.Copy,
                                     scale=dwT[:, NC - 1, tap:tap + 1]).then_inc(term_ok, 1)

            for u, (what, i, _) in enumerate(UNITS):
                b = bank(2 * PAIR[what, i], 2)
                act.wait_ge(unit_mm, u + 1)
                if u + 2 < NU:
                    high(u + 2)
                if what == "conv":
                    reach(act, u_ok, i - 1)
                    nc.scalar.activation(sig[:, i % 2], b[:, BANK:], ACT.Sigmoid).then_inc(sig_ok, 1)
                    if i == NC - 1:
                        act.wait_ge(lr_mm, 1)
                        act.wait_ge(consts, 10)
                        nc.scalar.activation(lrT[0:RANK, :], bank(2 * PAIR["lr"])[0:RANK, :], ACT.Copy).then_inc(unit_ok, 1)
                elif what == "kv":
                    nc.scalar.activation(kv[:, :, i * QK:(i + 1) * QK], b.rearrange("p (t n) -> p t n", t=NT), ACT.Copy).then_inc(unit_ok, 1)
                elif what == "q":
                    nc.scalar.activation(qT.rearrange("p m n -> p (m n)"), b, ACT.Copy, scale=DK ** -0.5).then_inc(unit_ok, 1)
                else:
                    nc.scalar.activation(gT[:, 2 * i:2 * i + 2].rearrange("p m n -> p (m n)"), b, ACT.Silu).then_inc(unit_ok, 1)
                if (what, i) == ("kv", 1):
                    act.wait_ge(z_mm, 1)
                    z = bank(2 * PAIR["z"], 2).rearrange("p (t n) -> p t n", t=NT)
                    link(nc.scalar.activation(soft_l, z, ACT.Abs))
                    link(nc.scalar.activation(soft_l, soft_l, ACT.Exp, scale=-1.0))
                    link(nc.scalar.activation(soft_l, soft_l, ACT.Ln, bias=1.0))
                    nc.scalar.activation(soft_m, z, ACT.Relu, scale=-1.0).then_inc(gate_parts, 1)
                if (what, i) == ("kv", 2):
                    act.wait_ge(later_mm, 1)
                    link(nc.scalar.activation(soft_m, bank(2 * PAIR["later"], 2).rearrange("p (t n) -> p t n", t=NT), ACT.Exp, scale=-1.0 / TAU))
                    nc.scalar.activation(small["decay"], bank(6)[:, 0:16], ACT.Exp, scale=-1.0 / TAU).then_inc(decay_ok, 1)
                    act.dma_start(w_r, w_router.rearrange("(k p) e -> p k e", p=P)).then_inc(w_r_in, 16)
                if u == NC:
                    act.wait_ge(u_ok, NC)
                    nc.scalar.activation(conv[:, NC - 1], uT[:, NC - 1, 0:T], ACT.Identity, scale=dwT[:, NC - 1, 0:1],
                                         bias=small["par"][:, 64 + NC - 1:64 + NC]).then_inc(first_tap, 1)
                for tap in TERMS.get(u, ()):
                    term_of(tap)
            act.wait_ge(w_out_in, 16)
            for k in GLA_FIRST:
                nc.scalar.activation(wo_hi[:, k], w_o[:, k], ACT.Copy).then_inc(wo_hi_ok, 1)
            for h in range(HEADS):
                act.wait_ge(o_mm, h + 1)
                reach(act, osum_mm, h - 1)
                nc.scalar.activation(o_sq[:, h % 2], bank(O_BANK[h]), ACT.Square).then_inc(osq_ok, 1)
            act.wait_ge(osum_mm, HEADS)
            nc.scalar.activation(small["ostd"], bank(6)[:, 0:16], ACT.Sqrt, scale=1.0 / DV, bias=small["eps"]).then_inc(ostd_ok, 1)
            for h in range(HEADS):
                act.wait_ge(ygla_ok, h + 1)
                nc.scalar.activation(g_hi[:, h], gT[:, h], ACT.Copy).then_inc(yhi_ok, 1)
            for j in range(NC):
                act.wait_ge(cent_ok, j + 1)
                reach(act, var_mm, j - 1)
                nc.scalar.activation(o_sq[:, j % 2], conv[:, j], ACT.Square).then_inc(csq_ok, 1)
            act.wait_ge(var_mm, NC)
            nc.scalar.activation(o_std[:, 0], bank(3), ACT.Sqrt, scale=1.0 / CONV, bias=small["eps"]).then_inc(cstd_ok, 1)
            for j in range(NC):
                act.wait_ge(cnorm_ok, j + 1)
                link(nc.scalar.activation(conv[:, j], conv[:, j], ACT.Silu, scale=small["par"][:, 68 + j:69 + j],
                                          bias=small["par"][:, 72 + j:73 + j]))
                nc.scalar.activation(conv_hi[:, j], conv[:, j], ACT.Copy).then_inc(yhi_ok, 1)
            def h2T_out(t):
                act.wait_ge(h2T_up, t + 1)
                nc.scalar.activation(h2T[:, TILE[t], 0:4].rearrange("p k n -> p (k n)"), bank(2 * t), ACT.Copy).then_inc(h2T_a, 1)

            for t in range(NT):
                act.wait_ge(y_mm, t + 1)
                nc.scalar.activation(junk, bank(2 * t, 2), ACT.Square, accum_out=small["yss"][:, t:t + 1]).then_inc(yss_ok, 1)
                act.wait_ge(yss_ok, t + 1)
                nc.scalar.activation(small["ystd"][:, t:t + 1], small["yss"][:, t:t + 1], ACT.Sqrt, scale=1.0 / D,
                                     bias=small["eps"]).then_inc(ystd_ok, 1)
                act.wait_ge(x2_ok, 2 * t + 2)
                nc.scalar.activation(junk, x2[:, t], ACT.Square, accum_out=small["x2ss"][:, t:t + 1]).then_inc(x2ss_ok, 1)
                act.wait_ge(x2ss_ok, t + 1)
                nc.scalar.activation(small["x2std"][:, t:t + 1], small["x2ss"][:, t:t + 1], ACT.Sqrt, scale=1.0 / D,
                                     bias=small["eps"]).then_inc(x2std_ok, 1)
                if t >= 1:
                    h2T_out(t - 1)
            h2T_out(NT - 1)
            act.wait_ge(exp_in, 1)
            nc.scalar.activation(R["p"], R["sh"], ACT.Exp).then_inc(exp_ok, 1)

            def split13(i, p):
                g = p // 2
                if p % 2 == 0:
                    act.wait_ge(raw13_in[g], 32 * (i + 1))
                reach(act, fed13, KD * i + p - 3)
                nc.scalar.activation(hi13[:, p % 4], raw13[:, p], ACT.Copy).then_inc(hi13_ok, 1)

            def split2(i, p):
                g = p // 2
                if p % 2 == 0:
                    act.wait_ge(raw2_in[g], 32 * (i + 1))
                reach(act, fed2, 6 * i + p - 2)
                n = P if p < FULL else LAST
                nc.scalar.activation(hi2[0:n, p % 3], raw2[0:n, p], ACT.Copy).then_inc(hi2_ok, 1)

            def silu(i):
                act.wait_ge(fed13, KD * (i + 1))
                reach(act, he_ok, i)
                nc.scalar.activation(s_act.rearrange("p (b n) -> p b n", b=2), H1, ACT.Silu).then_inc(silu_ok, 1)

            def x_out(i):
                act.wait_ge(xeT_up, i + 1)
                reach(act, xhl_ok, 2 * i)
                nc.scalar.activation(xeT.rearrange("p k n -> p (k n)"), bank(TB, 2), ACT.Copy).then_inc(xeT_ok, 1)

            def he_high(i):
                act.wait_ge(heT_up, i + 1)
                reach(act, fed2, 6 * i)
                nc.scalar.activation(he_hi.rearrange("p k n -> p (k n)"), bank(TB, 2)[:, 0:6 * P], ACT.Copy).then_inc(hehi_ok, 1)

            def y_out(i):
                act.wait_ge(fed2, 6 * (i + 1))
                reach(act, ye_out, 16 * i)
                nc.scalar.activation(y_e[:, 0:BANK], bank(YB), ACT.Copy).then_inc(ye_a, 1)

            def one_pass(i0):
                for p in range(4):
                    split13(i0, p)
                x_out(i0)
                for p in range(4, KD):
                    split13(i0, p)
                silu(i0)
                x_out(i0 + 1)
                for p in range(4):
                    split13(i0 + 1, p)
                he_high(i0)

                def body(i):
                    for p in range(4, KD):
                        split13(i, p)
                    for p in range(3):
                        split2(i - 1, p)
                    silu(i)
                    x_out(i + 1)
                    for p in range(3, 6):
                        split2(i - 1, p)
                    for p in range(4):
                        split13(i + 1, p)
                    y_out(i - 1)
                    he_high(i)

                body(i0 + 1)
                with act.Fori(2, EXPERTS - 1) as e:
                    body(act.snap(i0 + e))
                i = i0 + EXPERTS - 1
                for p in range(4, KD):
                    split13(i, p)
                for p in range(3):
                    split2(i - 1, p)
                silu(i)
                for p in range(3, 6):
                    split2(i - 1, p)
                for p in range(3):
                    split2(i, p)
                y_out(i - 1)
                he_high(i)
                for p in range(3, 6):
                    split2(i, p)
                y_out(i)

            act.wait_ge(y_mm, NT)
            act.wait_ge(x2_ok, 2 * NT)
            one_pass(0)
            over = most(act)
            with act.If(over > threshold):
                with act.Fori(1, ROUNDS) as r:
                    one_pass(act.snap(r * EXPERTS))
            def root(t):
                act.wait_ge(f_mix, t + 1)
                nc.scalar.activation(result[:, t], mixed[:, t], ACT.Square, accum_out=small["fss"][:, t:t + 1]).then_inc(f_ss, 1)
                act.wait_ge(f_ss, t + 1)
                nc.scalar.activation(small["fstd"][:, t:t + 1], small["fss"][:, t:t + 1], ACT.Sqrt, scale=1.0 / D,
                                     bias=small["eps"]).then_inc(f_std, 1)

            for t in range(NT):
                act.wait_ge(back_in[t], 32)
                nc.scalar.activation(mixed[:, t], back[:, t, 0], ACT.Copy, scale=small["wts"][:, t:t + 1]).then_inc(f_m1, 1)
                if t >= 1:
                    root(t - 1)
            root(NT - 1)

        @block.vector
        def _(dve):
            v = nc.vector
            link = chain(dve, dve_step)
            v.memset(small["eps"], EPS).then_inc(eps_ok, 1)
            dve.wait_ge(cols_up, 1)
            link(v.tensor_copy(dwT, bank(7)[:, 128:256].rearrange("p (j n) -> p j n", j=NC)[:, :, 0:WIDTH]))
            v.tensor_copy(small["par"][:, 0:77], bank(7)[:, 0:77]).then_inc(cols_ok, 1)
            dve.wait_ge(act_step, 1)

            def ada(b):
                dve.wait_ge(ada_in[b % 2], 16 * (b // 2 + 1))
                reach(dve, ada_mm, b - 3)
                s = ada_sum[:, b % SUMS]
                link(v.tensor_scalar(s, ada_w[:, b % 2, 0], small["csil"][:, 0:1], None, ALU.mult))
                for k in range(1, KD):
                    ins = v.scalar_tensor_tensor(out=s, in0=ada_w[:, b % 2, k], scalar=small["csil"][:, k:k + 1],
                                                 in1=s, op0=ALU.mult, op1=ALU.add)
                    if k < KD - 1:
                        link(ins)
                ins.then_inc(ada_summed, 1)

            def ada_row(r):
                dve.wait_ge(ada_mm, 5 + r)
                what, h = r // 2, slice(r % 2 * BANK, (r % 2 + 1) * BANK)
                b = bank(6 + r % 2)
                if r == 0:
                    dve.wait_ge(rows_in, 96)
                if what == 0:
                    v.tensor_tensor(gate1[:, h], b, gate1[:, h], ALU.mult).then_inc(ada_taken, 1)
                elif what == 1:
                    v.tensor_copy(shift2[:, h], b).then_inc(ada_taken, 1)
                elif what == 2:
                    v.scalar_tensor_tensor(out=scale2[:, h], in0=b, scalar=1.0, in1=scale2[:, h], op0=ALU.add,
                                           op1=ALU.mult).then_inc(ada_taken, 1)
                else:
                    v.tensor_tensor(gate2[:, h], b, gate2[:, h], ALU.mult).then_inc(ada_taken, 1)

            dve.wait_ge(act_step, 1 + NT + 1)
            v.reciprocal(small["xr"], small["xstd"]).then_inc(xr_ok, 1)
            for b in range(4):
                ada(b)
            dve.wait_ge(ada_mm, 4)
            link(v.tensor_tensor(small["modc"], bank(7)[:, 0:16], small["par"][:, 0:16], ALU.add))
            link(v.tensor_copy(small["B1"], small["modc"][:, 0:8]))
            v.scalar_tensor_tensor(out=small["A1"], in0=small["modc"][:, 8:16], scalar=1.0, in1=small["par"][:, 48:56],
                                   op0=ALU.add, op1=ALU.mult).then_inc(mod1_ok, 1)
            dve.wait_ge(mod1_ok, 1)

            def h_low(k):
                dve.wait_ge(hT_a, k + 1)
                v.tensor_tensor(hT_lo[:, k], h_tmp[:, k % 2], hT_hi[:, k].bitcast(f32), ALU.subtract).then_inc(hT_v, 1)

            for k in range(KD):
                dve.wait_ge(xT_up, k + 1)
                reach(dve, hT_v, k - 1)
                v.tensor_scalar(h_tmp[:, k % 2], bank(k), small["A1"][:, k:k + 1], small["B1"][:, k:k + 1], ALU.mult,
                                ALU.add).then_inc(tmp_ok, 1)
                if k >= 1:
                    h_low(k - 1)
            h_low(KD - 1)
            link(v.memset(uT[:, :, 0:WIDTH - 1], 0.0))

            def gated(j):
                dve.wait_ge(sig_ok, j + 1)
                v.tensor_tensor(uT[:, j, WIDTH - 1:], bank(2 * PAIR["conv", j]), sig[:, j % 2], ALU.mult).then_inc(u_ok, 1)

            def taps(j, first, last):
                if first == 0:
                    dve.wait_ge(u_ok, j + 1)
                    v.tensor_scalar(conv[:, j], uT[:, j, 0:T], dwT[:, j, 0:1], small["par"][:, 64 + j:65 + j], ALU.mult,
                                    ALU.add).then_inc(tap_ok, 1)
                    first = 1
                with dve.Fori(first, last) as tap:
                    dve.wait_ge(tap_ok, tap + (WIDTH * j if j < NC - 1 else WIDTH * j - SHARED))
                    v.scalar_tensor_tensor(out=conv[:, j], in0=uT[:, j, bass.ds(tap, T)], scalar=dwT[:, j, bass.ds(tap, 1)],
                                           in1=conv[:, j], op0=ALU.mult, op1=ALU.add).then_inc(tap_ok, 1)

            ada(4)
            ada(5)
            gated(0)
            ada(6)
            gated(1)
            ada(7)
            ada_row(0)
            ada(8)
            ada_row(1)
            ada_row(2)
            gated(2)
            ada(9)
            ada(10)
            ada_row(3)
            ada_row(4)
            gated(3)
            ada(11)
            ada_row(5)
            for j in range(NC - 1):
                taps(j, 0, WIDTH)
                if j == 0:
                    ada_row(6)
                    ada_row(7)
            dve.wait_ge(decay_ok, 1)
            n_state = 0
            for n in range(NCH):
                dve.wait_ge(upd_mm, n + 1)
                u = bank(6 + n % 2)
                for p in range(2):
                    for h in range(2):
                        rows = slice(h * DK, (h + 1) * DK)
                        src = u[rows, p * QK + h * DV:p * QK + (h + 1) * DV]
                        if n == 0:
                            v.tensor_copy(state[rows, n, p], src).then_inc(state_ok, 1)
                        else:
                            dve.wait_ge(state_ok, 4 * (n - 1) + 2 * p + h + 1)
                            v.scalar_tensor_tensor(out=state[rows, n, p], in0=state[rows, n - 1, p],
                                                   scalar=small["decay"][rows, p * NCH + n:p * NCH + n + 1], in1=src,
                                                   op0=ALU.mult, op1=ALU.add).then_inc(state_ok, 1)

            def y_low(n):
                k = GLA_FIRST[n]
                dve.wait_ge(yhi_ok, n + 1)
                src, hi, lo = (conv, conv_hi, conv_lo) if k < NC else (gT, g_hi, g_lo)
                v.tensor_tensor(lo[:, k % NC], src[:, k % NC], hi[:, k % NC].bitcast(f32), ALU.subtract).then_inc(ylo_ok, 1)

            dve.wait_ge(term_added, SHARED - 1)
            taps(NC - 1, SHARED, WIDTH)
            dve.wait_ge(unit_ok, 7)
            dve.wait_ge(ostd_ok, 1)
            link(v.reciprocal(small["or"], small["ostd"]))

            def diagonal(h):
                v.tensor_tensor(o_std[:, h % 2].rearrange("p (t n) -> p t n", t=NT), ident.unsqueeze(1).broadcast_to((P, NT, P)),
                                small["or"][:, NT * h:NT * (h + 1)].unsqueeze(2).broadcast_to((P, NT, P)), ALU.mult).then_inc(diag_ok, 1)

            diagonal(0)
            diagonal(1)
            for h in range(HEADS):
                dve.wait_ge(spread_mm, h + 1)
                link(v.tensor_tensor(gT[:, h], bank(6 + h % 2), gT[:, h], ALU.mult))
                if h < HEADS - 2:
                    diagonal(h + 2)
                v.scalar_tensor_tensor(out=gT[:, h], in0=bank(O_BANK[h]), scalar=small["par"][:, 76:77], in1=gT[:, h],
                                       op0=ALU.mult, op1=ALU.mult).then_inc(ygla_ok, 1)
            for n in range(HEADS):
                y_low(n)
            dve.wait_ge(mean_mm, NC)
            for j in range(NC):
                v.scalar_tensor_tensor(out=conv[:, j], in0=bank(2), scalar=-1.0 / CONV, in1=conv[:, j], op0=ALU.mult,
                                       op1=ALU.add).then_inc(cent_ok, 1)
            dve.wait_ge(cstd_ok, 1)
            link(v.reciprocal(o_std[:, 0], o_std[:, 0]))
            dve.wait_ge(cent_ok, NC)
            for j in range(NC):
                v.tensor_tensor(conv[:, j], conv[:, j], o_std[:, 0], ALU.mult).then_inc(cnorm_ok, 1)
            for n in range(HEADS, KD):
                y_low(n)
            def h2T_out(t):
                dve.wait_ge(h2T_up, t + 1)
                v.tensor_copy(h2T[:, TILE[t], 4:KD].rearrange("p k n -> p (k n)"), bank(2 * t + 1)).then_inc(h2T_v, 1)

            for t in range(NT):
                dve.wait_ge(ystd_ok, t + 1)
                link(v.reciprocal(small["yr"][:, t:t + 1], small["ystd"][:, t:t + 1]))
                v.scalar_tensor_tensor(out=y_tmp, in0=bank(2 * t, 2), scalar=small["yr"][:, t:t + 1], in1=gate1,
                                       op0=ALU.mult, op1=ALU.mult).then_inc(x2_ok, 1)
                dve.wait_ge(x2_ok, 2 * t + 1)
                dve.wait_ge(x_again[t // 2], 16)
                v.tensor_tensor(x2[:, t], x2[:, t], y_tmp, ALU.add).then_inc(x2_ok, 1)
                if t >= 1:
                    h2T_out(t - 1)
                dve.wait_ge(x2std_ok, t + 1)
                link(v.reciprocal(small["x2r"][:, t:t + 1], small["x2std"][:, t:t + 1]))
                link(v.scalar_tensor_tensor(out=h2[:, t], in0=x2[:, t], scalar=small["x2r"][:, t:t + 1], in1=scale2,
                                            op0=ALU.mult, op1=ALU.mult))
                v.tensor_tensor(h2[:, t], h2[:, t], shift2, ALU.add).then_inc(h2_ok, 1)
            h2T_out(NT - 1)

            dve.wait_ge(logit_mm, NT)
            E4 = (P, NT, EXPERTS)
            lg = psum.rearrange("p (t e) -> p t e", t=NT)[:, :, 0:EXPERTS]
            wide = lambda a: a.unsqueeze(2).broadcast_to(E4)
            link(v.tensor_reduce(R["a"], lg, AX.X, ALU.max))
            v.tensor_tensor(R["sh"], lg, wide(R["a"]), ALU.subtract).then_inc(exp_in, 1)
            dve.wait_ge(exp_ok, 1)
            link(v.tensor_reduce(R["a"], R["p"], AX.X, ALU.add))
            link(v.reciprocal(R["a"], R["a"]))
            link(v.tensor_tensor(R["p"], R["p"], wide(R["a"]), ALU.mult))
            link(v.tensor_tensor(R["sel"], R["p"], small["brow"].unsqueeze(1).broadcast_to(E4), ALU.add))
            s4 = R["sel"].rearrange("p t (g i) -> p (t g) i", i=4)
            q = [R["q"][:, i] for i in range(4)]
            link(v.tensor_tensor(q[0], s4[:, :, 0], s4[:, :, 1], ALU.max))
            link(v.tensor_tensor(q[1], s4[:, :, 0], s4[:, :, 1], ALU.min))
            link(v.tensor_tensor(q[2], s4[:, :, 2], s4[:, :, 3], ALU.max))
            link(v.tensor_tensor(q[3], s4[:, :, 2], s4[:, :, 3], ALU.min))
            link(v.tensor_tensor(q[1], q[1], q[3], ALU.max))
            link(v.tensor_tensor(q[3], q[0], q[2], ALU.min))
            link(v.tensor_tensor(q[0], q[0], q[2], ALU.max))
            link(v.tensor_tensor(q[1], q[1], q[3], ALU.max))
            link(v.tensor_tensor(q[0], q[0], q[1], ALU.add))
            gs = q[0].rearrange("p (t g) -> p t g", g=GROUPS)
            gm = q[1].rearrange("p (t g) -> p t g", g=GROUPS)
            G4 = (P, NT, GROUPS)
            link(v.tensor_reduce(R["a"], gs, AX.X, ALU.max))
            link(v.tensor_tensor(gm, gs, R["a"].unsqueeze(2).broadcast_to(G4), ALU.is_ge))
            link(v.tensor_tensor(gm, gm, small["gkey"].unsqueeze(1).broadcast_to(G4), ALU.mult))
            link(v.tensor_reduce(R["a"], gm, AX.X, ALU.max))
            link(v.tensor_tensor(gm, gm, R["a"].unsqueeze(2).broadcast_to(G4), ALU.is_equal))
            gw = q[1].unsqueeze(2).broadcast_to((P, NT * GROUPS, 4))
            link(v.tensor_tensor(s4, s4, gw, ALU.mult))
            link(v.tensor_scalar(q[1], q[1], -1.0, BIG, ALU.add, ALU.mult))
            link(v.tensor_tensor(s4, s4, gw, ALU.add))
            for k in range(2):
                hot = R["hot"][k]
                link(v.tensor_reduce(R["a"], R["sel"], AX.X, ALU.max))
                link(v.tensor_tensor(hot, R["sel"], wide(R["a"]), ALU.is_ge))
                link(v.tensor_tensor(hot, hot, small["key"].unsqueeze(1).broadcast_to(E4), ALU.mult))
                link(v.tensor_reduce(R["kmax"][:, k], hot, AX.X, ALU.max))
                link(v.tensor_tensor(hot, hot, wide(R["kmax"][:, k]), ALU.is_equal))
                if k == 0:
                    link(v.scalar_tensor_tensor(out=R["sel"], in0=hot, scalar=-3.0 * BIG, in1=R["sel"], op0=ALU.mult, op1=ALU.add))
            v.tensor_tensor(R["mask"], R["hot"][0], R["hot"][1], ALU.add).then_inc(mask_ok, 1)
            for k in range(2):
                link(v.tensor_tensor(R["sel"], R["p"], R["hot"][k], ALU.mult))
                link(v.tensor_reduce(R["w"][:, k], R["sel"], AX.X, ALU.add))
            link(v.tensor_tensor(R["a"], R["w"][:, 0], R["w"][:, 1], ALU.add))
            link(v.reciprocal(R["a"], R["a"]))
            wts = small["wts"].rearrange("p (k t) -> p k t", k=2)
            link(v.tensor_tensor(wts, R["w"], R["a"].unsqueeze(1).broadcast_to((P, 2, NT)), ALU.mult))
            dve.wait_ge(rank_mm, 1)
            rank = bank(1)[:, 0:NT * EXPERTS].rearrange("p (t e) -> p t e", t=NT)
            for k in range(2):
                link(v.tensor_tensor(R["sel"], rank, R["hot"][k], ALU.mult))
                link(v.tensor_reduce(R["w"][:, k], R["sel"], AX.X, ALU.add))
            link(v.tensor_scalar(R["sum"], R["w"], float(BLOCK), None, ALU.is_ge))
            for m in range(2, ROUNDS):
                link(v.scalar_tensor_tensor(out=R["sum"], in0=R["w"], scalar=float(m * BLOCK), in1=R["sum"], op0=ALU.is_ge, op1=ALU.add))
            link(v.scalar_tensor_tensor(out=R["w"], in0=R["sum"], scalar=float((EXPERTS - 1) * BLOCK), in1=R["w"], op0=ALU.mult, op1=ALU.add))
            link(v.scalar_tensor_tensor(out=R["w"], in0=R["kmax"], scalar=-float(BLOCK), in1=R["w"], op0=ALU.mult, op1=ALU.add))
            link(v.tensor_scalar(pos.rearrange("p (k t) -> p k t", k=2), R["w"], float(EXPERTS * BLOCK), None, ALU.add))
            link(v.tensor_reduce(R["a"][:, 0:1], bank(1)[:, NT * EXPERTS:(NT + 1) * EXPERTS], AX.X, ALU.max))
            v.tensor_copy(count, R["a"][:, 0:1]).then_inc(pos_ok, 1)

            def split13(i, p):
                dve.wait_ge(hi13_ok, KD * i + p + 1)
                v.tensor_tensor(lo13[:, p % 4], raw13[:, p], hi13[:, p % 4].bitcast(f32), ALU.subtract).then_inc(lo13_ok, 1)

            def split2(i, p):
                dve.wait_ge(hi2_ok, 6 * i + p + 1)
                n = P if p < FULL else LAST
                v.tensor_tensor(lo2[0:n, p % 3], raw2[0:n, p], hi2[0:n, p % 3].bitcast(f32), ALU.subtract).then_inc(lo2_ok, 1)

            def gate(i):
                dve.wait_ge(silu_ok, i + 1)
                reach(dve, heT_up, i)
                v.tensor_tensor(he[:, 0:F].rearrange("p (b n) -> p b n", b=2), s_act.rearrange("p (b n) -> p b n", b=2), H3,
                                ALU.mult).then_inc(he_ok, 1)

            def he_low(i):
                dve.wait_ge(hehi_ok, i + 1)
                v.tensor_tensor(he_lo.rearrange("p k n -> p (k n)"), bank(TB, 2)[:, 0:6 * P],
                                he_hi.rearrange("p k n -> p (k n)").bitcast(f32), ALU.subtract).then_inc(helo_ok, 1)

            def y_out(i):
                dve.wait_ge(fed2, 6 * (i + 1))
                reach(dve, ye_out, 16 * i)
                v.tensor_copy(y_e[:, BANK:], bank(YB + 1)).then_inc(ye_v, 1)

            def one_pass(i0):
                for p in range(KD):
                    split13(i0, p)
                gate(i0)
                for p in range(4):
                    split13(i0 + 1, p)
                he_low(i0)

                def body(i):
                    for p in range(4, KD):
                        split13(i, p)
                    for p in range(3):
                        split2(i - 1, p)
                    gate(i)
                    for p in range(3, 6):
                        split2(i - 1, p)
                    for p in range(4):
                        split13(i + 1, p)
                    y_out(i - 1)
                    he_low(i)

                body(i0 + 1)
                with dve.Fori(2, EXPERTS - 1) as e:
                    body(dve.snap(i0 + e))
                i = i0 + EXPERTS - 1
                for p in range(4, KD):
                    split13(i, p)
                for p in range(3):
                    split2(i - 1, p)
                gate(i)
                for p in range(3, 6):
                    split2(i - 1, p)
                for p in range(3):
                    split2(i, p)
                y_out(i - 1)
                he_low(i)
                for p in range(3, 6):
                    split2(i, p)
                y_out(i)

            link(v.memset(he[:, F:], 0.0))
            one_pass(0)
            over = most(dve)
            with dve.If(over > threshold):
                with dve.Fori(1, ROUNDS) as r:
                    one_pass(dve.snap(r * EXPERTS))
            def mix(t):
                dve.wait_ge(f_m1, t + 1)
                v.scalar_tensor_tensor(out=mixed[:, t], in0=back[:, t, 1], scalar=small["wts"][:, NT + t:NT + t + 1],
                                       in1=mixed[:, t], op0=ALU.mult, op1=ALU.add).then_inc(f_mix, 1)

            mix(0)
            for t in range(NT):
                if t + 1 < NT:
                    mix(t + 1)
                dve.wait_ge(f_std, t + 1)
                v.reciprocal(small["fr"][:, t:t + 1], small["fstd"][:, t:t + 1]).then_inc(f_r, 1)
                dve.wait_ge(f_r, 2 * t + 1)
                v.scalar_tensor_tensor(out=result[:, t], in0=mixed[:, t], scalar=small["fr"][:, t:t + 1], in1=gate2,
                                       op0=ALU.mult, op1=ALU.mult).then_inc(f_r, 1)
                if t >= 2:
                    dve.wait_ge(f_r, 2 * t + 2)
                    v.tensor_tensor(result[:, t], result[:, t], x2[:, t], ALU.add).then_inc(f_ok, 1)

        @block.tensor
        def _(pe):
            mm = nc.tensor.matmul
            pe.wait_ge(consts, 10)
            pe.wait_ge(par_in, 16 * 8)
            nc.tensor.transpose(bank(7)[:, 0:77], par_rows, ident[0:77, 0:77])
            for j in range(NC):
                last = nc.tensor.transpose(bank(7)[:, 128 + 32 * j:128 + 32 * j + WIDTH], dw_rows[:, j * P:(j + 1) * P],
                                           ident[0:WIDTH, 0:WIDTH])
            last.then_inc(cols_up, 1)

            def x_up(k):
                for t in range(NT):
                    if k == 0:
                        pe.wait_ge(xhat_ok, t + 1)
                    last = nc.tensor.transpose(bank(k)[:, t * P:(t + 1) * P], xhat[:, t, k * P:(k + 1) * P], ident)
                last.then_inc(xT_up, 1)

            pe.wait_ge(cols_ok, 1)
            for k in range(KD - 1):
                x_up(k)
            for b in range(4):
                pe.wait_ge(ada_summed, b + 1)
                for j in range(4):
                    last = mm(bank(7)[:, 4 * b + j:4 * b + j + 1], ada_sum[:, b % SUMS, j * P:(j + 1) * P], ones[:, 0:1],
                              start=True, stop=True)
                last.then_inc(ada_mm, 1)
            pe.wait_ge(mod1_ok, 1)
            x_up(KD - 1)

            def ada_row(r):
                pe.wait_ge(biased, r + 1)
                reach(pe, ada_taken, r - 1)
                mm(bank(6 + r % 2), ones, ada_sum[:, r % SUMS], start=True, stop=True).then_inc(ada_mm, 1)

            def product(u, rows=()):
                what, i, _ = UNITS[u]
                b, s = 2 * PAIR[what, i], u % 2
                rows = list(rows)
                pe.wait_ge(wi_hi_ok, u + 1)
                if what == "kv":
                    pe.wait_ge(wi_lo_ok, u + 1)
                    for t in range(NT):
                        for k in range(KD):
                            for n, (h, w) in enumerate(((hT_hi, wi_hi), (hT_hi, wi_lo), (hT_lo, wi_hi))):
                                last = mm(bank(b, 2)[:, t * QK:(t + 1) * QK], h[:, k, t * P:(t + 1) * P], w[:, s, k],
                                          start=k == 0 and n == 0, stop=k == KD - 1 and n == 2)
                        if t == 1 and rows:
                            ada_row(rows.pop(0))
                else:
                    for m in range(2):
                        cols = slice(m * P, (m + 1) * P)
                        for k in range(KD):
                            if u == 0:
                                pe.wait_ge(hT_v, k + 1)
                            mm(bank(b + m), wi_hi[:, s, k, cols], hT_hi[:, k], start=k == 0, stop=False)
                            mm(bank(b + m), wi_hi[:, s, k, cols], hT_lo[:, k], start=False, stop=False)
                        pe.wait_ge(wi_lo_ok, u + 1)
                        for k in range(KD):
                            last = mm(bank(b + m), wi_lo[:, s, k, cols], hT_hi[:, k], start=False, stop=k == KD - 1)
                        if m == 0 and rows:
                            ada_row(rows.pop(0))
                last.then_inc(unit_mm, 1)
                for r in rows:
                    ada_row(r)

            product(0)
            product(1)
            ada_row(0)
            product(2, (1, 2))
            pe.wait_ge(u_ok, 1)
            product(3, (3, 4))
            pe.wait_ge(u_ok, 2)
            pe.wait_ge(lrw_ok, 2)
            for k in range(KD):
                for n, (h, w) in enumerate(((hT_hi, lr_hi), (hT_hi, lr_lo), (hT_lo, lr_hi))):
                    last = mm(bank(2 * PAIR["lr"]), w[:, k], h[:, k], start=k == 0 and n == 0, stop=k == KD - 1 and n == 2)
            last.then_inc(lr_mm, 1)
            pe.wait_ge(u_ok, 3)
            product(4, (5, 6))
            pe.wait_ge(u_ok, 4)
            product(5, (7,))
            pe.wait_ge(rows_in, 96)
            pe.wait_ge(unit_ok, 2)
            for t in range(NT):
                last = mm(bank(2 * PAIR["z"], 2)[:, t * QK:(t + 1) * QK], lrT[:, t * P:(t + 1) * P], w_up, start=True, stop=True)
            last.then_inc(z_mm, 1)
            product(6)
            pe.wait_ge(soft_ok, 1)
            for t in range(NT):
                last = mm(bank(2 * PAIR["later"], 2)[:, t * QK:(t + 1) * QK], later, soft_l[:, t], start=True, stop=True)
            pe.wait_ge(ada_taken, 8)
            for t in range(NT):
                for p in range(2):
                    last = mm(bank(6)[:, p * NCH + 2 * t:p * NCH + 2 * t + 2], soft_l[:, t, p * P:(p + 1) * P], small["half"],
                              start=True, stop=True)
            last.then_inc(later_mm, 1)
            pe.wait_ge(unit_ok, 3)
            product(7)
            pe.wait_ge(unit_ok, 4)
            product(8)
            pe.wait_ge(unit_ok, 5)
            product(9)
            pe.wait_ge(decay_ok, 1)
            pe.wait_ge(kdec_ok, 2)
            for n in range(NCH):
                reach(pe, state_ok, 4 * (n - 1))
                for p in range(2):
                    last = mm(bank(6 + n % 2)[:, p * QK:(p + 1) * QK], k_dec[:, n // 2, n % 2, p * P:(p + 1) * P],
                              kv[:, n // 2, QK + p * QK:QK + (p + 1) * QK], start=True, stop=True)
                last.then_inc(upd_mm, 1)
            pe.wait_ge(unit_ok, 7)
            for h in range(HEADS):
                rows = slice(h % 2 * DK, (h % 2 + 1) * DK)
                for n in range(NCH):
                    pe.wait_ge(state_ok, 4 * n + 4)
                    last = mm(bank(O_BANK[h])[:, n * CHUNK:(n + 1) * CHUNK], state[rows, n, h // 2],
                              qT[rows, h // 2, n * CHUNK:(n + 1) * CHUNK], start=True, stop=True)
                last.then_inc(o_mm, 1)
            for h in range(HEADS):
                pe.wait_ge(osq_ok, h + 1)
                for t in range(NT):
                    last = mm(bank(6)[:, NT * h + t:NT * h + t + 1], o_sq[:, h % 2, t * P:(t + 1) * P], ones[:, 0:1],
                              start=True, stop=True)
                last.then_inc(osum_mm, 1)
            for h in range(HEADS):
                pe.wait_ge(diag_ok, h + 1)
                reach(pe, ygla_ok, h - 1)
                mm(bank(6 + h % 2), ones, o_std[:, h % 2], start=True, stop=True).then_inc(spread_mm, 1)

            def conv_mean(j):
                pe.wait_ge(tap_ok, (j + 1) * WIDTH if j < NC - 1 else NC * WIDTH - SHARED)
                mm(bank(2), ones, conv[:, j], start=j == 0, stop=j == NC - 1).then_inc(mean_mm, 1)

            def y_part(t, part):
                for n, k in enumerate(GLA_FIRST):
                    if n // NC != part:
                        continue
                    if t == 0:
                        pe.wait_ge(ylo_ok, n + 1)
                        pe.wait_ge(wo_lo_ok, n + 1)
                    hi, lo = (conv_hi, conv_lo) if k < NC else (g_hi, g_lo)
                    for m, (y, w) in enumerate(((hi, wo_hi), (hi, wo_lo), (lo, wo_hi))):
                        for h in range(2):
                            last = mm(bank(2 * t + h), y[:, k % NC, t * P:(t + 1) * P], w[:, k, h * BANK:(h + 1) * BANK],
                                      start=n == 0 and m == 0, stop=n == KD - 1 and m == 2)
                return last

            for j in range(NC - 1):
                conv_mean(j)
            pe.wait_ge(ygla_ok, HEADS)
            y_part(0, 0)
            y_part(2, 0)
            conv_mean(NC - 1)
            y_part(3, 0)
            for j in range(NC):
                pe.wait_ge(csq_ok, j + 1)
                mm(bank(3), ones, o_sq[:, j % 2], start=j == 0, stop=j == NC - 1).then_inc(var_mm, 1)
            y_part(0, 1).then_inc(y_mm, 1)
            pe.wait_ge(cstd_ok, 1)
            y_part(1, 0)
            for t in range(1, NT):
                y_part(t, 1).then_inc(y_mm, 1)
            def turn_h2(t):
                pe.wait_ge(h2_ok, t + 1)
                for k in range(KD):
                    last = nc.tensor.transpose(bank(2 * t, 2)[:, k * P:(k + 1) * P], h2[:, t, k * P:(k + 1) * P], ident)
                last.then_inc(h2T_up, 1)

            def logits(t):
                pe.wait_ge(h2T_a, t + 1)
                pe.wait_ge(h2T_v, t + 1)
                for k in range(KD):
                    last = mm(bank(2 * t)[:, 0:EXPERTS], h2T[:, TILE[t], k], w_r[:, k], start=k == 0, stop=k == KD - 1)
                last.then_inc(logit_mm, 1)

            pe.wait_ge(w_r_in, 16)
            turn_h2(0)
            for t in range(1, NT):
                turn_h2(t)
                logits(t - 1)
            logits(NT - 1)
            pe.wait_ge(mask_ok, 1)
            for t in range(NT):
                dst = bank(1)[:, t * EXPERTS:(t + 1) * EXPERTS]
                mm(dst, before, R["mask"][:, t], start=True, stop=t == 0)
                for s in range(t):
                    mm(dst, ones_b, R["mask"][:, s], start=False, stop=s == t - 1)
            for s in range(NT):
                last = mm(bank(1)[:, NT * EXPERTS:(NT + 1) * EXPERTS], ones_b, R["mask"][:, s], start=s == 0, stop=s == NT - 1)
            last.then_inc(rank_mm, 1)

            def turn_x(i):
                pe.wait_ge(xe_in, 16 * (i + 1))
                reach(pe, helo_ok, i - 1)
                for k in range(KD):
                    last = nc.tensor.transpose(bank(TB, 2)[:, k * P:(k + 1) * P], xe[:, k * P:(k + 1) * P], ident)
                last.then_inc(xeT_up, 1)

            def first(i):
                pe.wait_ge(xhl_ok, 2 * i + 2)
                reach(pe, he_ok, i)
                for p in range(KD):
                    pe.wait_ge(lo13_ok, KD * i + p + 1)
                    for n, (s, w) in enumerate(((x_hi, hi13), (x_hi, lo13), (x_lo, hi13))):
                        for b in range(4):
                            last = mm(bank(b)[:, 0:F2], s[:, p], w[:, p % 4, b * F2:(b + 1) * F2],
                                      start=p == 0 and n == 0, stop=p == KD - 1 and n == 2)
                    last.then_inc(fed13, 1)

            def second(i):
                reach(pe, helo_ok, i + 1)
                reach(pe, ye_a, i)
                reach(pe, ye_v, i)
                for p in range(6):
                    pe.wait_ge(lo2_ok, 6 * i + p + 1)
                    n_ = P if p < FULL else LAST
                    for n, (s, w) in enumerate(((he_hi, hi2), (he_hi, lo2), (he_lo, hi2))):
                        for b in range(2):
                            last = mm(bank(YB + b), s[0:n_, p], w[0:n_, p % 3, b * BANK:(b + 1) * BANK],
                                      start=p == 0 and n == 0, stop=p == 5 and n == 2)
                    last.then_inc(fed2, 1)

            def turn_he(i):
                pe.wait_ge(he_ok, i + 1)
                pe.wait_ge(xeT_ok, i + 2) if not last_of_pass[0] else pe.wait_ge(xeT_ok, i + 1)
                for k in range(6):
                    last = nc.tensor.transpose(bank(TB, 2)[:, k * P:(k + 1) * P], he[:, k * P:(k + 1) * P], ident)
                last.then_inc(heT_up, 1)

            last_of_pass = [False]

            def one_pass(i0):
                last_of_pass[0] = False
                turn_x(i0)
                first(i0)
                turn_x(i0 + 1)
                turn_he(i0)
                with pe.Fori(1, EXPERTS - 1) as e:
                    i = pe.snap(i0 + e)
                    first(i)
                    turn_x(i + 1)
                    second(i - 1)
                    turn_he(i)
                i = i0 + EXPERTS - 1
                first(i)
                second(i - 1)
                last_of_pass[0] = True
                turn_he(i)
                second(i)

            one_pass(0)
            over = most(pe)
            with pe.If(over > threshold):
                with pe.Fori(1, ROUNDS) as r:
                    one_pass(pe.snap(r * EXPERTS))


def kernel(**inputs):
    import numpy as np
    import concourse.bacc as bacc
    from concourse.bass_utils import run_bass_kernel_spmd

    nc = bacc.Bacc("TRN2", target_bir_lowering=False, num_devices=1)
    arrays, args = {}, {}
    for name in ("x", "c", "w_ada", "b_ada", "g_pre_mix", "g_post_mix", "g_pre_ffn", "g_post_ffn", "w_in", "w_dw",
                 "b_dw", "conv_ln_g", "conv_ln_b", "w_gate_up", "b_gate", "gla_norm_g", "w_out", "w_router",
                 "b_router", "w1", "w3", "w2"):
        a = np.ascontiguousarray(inputs[name])
        arrays[f"in_{name}"] = a
        args[name] = nc.dram_tensor(f"in_{name}", a.shape, mybir.dt.from_np(a.dtype), kind="ExternalInput").ap()
    out = nc.dram_tensor("out", (1, T, D), mybir.dt.float32, kind="ExternalOutput").ap()
    build(nc, out=out, **args)
    result = run_bass_kernel_spmd(nc, [arrays], core_ids=[0])
    return result.results[0]["out"]
```

```python
import concourse.bass as bass
from concourse import mybir

P = 128
BANK = 512
T, D = 512, 1024
NT, KD = T // P, D // P
CONV, WIDTH = 512, 31
SHARED = 23
NC = CONV // P
HEADS, DK, DV, CHUNK = 4, 64, 128, 64
QK = HEADS * DK
NCH = T // CHUNK
RANK, TAU = 16, 16.0
SUMS = 4
UNIT = 256
EXPERTS, GROUPS, F = 16, 4, 704
FULL, LAST = F // P, F % P
F2 = F // 2
BLOCK = 128
ROUNDS = T // BLOCK
EPS = 1e-6
BIG = 1e30


def build(nc, x, c, w_ada, b_ada, g_pre_mix, g_post_mix, g_pre_ffn, g_post_ffn, w_in, w_dw, b_dw,
          conv_ln_g, conv_ln_b, w_gate_up, b_gate, gla_norm_g, w_out, w_router, b_router,
          w1, w3, w2, out, threshold=BLOCK):
    f32, f32r = mybir.dt.float32, mybir.dt.float32r
    i32, u32, bf16 = mybir.dt.int32, mybir.dt.uint32, mybir.dt.bfloat16
    ALU, ACT, AX = mybir.AluOpType, mybir.ActivationFunctionType, mybir.AxisListType

    base = (nc.sbuf_base + 31) // 32 * 32

    def at(name, shape, dt, offset):
        return nc.alloc_sbuf_tensor_at(name, list(shape), dt, offset=base + 4 * offset).ap()

    PIECE = 2 * F
    RAW, SPLIT = 0, KD * PIECE + 6 * D
    KEEP = 2 * SPLIT
    raw13 = at("raw13", [P, KD, PIECE], f32, RAW)
    raw2 = at("raw2", [P, 6, D], f32, RAW + KD * PIECE)
    ada_w = at("ada_w", [P, 2, KD, BANK], f32, RAW)
    w_o = at("w_o", [P, KD, D], f32, RAW)
    w_i = at("w_i", [P, 2, KD, UNIT], f32, RAW + 8192)
    o = RAW + 12288
    ada_sum = at("ada_sum", [P, SUMS, BANK], f32, o)
    ada_bias = at("ada_bias", [P, 2, BANK], f32, o + 2048)
    lrT = at("lrT", [RANK + 1, T], f32, o + 3072)
    w_up = at("w_up", [RANK + 1, QK], f32, o + 3584)
    k_dec = at("k_dec", [P, NT, 2, QK], f32, o)
    state = at("state", [P, NCH, 2, DV], f32, o + 2048)
    h2 = at("h2", [P, NT, D], f32, o)
    o += 4096
    dw_rows = at("dw_rows", [WIDTH, CONV], f32, o)
    part3 = at("part3", [P, T], f32, o)
    par_rows = at("par_rows", [77, P], f32, o + 512)
    dwT = at("dwT", [P, NC, WIDTH], f32, o + 640)
    hi13 = at("hi13", [P, 4, PIECE], f32r, SPLIT)
    lo13 = at("lo13", [P, 4, PIECE], f32r, SPLIT + 4 * PIECE)
    hi2 = at("hi2", [P, 3, D], f32r, SPLIT + 8 * PIECE)
    lo2 = at("lo2", [P, 3, D], f32r, SPLIT + 8 * PIECE + 3 * D)
    wi_hi = at("wi_hi", [P, 2, KD, UNIT], f32r, SPLIT)
    wi_lo = at("wi_lo", [P, 2, KD, UNIT], f32r, SPLIT + 4096)
    ada_w23 = at("ada_w23", [P, 2, KD, BANK], f32, SPLIT + 8192)
    hT_hi = at("hT_hi", [P, KD, T], f32r, SPLIT + 8192)
    hT_lo = at("hT_lo", [P, KD, T], f32r, SPLIT + 12288)
    wo_hi = at("wo_hi", [P, KD, D], f32r, SPLIT)
    wo_lo = at("wo_lo", [P, KD, D], f32r, SPLIT + 8192)
    gate1 = at("gate1", [P, D], f32, SPLIT + 16384)
    o = KEEP
    ident = at("ident", [P, P], f32, o)
    ones = at("ones", [P, P], f32, o + 128)
    later = at("later", [P, P], f32, o + 256)
    w_r = at("w_r", [P, KD, EXPERTS], f32, o + 256)
    before = at("before", [P, P], bf16, o + 384)
    ones_b = at("ones_b", [P, P], bf16, o + 448)
    o += 512
    SMALLS = 344
    smalls = at("smalls", [P, SMALLS], f32, o)
    small, o = {}, 0
    for name, n in (("par", 80), ("half", 2), ("csil", 8), ("A1", 8), ("B1", 8), ("modc", 16), ("eps", 1),
                    ("xss", 4), ("xstd", 4), ("xr", 4), ("yss", 4), ("ystd", 4), ("yr", 4), ("x2ss", 4),
                    ("x2std", 4), ("x2r", 4), ("decay", 16), ("brow", 16), ("wts", 8), ("fss", 4),
                    ("fstd", 4), ("fr", 4), ("key", 16), ("gkey", 4), ("ostd", 16), ("or", 16)):
        small[name] = smalls[:, o:o + n]
        o += n
    pos = smalls[:, o:o + 8].bitcast(u32)
    count = smalls[:, o + 8:o + 9].bitcast(i32)
    ids = smalls[:, o + 12:o + 16].bitcast(i32)
    rows_now = smalls[:, o + 10:o + 11].bitcast(i32)
    no_row = smalls[:, o + 11:o + 12].bitcast(i32)
    rows_of = smalls[:, o + 16:o + 16 + ROUNDS * EXPERTS].bitcast(i32)
    assert o + 16 + ROUNDS * EXPERTS <= SMALLS
    o = KEEP + 512 + SMALLS
    gate2 = at("gate2", [P, D], f32, o)
    scale2 = at("scale2", [P, D], f32, o + 1024)
    shift2 = at("shift2", [P, D], f32, o + 2048)
    o += 3072
    x2 = at("x2", [P, NT, D], f32, o)
    soft_l = at("soft_l", [P, NT, QK], f32, o)
    w_lr = at("w_lr", [P, KD, P], f32, o)
    soft_m = at("soft_m", [P, NT, QK], f32, o + 1024)
    o_sq = at("o_sq", [P, 2, BANK], f32, o + 2048)
    sig = at("sig", [P, 2, BANK], f32, o + 2048)
    head_sq = at("head_sq", [P, HEADS, BANK], f32, o + 2048)
    o_std = at("o_std", [P, 2, BANK], f32, o + 3072)
    h_tmp = at("h_tmp", [P, 2, BANK], f32, o + 3072)
    term = at("term", [P, 2, BANK], f32, o + 3072)
    o += 4096
    x_rows = at("x_rows", [P, NT, D], f32, o)
    lr_hi = at("lr_hi", [P, KD, P], f32r, o)
    lr_lo = at("lr_lo", [P, KD, P], f32r, o + 1024)
    kv = at("kv", [P, NT, 3 * QK], f32, o)
    g_hi = at("g_hi", [P, HEADS, T], f32r, o)
    gT = at("gT", [P, HEADS, T], f32, o + 3072)
    g_lo = at("g_lo", [P, HEADS, T], f32r, o + 3072)
    h2T = at("h2T", [P, NT + 1, KD, P], f32, o)
    y_tmp = at("y_tmp", [P, D], f32, o + 2048)
    xe = at("xe", [P, D], f32, o)
    x_hi = at("x_hi", [P, KD, P], f32r, o + 2048)
    x_lo = at("x_lo", [P, KD, P], f32r, o + 3072)
    o += 5120
    xhat = at("xhat", [P, NT, D], f32, o)
    conv = at("conv", [P, NC, T], f32, o)
    conv_lo = at("conv_lo", [P, NC, T], f32r, o)
    uT = at("uT", [P, NC, WIDTH - 1 + T], f32, o + 2048)
    conv_hi = at("conv_hi", [P, NC, T], f32r, o + 2048)
    rt = at("rt", [P, 1024], f32, o + 2048)
    s_act = at("s_act", [P, F], f32, o)
    he = at("he", [P, 6 * P], f32, o + 704)
    he_hi = at("he_hi", [P, 6, P], f32r, o + 1472)
    he_lo = at("he_lo", [P, 6, P], f32r, o + 2240)
    y_e = at("y_e", [P, D], f32, o + 3008)
    o += 4216
    qT = at("qT", [P, 2, T], f32, o)
    junk = at("junk", [P, D], f32, o)
    o += 1024
    assert base + 4 * o <= nc.sbuf_usable_end, (base + 4 * o, nc.sbuf_usable_end)
    back = at("back", [P, NT, 2, D], f32, RAW)
    mixed = at("mixed", [P, NT, D], f32, SPLIT)
    result = at("result", [P, NT, D], f32, SPLIT + 4096)

    psum = nc.alloc_psum_tensor("psum", [P, 8 * BANK], f32).ap()

    def bank(b, n=1):
        return psum[:, b * BANK:(b + n) * BANK]

    H1 = psum[:, 0:2 * BANK].rearrange("p (b n) -> p b n", b=2)[:, :, 0:F2]
    H3 = psum[:, 2 * BANK:4 * BANK].rearrange("p (b n) -> p b n", b=2)[:, :, 0:F2]
    TB, YB = 4, 6

    h2_rows = nc.dram_tensor("h2_rows", (T, D), f32).ap()
    token = nc.dram_tensor("token", (T * EXPERTS, 1), i32).ap()
    y_rows = nc.dram_tensor("y_rows", (T * EXPERTS, D), f32).ap()
    h2_rows_v = h2_rows.rearrange("(t p) d -> p t d", p=P)
    token_v = token.rearrange("(r p e) one -> p r (e one)", p=P, e=EXPERTS)
    y_rows_v = y_rows.rearrange("(r p e) d -> r e p d", p=P, e=EXPERTS)

    w_ada_v = w_ada[0].rearrange("(k p) n -> p k n", p=P)
    w_in_v = w_in[0].rearrange("(k p) n -> p k n", p=P)
    x_v = x[0].rearrange("(t p) d -> p t d", p=P)
    out_v = out[0].rearrange("(t p) d -> p t d", p=P)
    w1_v = w1[0].rearrange("e (k p) f -> e p k f", p=P)
    w3_v = w3[0].rearrange("e (k p) f -> e p k f", p=P)
    w2_v = w2[0, :, 0:FULL * P, :].rearrange("e (k p) d -> e p k d", p=P)

    def sem(name):
        return nc.alloc_semaphore(name)

    par_in, consts, cols_up, cols_ok = map(sem, ("par_in", "consts", "cols_up", "cols_ok"))
    x_in = [sem(f"x_in{t}") for t in range(NT)]
    ada_in = [sem(f"ada_in{i}") for i in range(4)]
    bias_in, lr_zero, diag_ok, spread_mm = map(sem, ("bias_in", "lr_zero", "diag_ok", "spread_mm"))
    ada_summed, ada_mm, ada_taken = map(sem, ("ada_summed", "ada_mm", "ada_taken"))
    w_out_in, rows_in, w_r_in, lr_in = map(sem, ("w_out_in", "rows_in", "w_r_in", "lr_in"))
    wi_in = [sem(f"wi_in{i}") for i in range(2)]
    wi_hi_ok, wi_lo_ok, wo_hi_ok, wo_lo_ok, lrw_ok, biased = map(
        sem, ("wi_hi_ok", "wi_lo_ok", "wo_hi_ok", "wo_lo_ok", "lrw_ok", "biased"))
    yhi_ok, ylo_ok, tmp_ok, lr_mm = map(sem, ("yhi_ok", "ylo_ok", "tmp_ok", "lr_mm"))
    x_again = [sem(f"x_again{i}") for i in range(2)]
    xhat_ok, xT_up, mod1_ok, hT_a, hT_v = map(sem, ("xhat_ok", "xT_up", "mod1_ok", "hT_a", "hT_v"))
    sig_ok, u_ok = map(sem, ("sig_ok", "u_ok"))
    unit_mm, unit_ok, z_mm, gate_parts, soft_ok, later_mm = map(
        sem, ("unit_mm", "unit_ok", "z_mm", "gate_parts", "soft_ok", "later_mm"))
    decay_ok, kdec_ok, upd_mm, state_ok = map(sem, ("decay_ok", "kdec_ok", "upd_mm", "state_ok"))
    tap_ok = [sem(f"tap_ok{j}") for j in range(NC)]
    TAP0 = [0] * (NC - 1) + [SHARED]
    mean_mm, cent_ok, csq_ok, var_mm, cstd_ok, cnorm_ok = map(
        sem, ("mean_mm", "cent_ok", "csq_ok", "var_mm", "cstd_ok", "cnorm_ok"))
    o_mm, osq_ok, osum_mm, ostd_ok, ygla_ok = map(sem, ("o_mm", "osq_ok", "osum_mm", "ostd_ok", "ygla_ok"))
    y_mm, yss_ok, ystd_ok, x2_ok, x2ss_ok, x2std_ok, h2_ok = map(
        sem, ("y_mm", "yss_ok", "ystd_ok", "x2_ok", "x2ss_ok", "x2std_ok", "h2_ok"))
    h2T_up, h2T_a, h2T_v, logit_mm, exp_ok, exp_in, mask_ok, rank_mm, pos_ok = map(
        sem, ("h2T_up", "h2T_a", "h2T_v", "logit_mm", "exp_ok", "exp_in", "mask_ok", "rank_mm", "pos_ok"))
    ids_ok, picked, token_ok, scattered, rows_of_in, h2_out = map(sem, ("ids_ok", "picked", "token_ok", "scattered", "rows_of_in", "h2_out"))
    first_tap, term_ok, term_added = map(sem, ("first_tap", "term_ok", "term_added"))
    logT_mm, logT_ok = map(sem, ("logT_mm", "logT_ok"))
    eps_ok, xr_ok = map(sem, ("eps_ok", "xr_ok"))
    act_step, pool_step, dve_step = map(sem, ("act_step", "pool_step", "dve_step"))
    raw13_in = [sem(f"raw13_in{i}") for i in range(4)]
    raw2_in = [sem(f"raw2_in{i}") for i in range(3)]
    hi13_ok, lo13_ok, fed13, hi2_ok, lo2_ok, fed2 = map(
        sem, ("hi13_ok", "lo13_ok", "fed13", "hi2_ok", "lo2_ok", "fed2"))
    xe_in, xeT_up, xhi_ok, xlo_ok = map(sem, ("xe_in", "xeT_up", "xhi_ok", "xlo_ok"))
    silu_ok, he_ok, heT_up, hehi_ok, helo_ok = map(
        sem, ("silu_ok", "he_ok", "heT_up", "hehi_ok", "helo_ok"))
    ye_a, ye_v, ye_out = map(sem, ("ye_a", "ye_v", "ye_out"))
    back_in = [[sem(f"back_in{t}_{k}") for k in range(2)] for t in range(NT)]
    f_okp, f_m1, f_mix, f_ss, f_std, f_r, f_ok, stored = map(sem, ("f_okp", "f_m1", "f_mix", "f_ss", "f_std", "f_r", "f_ok", "stored"))

    def reach(eng, s, value):
        if not isinstance(value, int) or value > 0:
            eng.wait_ge(s, value)

    def chain(eng, s):
        n = [0]

        def link(ins):
            ins.then_inc(s, 1)
            n[0] += 1
            eng.wait_ge(s, n[0])
        return link

    def ada_block(b):
        return (ada_w23 if b in (2, 3) else ada_w)[:, b % 2]

    def most(eng):
        eng.wait_ge(pos_ok, 1)
        return eng.value_load(count[0:1, 0:1], min_val=0, max_val=T)

    V0 = 2 * CONV + 2 * QK
    G0 = V0 + HEADS * DV
    UNITS = ([("conv", j, (j * P, CONV + j * P)) for j in range(NC)]
             + [("kv", 0, (2 * CONV + QK,)), ("kv", 1, (V0,)), ("kv", 2, (V0 + UNIT,)), ("q", 0, (2 * CONV,)),
                ("g", 0, (G0,)), ("g", 1, (G0 + UNIT,))])
    NU = len(UNITS)
    LR0 = G0 + HEADS * DV
    PAIR = {("conv", 0): 0, ("conv", 1): 1, ("conv", 2): 2, ("conv", 3): 0, "lr": 1, ("kv", 0): 2, ("kv", 1): 0,
            ("kv", 2): 1, "z": 2, ("q", 0): 0, ("g", 0): 1, "later": 2, ("g", 1): 1}
    O_BANK = [4, 5, 0, 1]
    TILE = [0, 1, 3, 4]
    TERMS = {4: range(1, 5), 5: range(5, 9), 6: range(9, 14), 7: range(14, 19), 8: range(19, SHARED)}
    GLA_FIRST = [*range(NC, KD), *range(NC)]

    R = {}
    o = 0
    for name, shape in (("sh", (NT, EXPERTS)), ("p", (NT, EXPERTS)), ("sel", (NT, EXPERTS)), ("q", (4, NT * GROUPS)),
                        ("hot0", (NT, EXPERTS)), ("hot1", (NT, EXPERTS)), ("kmax", (2, NT)), ("w", (2, NT)),
                        ("sum", (2, NT)), ("m32", (NT, EXPERTS // 2))):
        n = shape[0] * shape[1]
        part = rt[:, o:o + n].rearrange("p (a b) -> p a b", a=shape[0])
        R[name] = part
        o += n
    R["a"] = rt[:, o:o + NT]
    R["mask"] = rt[:, o - NT * EXPERTS // 2:o].bitcast(bf16).rearrange("p (a b) -> p a b", a=NT)
    R["hot"] = [R["hot0"], R["hot1"]]
    assert o + NT <= T
    logT = rt[0:EXPERTS, T:2 * T]

    block = nc.Block()
    with block:

        @block.sync
        def _(sp):
            row = 0
            for src, n in ((b_ada, 48), (g_pre_mix, 8)):
                sp.dma_start(par_rows[row:row + n, :], src.rearrange("o (r q) -> (o r) q", q=P)).then_inc(par_in, 16)
                row += n

            def ada(b):
                if b >= 4:
                    sp.wait_ge(ada_summed, b - 3 if b < 6 else b - 1)
                sp.dma_start(ada_block(b), w_ada_v[:, :, b * BANK:(b + 1) * BANK]).then_inc(ada_in[b % 4], 16)

            def unit(u):
                starts = UNITS[u][2]
                n = UNIT // len(starts)
                if u >= 2:
                    sp.wait_ge(wi_lo_ok, u - 1)
                for m, c0 in enumerate(starts):
                    sp.dma_start(w_i[:, u % 2, :, m * n:(m + 1) * n], w_in_v[:, :, c0:c0 + n]).then_inc(
                        wi_in[u % 2], 32 // len(starts))

            for t in range(NT):
                sp.dma_start(x_rows[:, t], x_v[:, t]).then_inc(x_in[t], 16)
            for b in range(4):
                ada(b)
            unit(0)
            sp.wait_ge(lr_zero, 1)
            sp.dma_start(w_lr[:, :, 0:RANK], w_in_v[:, :, LR0:LR0 + RANK]).then_inc(lr_in, 16)
            unit(1)
            ada(4)
            ada(5)
            for u, blocks in ((2, (6,)), (3, (7,)), (4, (8, 9)), (5, (10,)), (6, (11,))):
                unit(u)
                for b in blocks:
                    ada(b)
            for u in range(7, NU):
                unit(u)
            sp.wait_ge(ada_summed, 12)
            sp.dma_start(w_o, w_out[0].rearrange("(k p) n -> p k n", p=P)).then_inc(w_out_in, 16)

            def up(i, e, groups=range(4)):
                for g in groups:
                    reach(sp, lo13_ok, KD * (i - 1) + 2 * (g + 1))
                    piece = raw13[:, 2 * g:2 * g + 2]
                    sp.dma_start(piece[:, :, 0:F], w1_v[e, :, 2 * g:2 * g + 2, :]).then_inc(raw13_in[g], 16)
                    sp.dma_start(piece[:, :, F:], w3_v[e, :, 2 * g:2 * g + 2, :]).then_inc(raw13_in[g], 16)

            def down(i, e):
                for g in range(3):
                    reach(sp, lo2_ok, 6 * (i - 1) + 2 * (g + 1))
                    if g < 2:
                        sp.dma_start(raw2[:, 2 * g:2 * g + 2], w2_v[e, :, 2 * g:2 * g + 2, :]).then_inc(raw2_in[g], 32)
                    else:
                        sp.dma_start(raw2[:, 4], w2_v[e, :, 4, :]).then_inc(raw2_in[g], 16)
                        sp.dma_start(raw2[0:LAST, 5], w2[0, e, FULL * P:, :]).then_inc(raw2_in[g], 16)

            sp.wait_ge(kdec_ok, 2)
            sp.dma_start(x2[:, 0:2], x_v[:, 0:2]).then_inc(x_again[0], 16)
            sp.wait_ge(wo_lo_ok, KD)
            up(0, 0)
            sp.wait_ge(ygla_ok, HEADS)
            sp.wait_ge(cnorm_ok, NC)
            sp.dma_start(x2[:, 2:4], x_v[:, 2:4]).then_inc(x_again[1], 16)
            for t in range(NT):
                sp.wait_ge(h2_ok, t + 1)
                sp.dma_start(h2_rows_v[:, t], h2[:, t]).then_inc(h2_out, 16)
            sp.wait_ge(h2_out, 16 * NT)
            sp.wait_ge(h2T_up, NT)

            def one_pass(i0):
                down(i0, 0)
                up(i0 + 1, 1)
                with sp.Fori(2, EXPERTS - 1) as e:
                    up(i0 + e, e)
                    down(i0 + e - 1, e - 1)
                e = EXPERTS - 1
                up(i0 + e, e, range(2))
                down(i0 + e - 1, e - 1)
                up(i0 + e, e, range(2, 4))
                down(i0 + e, e)

            one_pass(0)
            over = most(sp)
            with sp.If(over > threshold):
                with sp.Fori(1, ROUNDS) as r:
                    i0 = sp.snap(r * EXPERTS)
                    up(i0, 0)
                    one_pass(i0)
            for t in range(NT):
                sp.wait_ge(*((f_okp, t + 1) if t < 2 else (f_ok, t - 1)))
                sp.dma_start(out_v[:, t], result[:, t]).then_inc(stored, 16)
            sp.wait_ge(stored, 16 * NT)

        @block.gpsimd
        def _(gp):
            gp.iota(small["key"], pattern=[[-1, EXPERTS]], base=EXPERTS, channel_multiplier=0,
                    allow_small_or_imprecise_dtypes=True).then_inc(consts, 1)
            gp.iota(small["gkey"], pattern=[[-1, GROUPS]], base=GROUPS, channel_multiplier=0,
                    allow_small_or_imprecise_dtypes=True).then_inc(consts, 1)
            gp.memset(ident, 0.0).then_inc(pool_step, 1)
            gp.memset(ones, 1.0).then_inc(consts, 1)
            gp.memset(small["half"], 1.0).then_inc(pool_step, 1)
            gp.memset(w_lr, 0.0).then_inc(lr_zero, 1)
            gp.memset(lrT, 1.0).then_inc(consts, 1)
            gp.wait_ge(pool_step, 2)
            gp.wait_ge(consts, 4)
            gp.affine_select(out=ident, in_=ident, compare_op=ALU.not_equal, fill=1.0, base=0,
                             pattern=[[-1, P]], channel_multiplier=1).then_inc(consts, 1)
            gp.memset(ones_b, 1.0).then_inc(consts, 1)
            gp.wait_ge(consts, 6)
            gp.affine_select(out=before, in_=ones, compare_op=ALU.is_gt, fill=0.0, base=0,
                             pattern=[[1, P]], channel_multiplier=-1).then_inc(consts, 1)
            gp.affine_select(out=later, in_=ones, compare_op=ALU.is_gt, fill=0.0, base=0,
                             pattern=[[-1, P]], channel_multiplier=1).then_inc(pool_step, 1)
            gp.wait_ge(pool_step, 3)
            gp.affine_select(out=later[:, 0:CHUNK], in_=later[:, 0:CHUNK], compare_op=ALU.is_gt, fill=0.0, base=CHUNK,
                             pattern=[[0, CHUNK]], channel_multiplier=-1).then_inc(consts, 1)
            gp.affine_select(out=small["half"][:, 0:1], in_=small["half"][:, 0:1], compare_op=ALU.is_gt, fill=0.0,
                             base=CHUNK, pattern=[[0, 1]], channel_multiplier=-1).then_inc(consts, 1)
            gp.affine_select(out=small["half"][:, 1:2], in_=small["half"][:, 1:2], compare_op=ALU.is_ge, fill=0.0,
                             base=-CHUNK, pattern=[[0, 1]], channel_multiplier=1).then_inc(consts, 1)
            gp.iota(ids, pattern=[[P, NT]], base=0, channel_multiplier=1).then_inc(ids_ok, 1)
            gp.memset(rows_of, 0).then_inc(ids_ok, 1)
            gp.memset(no_row, 0).then_inc(ids_ok, 1)
            gp.wait_ge(ids_ok, 3)
            gp.dma_start(token_v, rows_of.rearrange("p (r e) -> p r e", r=ROUNDS)).then_inc(token_ok, 16)

            def low(u):
                gp.wait_ge(wi_hi_ok, u + 1)
                gp.tensor_tensor(wi_lo[:, u % 2], w_i[:, u % 2], wi_hi[:, u % 2].bitcast(f32), ALU.subtract).then_inc(wi_lo_ok, 1)
                gp.wait_ge(wi_lo_ok, u + 1)

            def bias(r):
                gp.wait_ge(ada_summed, 5 + r)
                gp.wait_ge(bias_in, 32)
                row, s = slice(32 * (r % 4), 32 * (r % 4) + 1), r % SUMS
                gp.tensor_tensor(ada_sum[row, s], ada_sum[row, s], ada_bias[row, r // 4], ALU.add).then_inc(biased, 1)
                gp.wait_ge(biased, r + 1)

            low(0)
            gp.wait_ge(lrw_ok, 1)
            gp.tensor_tensor(lr_lo, w_lr, lr_hi.bitcast(f32), ALU.subtract).then_inc(lrw_ok, 1)
            gp.wait_ge(lrw_ok, 2)
            low(1)
            def added(tap):
                gp.wait_ge(*((first_tap, 1) if tap == 1 else (term_added, tap - 1)))
                gp.wait_ge(term_ok, tap)
                gp.tensor_tensor(conv[:, NC - 1], conv[:, NC - 1], term[:, tap % 2], ALU.add).then_inc(term_added, 1)

            for u in range(2, NU):
                if u == NU - 1:
                    gp.wait_ge(ada_mm, 12)
                    gp.memset(k_dec[0:CHUNK, :, 1, :], 0.0).then_inc(pool_step, 1)
                    gp.wait_ge(pool_step, 4)
                    gp.memset(k_dec[CHUNK:P, :, 0, :], 0.0).then_inc(pool_step, 1)
                    gp.wait_ge(pool_step, 5)
                    gp.wait_ge(decay_ok, 1)
                    gp.tensor_tensor(k_dec[0:CHUNK, :, 0, :], kv[0:CHUNK, :, 0:QK], soft_m[0:CHUNK], ALU.mult).then_inc(kdec_ok, 1)
                    gp.wait_ge(kdec_ok, 1)
                    gp.tensor_tensor(k_dec[CHUNK:P, :, 1, :], kv[CHUNK:P, :, 0:QK], soft_m[CHUNK:P], ALU.mult).then_inc(kdec_ok, 1)
                    gp.wait_ge(kdec_ok, 2)
                low(u)
                for r in {2: (0, 1), 3: (2, 3), 4: (4,), 5: (5, 6), 6: (7,)}.get(u, ()):
                    bias(r)
                if u == 7:
                    gp.wait_ge(gate_parts, 1)
                    gp.tensor_tensor(soft_l, soft_l, soft_m, ALU.add).then_inc(soft_ok, 1)
                    gp.wait_ge(soft_ok, 1)
                for tap in TERMS.get(u - 2, ()):
                    added(tap)
            for tap in TERMS[NU - 2]:
                added(tap)
            for n, k in enumerate(GLA_FIRST):
                gp.wait_ge(wo_hi_ok, n + 1)
                gp.tensor_tensor(wo_lo[:, k], w_o[:, k], wo_hi[:, k].bitcast(f32), ALU.subtract).then_inc(wo_lo_ok, 1)
                gp.wait_ge(wo_lo_ok, n + 1)
            gp.wait_ge(y_mm, NT)
            for p in range(4):
                gp.wait_ge(hi13_ok, p + 1)
                gp.tensor_tensor(lo13[:, p], raw13[:, p], hi13[:, p].bitcast(f32), ALU.subtract).then_inc(lo13_ok, 1)
            gp.wait_ge(lo13_ok, 4)
            gp.wait_ge(pos_ok, 1)
            gp.wait_ge(token_ok, 16)
            for t in range(NT):
                for k in range(2):
                    gp.indirect_dma_start(
                        out=token, out_offset=bass.IndirectOffsetOnAxis(ap=pos[:, 4 * k + t:4 * k + t + 1], axis=0),
                        in_=ids[:, t:t + 1], in_offset=None).then_inc(scattered, 16)
            gp.wait_ge(scattered, 32 * NT)
            gp.dma_start(rows_of.rearrange("p (r e) -> p r e", r=ROUNDS), token_v).then_inc(rows_of_in, 16)
            gp.wait_ge(rows_of_in, 16)
            gp.wait_ge(h2_out, 16 * NT)

            def load(i):
                reach(gp, xeT_up, i)
                column = rows_of[:, i:i + 1] if isinstance(i, int) else rows_of[:, bass.ds(i, 1)]
                reach(gp, picked, 2 * i)
                gp.tensor_tensor(rows_now, column, no_row, ALU.add).then_inc(picked, 1)
                gp.wait_ge(picked, 2 * i + 1)
                gp.tensor_tensor(no_row, no_row, no_row, ALU.add).then_inc(picked, 1)
                gp.indirect_dma_start(out=xe, out_offset=None, in_=h2_rows,
                                      in_offset=bass.IndirectOffsetOnAxis(ap=rows_now, axis=0)).then_inc(xe_in, 16)

            def store(i, r, e):
                gp.wait_ge(ye_a, i + 1)
                gp.wait_ge(ye_v, i + 1)
                gp.dma_start(y_rows_v[r, e], y_e).then_inc(ye_out, 16)

            def one_pass(i0, r):
                for e in range(3):
                    load(i0 + e)
                with gp.Fori(1, EXPERTS - 2) as e:
                    i = gp.snap(i0 + e)
                    load(i + 2)
                    store(i - 1, r, e - 1)
                for e in range(EXPERTS - 3, EXPERTS):
                    store(i0 + e, r, e)

            def gather(rounds):
                rows = y_rows[0:rounds * EXPERTS * BLOCK]
                for t in range(NT):
                    for k in range(2):
                        gp.indirect_dma_start(
                            out=back[:, t, k], out_offset=None, in_=rows,
                            in_offset=bass.IndirectOffsetOnAxis(ap=pos[:, 4 * k + t:4 * k + t + 1], axis=0)).then_inc(back_in[t][k], 16)

            one_pass(0, 0)
            over = most(gp)
            with gp.If(over > threshold):
                with gp.Fori(1, ROUNDS) as r:
                    one_pass(gp.snap(r * EXPERTS), r)
                gp.wait_ge(ye_out, 16 * ROUNDS * EXPERTS)
                gather(ROUNDS)
            with gp.Else():
                gp.wait_ge(ye_out, 16 * EXPERTS)
                gather(1)
            for t in range(2):
                gp.wait_ge(f_r, 2 * t + 2)
                gp.tensor_tensor(result[:, t], result[:, t], x2[:, t], ALU.add).then_inc(f_okp, 1)
                gp.wait_ge(f_okp, t + 1)
            gp.wait_ge(back_in[NT - 1][1], 16)

        @block.scalar
        def _(act):
            link = chain(act, act_step)
            row = 56
            for src, n in ((c, 8), (b_dw, 4), (conv_ln_g, 4), (conv_ln_b, 4), (gla_norm_g, 1)):
                act.dma_start(par_rows[row:row + n, :], src.rearrange("o (r q) -> (o r) q", q=P)).then_inc(par_in, 16)
                row += n
            act.dma_start(dw_rows, w_dw[0]).then_inc(par_in, 16)
            b_rows = b_ada[0, 2 * D:].rearrange("(s r n) -> s r n", s=2, r=4)
            for i in range(2):
                act.dma_start(ada_bias[0:P:32, i], b_rows[i]).then_inc(bias_in, 16)
            act.dma_start(w_up[0:RANK, :], w_gate_up[0]).then_inc(rows_in, 16)
            act.dma_start(w_up[RANK:RANK + 1, :], b_gate).then_inc(rows_in, 16)
            act.dma_start(small["brow"], b_router.rearrange("(o n) -> o n", o=1).broadcast_to((P, EXPERTS))).then_inc(rows_in, 16)
            act.dma_start(gate1, g_post_mix.broadcast_to((P, D))).then_inc(rows_in, 16)
            act.dma_start(gate2, g_post_ffn.broadcast_to((P, D))).then_inc(rows_in, 16)
            act.dma_start(scale2, g_pre_ffn.broadcast_to((P, D))).then_inc(rows_in, 16)
            act.wait_ge(cols_ok, 1)
            link(nc.scalar.activation(small["csil"], small["par"][:, 56:64], ACT.Silu))
            for t in range(NT):
                act.wait_ge(x_in[t], 16)
                link(nc.scalar.activation(xhat[:, t], x_rows[:, t], ACT.Square, accum_out=small["xss"][:, t:t + 1]))
            act.wait_ge(eps_ok, 1)
            link(nc.scalar.activation(small["xstd"], small["xss"], ACT.Sqrt, scale=1.0 / D, bias=small["eps"]))
            act.wait_ge(xr_ok, 1)
            for t in range(NT):
                nc.scalar.activation(xhat[:, t], x_rows[:, t], ACT.Copy, scale=small["xr"][:, t:t + 1]).then_inc(xhat_ok, 1)
            def high(u):
                act.wait_ge(wi_in[u % 2], 32 * (u // 2 + 1))
                if u >= 2:
                    act.wait_ge(unit_mm, u - 1)
                nc.scalar.activation(wi_hi[:, u % 2], w_i[:, u % 2], ACT.Copy).then_inc(wi_hi_ok, 1)

            high(0)
            act.wait_ge(lr_in, 16)
            act.wait_ge(xhat_ok, NT)
            nc.scalar.activation(lr_hi, w_lr, ACT.Copy).then_inc(lrw_ok, 1)
            for k in range(KD):
                act.wait_ge(tmp_ok, k + 1)
                nc.scalar.activation(hT_hi[:, k], h_tmp[:, k % 2], ACT.Copy).then_inc(hT_a, 1)
            high(1)
            def term_of(tap):
                reach(act, term_added, tap - 2)
                nc.scalar.activation(term[:, tap % 2], uT[:, NC - 1, tap:tap + T], ACT.Copy,
                                     scale=dwT[:, NC - 1, tap:tap + 1]).then_inc(term_ok, 1)

            def conv_square(j):
                act.wait_ge(cent_ok, j + 1)
                reach(act, var_mm, j - 1)
                nc.scalar.activation(o_sq[:, j % 2], conv[:, j], ACT.Square).then_inc(csq_ok, 1)

            for u, (what, i, _) in enumerate(UNITS):
                b = bank(2 * PAIR[what, i], 2)
                act.wait_ge(unit_mm, u + 1)
                if u + 2 < NU:
                    high(u + 2)
                if what == "conv":
                    reach(act, u_ok, i - 1)
                    nc.scalar.activation(sig[:, i % 2], b[:, BANK:], ACT.Sigmoid).then_inc(sig_ok, 1)
                    if i == NC - 1:
                        act.wait_ge(lr_mm, 1)
                        act.wait_ge(consts, 10)
                        nc.scalar.activation(lrT[0:RANK, :], bank(2 * PAIR["lr"])[0:RANK, :], ACT.Copy).then_inc(unit_ok, 1)
                elif what == "kv":
                    nc.scalar.activation(kv[:, :, i * QK:(i + 1) * QK], b.rearrange("p (t n) -> p t n", t=NT), ACT.Copy).then_inc(unit_ok, 1)
                elif what == "q":
                    nc.scalar.activation(qT.rearrange("p m n -> p (m n)"), b, ACT.Copy, scale=DK ** -0.5).then_inc(unit_ok, 1)
                else:
                    nc.scalar.activation(gT[:, 2 * i:2 * i + 2].rearrange("p m n -> p (m n)"), b, ACT.Silu).then_inc(unit_ok, 1)
                if (what, i) == ("kv", 1):
                    act.wait_ge(z_mm, 1)
                    z = bank(2 * PAIR["z"], 2).rearrange("p (t n) -> p t n", t=NT)
                    link(nc.scalar.activation(soft_l, z, ACT.Abs))
                    link(nc.scalar.activation(soft_l, soft_l, ACT.Exp, scale=-1.0))
                    link(nc.scalar.activation(soft_l, soft_l, ACT.Ln, bias=1.0))
                    nc.scalar.activation(soft_m, z, ACT.Relu, scale=-1.0).then_inc(gate_parts, 1)
                if (what, i) == ("kv", 2):
                    act.wait_ge(later_mm, 1)
                    link(nc.scalar.activation(soft_m, bank(2 * PAIR["later"], 2).rearrange("p (t n) -> p t n", t=NT), ACT.Exp, scale=-1.0 / TAU))
                    nc.scalar.activation(small["decay"], bank(6)[:, 0:16], ACT.Exp, scale=-1.0 / TAU).then_inc(decay_ok, 1)
                    act.dma_start(w_r, w_router.rearrange("(k p) e -> p k e", p=P)).then_inc(w_r_in, 16)
                if u == NC:
                    act.wait_ge(u_ok, NC)
                    nc.scalar.activation(conv[:, NC - 1], uT[:, NC - 1, 0:T], ACT.Identity, scale=dwT[:, NC - 1, 0:1],
                                         bias=small["par"][:, 64 + NC - 1:64 + NC]).then_inc(first_tap, 1)
                for tap in TERMS.get(u, ()):
                    term_of(tap)
                if u == NU - 2:
                    for h in range(HEADS):
                        act.wait_ge(o_mm, h + 1)
                        if h == 2:
                            act.wait_ge(term_added, SHARED - 1)
                        nc.scalar.activation(head_sq[:, h], bank(O_BANK[h]), ACT.Square).then_inc(osq_ok, 1)
                    act.wait_ge(osum_mm, HEADS)
                    nc.scalar.activation(small["ostd"], bank(6)[:, 0:16], ACT.Sqrt, scale=1.0 / DV, bias=small["eps"]).then_inc(ostd_ok, 1)
                    conv_square(0)
                    conv_square(1)
            act.wait_ge(w_out_in, 16)
            for k in GLA_FIRST[:NC]:
                nc.scalar.activation(wo_hi[:, k], w_o[:, k], ACT.Copy).then_inc(wo_hi_ok, 1)
            conv_square(2)
            conv_square(3)
            for h in range(HEADS):
                act.wait_ge(ygla_ok, h + 1)
                nc.scalar.activation(g_hi[:, h], gT[:, h], ACT.Copy).then_inc(yhi_ok, 1)
            act.wait_ge(var_mm, NC)
            nc.scalar.activation(o_sq[:, 0], bank(3), ACT.Sqrt, scale=1.0 / CONV, bias=small["eps"]).then_inc(cstd_ok, 1)
            for k in GLA_FIRST[NC:]:
                nc.scalar.activation(wo_hi[:, k], w_o[:, k], ACT.Copy).then_inc(wo_hi_ok, 1)
            for j in range(NC):
                act.wait_ge(cnorm_ok, j + 1)
                link(nc.scalar.activation(conv[:, j], conv[:, j], ACT.Silu, scale=small["par"][:, 68 + j:69 + j],
                                          bias=small["par"][:, 72 + j:73 + j]))
                nc.scalar.activation(conv_hi[:, j], conv[:, j], ACT.Copy).then_inc(yhi_ok, 1)
            def h2T_out(t):
                act.wait_ge(h2T_up, t + 1)
                n = 1 if t == NT - 1 else 2
                nc.scalar.activation(h2T[:, TILE[t], 0:4 * n].rearrange("p k n -> p (k n)"), bank(2 * t, n), ACT.Copy).then_inc(h2T_a, 1)

            for t in range(NT):
                act.wait_ge(y_mm, t + 1)
                nc.scalar.activation(junk, bank(2 * t, 2), ACT.Square, accum_out=small["yss"][:, t:t + 1]).then_inc(yss_ok, 1)
                act.wait_ge(yss_ok, t + 1)
                nc.scalar.activation(small["ystd"][:, t:t + 1], small["yss"][:, t:t + 1], ACT.Sqrt, scale=1.0 / D,
                                     bias=small["eps"]).then_inc(ystd_ok, 1)
                if t == NT - 1:
                    for other in range(t):
                        h2T_out(other)
                act.wait_ge(x2_ok, 2 * t + 2)
                nc.scalar.activation(junk, x2[:, t], ACT.Square, accum_out=small["x2ss"][:, t:t + 1]).then_inc(x2ss_ok, 1)
                act.wait_ge(x2ss_ok, t + 1)
                nc.scalar.activation(small["x2std"][:, t:t + 1], small["x2ss"][:, t:t + 1], ACT.Sqrt, scale=1.0 / D,
                                     bias=small["eps"]).then_inc(x2std_ok, 1)
            h2T_out(NT - 1)
            def split13(i, p):
                g = p // 2
                if p % 2 == 0:
                    act.wait_ge(raw13_in[g], 32 * (i + 1))
                reach(act, fed13, KD * i + p - 3)
                nc.scalar.activation(hi13[:, p % 4], raw13[:, p], ACT.Copy).then_inc(hi13_ok, 1)

            act.wait_ge(y_mm, NT)
            split13(0, 0)
            act.wait_ge(exp_in, 1)
            nc.scalar.activation(R["p"], R["sh"], ACT.Exp).then_inc(exp_ok, 1)
            for p in range(1, 4):
                split13(0, p)

            def split2(i, p):
                g = p // 2
                if p % 2 == 0:
                    act.wait_ge(raw2_in[g], 32 * (i + 1))
                reach(act, fed2, 6 * i + p - 2)
                n = P if p < FULL else LAST
                nc.scalar.activation(hi2[0:n, p % 3], raw2[0:n, p], ACT.Copy).then_inc(hi2_ok, 1)

            def silu(i):
                act.wait_ge(fed13, KD * (i + 1))
                reach(act, he_ok, i)
                nc.scalar.activation(s_act.rearrange("p (b n) -> p b n", b=2), H1, ACT.Silu).then_inc(silu_ok, 1)

            def x_high(i):
                act.wait_ge(xeT_up, i + 1)
                reach(act, fed13, KD * i)
                nc.scalar.activation(x_hi.rearrange("p k n -> p (k n)"), bank(TB, 2), ACT.Copy).then_inc(xhi_ok, 1)

            def he_high(i):
                act.wait_ge(heT_up, i + 1)
                reach(act, fed2, 6 * i)
                nc.scalar.activation(he_hi.rearrange("p k n -> p (k n)"), bank(TB, 2)[:, 0:6 * P], ACT.Copy).then_inc(hehi_ok, 1)

            def y_out(i):
                act.wait_ge(fed2, 6 * (i + 1))
                reach(act, ye_out, 16 * i)
                nc.scalar.activation(y_e[:, 0:BANK], bank(YB), ACT.Copy).then_inc(ye_a, 1)

            def one_pass(i0, begun):
                for p in range(begun, 4):
                    split13(i0, p)
                x_high(i0)
                for p in range(4, KD):
                    split13(i0, p)
                silu(i0)
                x_high(i0 + 1)
                for p in range(4):
                    split13(i0 + 1, p)
                he_high(i0)

                def body(i, last=False):
                    for p in range(4, KD):
                        split13(i, p)
                    for p in range(3):
                        split2(i - 1, p)
                    silu(i)
                    x_high(i + 1)
                    for p in range(3, 6):
                        split2(i - 1, p)
                    if not last:
                        for p in range(4):
                            split13(i + 1, p)
                    y_out(i - 1)
                    he_high(i)

                body(i0 + 1)
                with act.Fori(2, EXPERTS - 2) as e:
                    body(act.snap(i0 + e))
                body(i0 + EXPERTS - 2, last=True)
                i = i0 + EXPERTS - 1
                for p in range(6):
                    split2(i - 1, p)
                for p in range(4):
                    split13(i, p)
                for p in range(4, KD):
                    split13(i, p)
                y_out(i - 1)
                for p in range(3):
                    split2(i, p)
                silu(i)
                he_high(i)
                for p in range(3, 6):
                    split2(i, p)
                y_out(i)

            one_pass(0, 4)
            over = most(act)
            with act.If(over > threshold):
                with act.Fori(1, ROUNDS) as r:
                    one_pass(act.snap(r * EXPERTS), 0)
            def root(t):
                act.wait_ge(f_mix, t + 1)
                nc.scalar.activation(result[:, t], mixed[:, t], ACT.Square, accum_out=small["fss"][:, t:t + 1]).then_inc(f_ss, 1)
                act.wait_ge(f_ss, t + 1)
                nc.scalar.activation(small["fstd"][:, t:t + 1], small["fss"][:, t:t + 1], ACT.Sqrt, scale=1.0 / D,
                                     bias=small["eps"]).then_inc(f_std, 1)

            for t in range(NT):
                act.wait_ge(back_in[t][0], 16)
                nc.scalar.activation(mixed[:, t], back[:, t, 0], ACT.Copy, scale=small["wts"][:, t:t + 1]).then_inc(f_m1, 1)
                if t >= 1:
                    root(t - 1)
            root(NT - 1)

        @block.vector
        def _(dve):
            v = nc.vector
            link = chain(dve, dve_step)
            v.memset(small["eps"], EPS).then_inc(eps_ok, 1)
            dve.wait_ge(cols_up, 1)
            link(v.tensor_copy(dwT, bank(7)[:, 128:256].rearrange("p (j n) -> p j n", j=NC)[:, :, 0:WIDTH]))
            v.tensor_copy(small["par"][:, 0:77], bank(7)[:, 0:77]).then_inc(cols_ok, 1)
            dve.wait_ge(act_step, 1)

            def ada(b):
                dve.wait_ge(ada_in[b % 4], 16 * (b // 4 + 1))
                reach(dve, ada_mm, b - 3)
                s = ada_sum[:, b % SUMS]
                link(v.tensor_scalar(s, ada_block(b)[:, 0], small["csil"][:, 0:1], None, ALU.mult))
                for k in range(1, KD):
                    ins = v.scalar_tensor_tensor(out=s, in0=ada_block(b)[:, k], scalar=small["csil"][:, k:k + 1],
                                                 in1=s, op0=ALU.mult, op1=ALU.add)
                    if k < KD - 1:
                        link(ins)
                ins.then_inc(ada_summed, 1)

            def ada_row(r):
                dve.wait_ge(ada_mm, 5 + r)
                what, h = r // 2, slice(r % 2 * BANK, (r % 2 + 1) * BANK)
                b = bank(6 + r % 2)
                if r == 0:
                    dve.wait_ge(rows_in, 96)
                if what == 0:
                    v.tensor_tensor(gate1[:, h], b, gate1[:, h], ALU.mult).then_inc(ada_taken, 1)
                elif what == 1:
                    v.tensor_copy(shift2[:, h], b).then_inc(ada_taken, 1)
                elif what == 2:
                    v.scalar_tensor_tensor(out=scale2[:, h], in0=b, scalar=1.0, in1=scale2[:, h], op0=ALU.add,
                                           op1=ALU.mult).then_inc(ada_taken, 1)
                else:
                    v.tensor_tensor(gate2[:, h], b, gate2[:, h], ALU.mult).then_inc(ada_taken, 1)

            dve.wait_ge(act_step, 1 + NT + 1)
            v.reciprocal(small["xr"], small["xstd"]).then_inc(xr_ok, 1)
            for b in range(4):
                ada(b)
            dve.wait_ge(ada_mm, 4)
            link(v.tensor_tensor(small["modc"], bank(7)[:, 0:16], small["par"][:, 0:16], ALU.add))
            link(v.tensor_copy(small["B1"], small["modc"][:, 0:8]))
            v.scalar_tensor_tensor(out=small["A1"], in0=small["modc"][:, 8:16], scalar=1.0, in1=small["par"][:, 48:56],
                                   op0=ALU.add, op1=ALU.mult).then_inc(mod1_ok, 1)
            dve.wait_ge(mod1_ok, 1)

            def h_low(k):
                dve.wait_ge(hT_a, k + 1)
                v.tensor_tensor(hT_lo[:, k], h_tmp[:, k % 2], hT_hi[:, k].bitcast(f32), ALU.subtract).then_inc(hT_v, 1)

            for k in range(KD):
                dve.wait_ge(xT_up, k + 1)
                reach(dve, hT_v, k - 1)
                v.tensor_scalar(h_tmp[:, k % 2], bank(k), small["A1"][:, k:k + 1], small["B1"][:, k:k + 1], ALU.mult,
                                ALU.add).then_inc(tmp_ok, 1)
                if k >= 1:
                    h_low(k - 1)
            h_low(KD - 1)
            link(v.memset(uT[:, :, 0:WIDTH - 1], 0.0))

            def gated(j):
                dve.wait_ge(sig_ok, j + 1)
                v.tensor_tensor(uT[:, j, WIDTH - 1:], bank(2 * PAIR["conv", j]), sig[:, j % 2], ALU.mult).then_inc(u_ok, 1)

            def taps(chunks, first, last, unroll):
                def step(j, tap):
                    acc = conv[:, j] if j < NC - 1 else part3
                    v.scalar_tensor_tensor(out=acc, in0=uT[:, j, bass.ds(tap, T)], scalar=dwT[:, j, bass.ds(tap, 1)],
                                           in1=acc, op0=ALU.mult, op1=ALU.add).then_inc(tap_ok[j], 1)

                for j in chunks:
                    if first > TAP0[j]:
                        dve.wait_ge(tap_ok[j], first - TAP0[j])
                        step(j, first)
                    elif j < NC - 1:
                        dve.wait_ge(u_ok, j + 1)
                        v.tensor_scalar(conv[:, j], uT[:, j, 0:T], dwT[:, j, 0:1], small["par"][:, 64 + j:65 + j], ALU.mult,
                                        ALU.add).then_inc(tap_ok[j], 1)
                    else:
                        dve.wait_ge(u_ok, j + 1)
                        v.tensor_scalar(part3, uT[:, j, SHARED:SHARED + T], dwT[:, j, SHARED:SHARED + 1], None,
                                        ALU.mult).then_inc(tap_ok[j], 1)
                assert (last - 1 - first) % unroll == 0
                with dve.Fori(0, (last - 1 - first) // unroll) as turn:
                    n = dve.snap(turn * unroll + 1)
                    for m in range(unroll):
                        for j in chunks:
                            dve.wait_ge(tap_ok[j], n + (first - TAP0[j] + m))
                            step(j, n + (first + m))

            ada(4)
            ada(5)
            gated(0)
            ada(6)
            gated(1)
            ada(7)
            ada_row(0)
            ada(8)
            ada_row(1)
            ada_row(2)
            gated(2)
            ada(9)
            ada(10)
            ada_row(3)
            ada_row(4)
            gated(3)
            ada(11)
            ada_row(5)
            taps(range(NC - 1), 0, 9, 4)
            ada_row(6)
            ada_row(7)
            taps(range(NC - 1), 9, SHARED, 1)
            taps(range(NC), SHARED, 25, 1)
            dve.wait_ge(decay_ok, 1)
            for n in range(NCH):
                dve.wait_ge(upd_mm, n + 1)
                u = bank(6 + n % 2)
                for p in range(2):
                    for h in range(2):
                        rows = slice(h * DK, (h + 1) * DK)
                        src = u[rows, p * QK + h * DV:p * QK + (h + 1) * DV]
                        if n == 0:
                            v.tensor_copy(state[rows, n, p], src).then_inc(state_ok, 1)
                        else:
                            dve.wait_ge(state_ok, 4 * (n - 1) + 2 * p + h + 1)
                            v.scalar_tensor_tensor(out=state[rows, n, p], in0=state[rows, n - 1, p],
                                                   scalar=small["decay"][rows, p * NCH + n:p * NCH + n + 1], in1=src,
                                                   op0=ALU.mult, op1=ALU.add).then_inc(state_ok, 1)

            def y_low(n):
                k = GLA_FIRST[n]
                dve.wait_ge(yhi_ok, n + 1)
                src, hi, lo = (conv, conv_hi, conv_lo) if k < NC else (gT, g_hi, g_lo)
                v.tensor_tensor(lo[:, k % NC], src[:, k % NC], hi[:, k % NC].bitcast(f32), ALU.subtract).then_inc(ylo_ok, 1)

            taps(range(NC), 25, WIDTH, 1)
            dve.wait_ge(term_added, SHARED - 1)
            dve.wait_ge(tap_ok[NC - 1], WIDTH - SHARED)
            v.tensor_tensor(conv[:, NC - 1], conv[:, NC - 1], part3, ALU.add).then_inc(tap_ok[NC - 1], 1)

            def diagonal(h):
                v.tensor_tensor(o_std[:, h % 2].rearrange("p (t n) -> p t n", t=NT), ident.unsqueeze(1).broadcast_to((P, NT, P)),
                                small["or"][:, NT * h:NT * (h + 1)].unsqueeze(2).broadcast_to((P, NT, P)), ALU.mult).then_inc(diag_ok, 1)

            dve.wait_ge(ostd_ok, 1)
            link(v.reciprocal(small["or"], small["ostd"]))
            diagonal(0)
            diagonal(1)
            dve.wait_ge(mean_mm, 1)
            for j in range(NC):
                v.scalar_tensor_tensor(out=conv[:, j], in0=bank(7), scalar=-1.0 / CONV, in1=conv[:, j], op0=ALU.mult,
                                       op1=ALU.add).then_inc(cent_ok, 1)
            for h in range(HEADS):
                dve.wait_ge(unit_ok, 6 + h // 2)
                dve.wait_ge(spread_mm, h + 1)
                link(v.tensor_tensor(gT[:, h], bank(6 + h % 2), gT[:, h], ALU.mult))
                if h < HEADS - 2:
                    diagonal(h + 2)
                v.scalar_tensor_tensor(out=gT[:, h], in0=bank(O_BANK[h]), scalar=small["par"][:, 76:77], in1=gT[:, h],
                                       op0=ALU.mult, op1=ALU.mult).then_inc(ygla_ok, 1)
            for n in range(HEADS):
                y_low(n)
            dve.wait_ge(cstd_ok, 1)
            link(v.reciprocal(o_sq[:, 0], o_sq[:, 0]))
            dve.wait_ge(cent_ok, NC)
            for j in range(NC):
                v.tensor_tensor(conv[:, j], conv[:, j], o_sq[:, 0], ALU.mult).then_inc(cnorm_ok, 1)
            for n in range(HEADS, KD):
                y_low(n)

            def h2T_out(t):
                dve.wait_ge(h2T_up, t + 1)
                v.tensor_copy(h2T[:, TILE[t], 4:KD].rearrange("p k n -> p (k n)"), bank(2 * t + 1)).then_inc(h2T_v, 1)

            for t in range(NT):
                dve.wait_ge(ystd_ok, t + 1)
                link(v.reciprocal(small["yr"][:, t:t + 1], small["ystd"][:, t:t + 1]))
                v.scalar_tensor_tensor(out=y_tmp, in0=bank(2 * t, 2), scalar=small["yr"][:, t:t + 1], in1=gate1,
                                       op0=ALU.mult, op1=ALU.mult).then_inc(x2_ok, 1)
                dve.wait_ge(x2_ok, 2 * t + 1)
                dve.wait_ge(x_again[t // 2], 16)
                v.tensor_tensor(x2[:, t], x2[:, t], y_tmp, ALU.add).then_inc(x2_ok, 1)
                dve.wait_ge(x2std_ok, t + 1)
                link(v.reciprocal(small["x2r"][:, t:t + 1], small["x2std"][:, t:t + 1]))
                link(v.scalar_tensor_tensor(out=h2[:, t], in0=x2[:, t], scalar=small["x2r"][:, t:t + 1], in1=scale2,
                                            op0=ALU.mult, op1=ALU.mult))
                v.tensor_tensor(h2[:, t], h2[:, t], shift2, ALU.add).then_inc(h2_ok, 1)
            h2T_out(NT - 1)

            for t in range(NT):
                dve.wait_ge(logT_mm, t + 1)
                v.tensor_copy(logT[:, t * P:(t + 1) * P], bank(2 * t + 1)[0:EXPERTS, 0:P]).then_inc(logT_ok, 1)

            dve.wait_ge(logit_mm, NT)
            E4 = (P, NT, EXPERTS)
            lg = psum.rearrange("p (t e) -> p t e", t=NT)[:, :, 0:EXPERTS]
            wide = lambda a: a.unsqueeze(2).broadcast_to(E4)
            link(v.tensor_reduce(R["a"], lg, AX.X, ALU.max))
            v.tensor_tensor(R["sh"], lg, wide(R["a"]), ALU.subtract).then_inc(exp_in, 1)
            dve.wait_ge(exp_ok, 1)
            link(v.tensor_reduce(R["a"], R["p"], AX.X, ALU.add))
            link(v.reciprocal(R["a"], R["a"]))
            link(v.tensor_tensor(R["p"], R["p"], wide(R["a"]), ALU.mult))
            link(v.tensor_tensor(R["sel"], R["p"], small["brow"].unsqueeze(1).broadcast_to(E4), ALU.add))
            s4 = R["sel"].rearrange("p t (g i) -> p (t g) i", i=4)
            q = [R["q"][:, i] for i in range(4)]
            link(v.tensor_tensor(q[0], s4[:, :, 0], s4[:, :, 1], ALU.max))
            link(v.tensor_tensor(q[1], s4[:, :, 0], s4[:, :, 1], ALU.min))
            link(v.tensor_tensor(q[2], s4[:, :, 2], s4[:, :, 3], ALU.max))
            link(v.tensor_tensor(q[3], s4[:, :, 2], s4[:, :, 3], ALU.min))
            link(v.tensor_tensor(q[1], q[1], q[3], ALU.max))
            link(v.tensor_tensor(q[3], q[0], q[2], ALU.min))
            link(v.tensor_tensor(q[0], q[0], q[2], ALU.max))
            link(v.tensor_tensor(q[1], q[1], q[3], ALU.max))
            link(v.tensor_tensor(q[0], q[0], q[1], ALU.add))
            gs = q[0].rearrange("p (t g) -> p t g", g=GROUPS)
            gm = q[1].rearrange("p (t g) -> p t g", g=GROUPS)
            G4 = (P, NT, GROUPS)
            link(v.tensor_reduce(R["a"], gs, AX.X, ALU.max))
            link(v.tensor_tensor(gm, gs, R["a"].unsqueeze(2).broadcast_to(G4), ALU.is_ge))
            link(v.tensor_tensor(gm, gm, small["gkey"].unsqueeze(1).broadcast_to(G4), ALU.mult))
            link(v.tensor_reduce(R["a"], gm, AX.X, ALU.max))
            link(v.tensor_tensor(gm, gm, R["a"].unsqueeze(2).broadcast_to(G4), ALU.is_equal))
            gw = q[1].unsqueeze(2).broadcast_to((P, NT * GROUPS, 4))
            link(v.tensor_tensor(s4, s4, gw, ALU.mult))
            link(v.tensor_scalar(q[1], q[1], -1.0, BIG, ALU.add, ALU.mult))
            link(v.tensor_tensor(s4, s4, gw, ALU.add))
            for k in range(2):
                hot = R["hot"][k]
                link(v.tensor_reduce(R["a"], R["sel"], AX.X, ALU.max))
                link(v.tensor_tensor(hot, R["sel"], wide(R["a"]), ALU.is_ge))
                link(v.tensor_tensor(hot, hot, small["key"].unsqueeze(1).broadcast_to(E4), ALU.mult))
                link(v.tensor_reduce(R["kmax"][:, k], hot, AX.X, ALU.max))
                link(v.tensor_tensor(hot, hot, wide(R["kmax"][:, k]), ALU.is_equal))
                if k == 0:
                    link(v.scalar_tensor_tensor(out=R["sel"], in0=hot, scalar=-3.0 * BIG, in1=R["sel"], op0=ALU.mult, op1=ALU.add))
            v.tensor_tensor(R["mask"], R["hot"][0], R["hot"][1], ALU.add).then_inc(mask_ok, 1)
            for k in range(2):
                link(v.tensor_tensor(R["sel"], R["p"], R["hot"][k], ALU.mult))
                link(v.tensor_reduce(R["w"][:, k], R["sel"], AX.X, ALU.add))
            link(v.tensor_tensor(R["a"], R["w"][:, 0], R["w"][:, 1], ALU.add))
            link(v.reciprocal(R["a"], R["a"]))
            wts = small["wts"].rearrange("p (k t) -> p k t", k=2)
            link(v.tensor_tensor(wts, R["w"], R["a"].unsqueeze(1).broadcast_to((P, 2, NT)), ALU.mult))
            dve.wait_ge(rank_mm, 1)
            rank = bank(1)[:, 0:NT * EXPERTS].rearrange("p (t e) -> p t e", t=NT)
            for k in range(2):
                link(v.tensor_tensor(R["sel"], rank, R["hot"][k], ALU.mult))
                link(v.tensor_reduce(R["w"][:, k], R["sel"], AX.X, ALU.add))
            link(v.scalar_tensor_tensor(out=R["w"], in0=R["w"], scalar=float(EXPERTS), in1=R["kmax"], op0=ALU.mult, op1=ALU.subtract))
            link(v.tensor_scalar(pos.rearrange("p (k t) -> p k t", k=2), R["w"], float(EXPERTS), None, ALU.add))
            link(v.tensor_reduce(R["a"][:, 0:1], bank(1)[:, NT * EXPERTS:(NT + 1) * EXPERTS], AX.X, ALU.max))
            v.tensor_copy(count, R["a"][:, 0:1]).then_inc(pos_ok, 1)

            def split13(i, p):
                dve.wait_ge(hi13_ok, KD * i + p + 1)
                v.tensor_tensor(lo13[:, p % 4], raw13[:, p], hi13[:, p % 4].bitcast(f32), ALU.subtract).then_inc(lo13_ok, 1)

            def split2(i, p):
                dve.wait_ge(hi2_ok, 6 * i + p + 1)
                n = P if p < FULL else LAST
                v.tensor_tensor(lo2[0:n, p % 3], raw2[0:n, p], hi2[0:n, p % 3].bitcast(f32), ALU.subtract).then_inc(lo2_ok, 1)

            def gate(i):
                dve.wait_ge(silu_ok, i + 1)
                reach(dve, heT_up, i)
                v.tensor_tensor(he[:, 0:F].rearrange("p (b n) -> p b n", b=2), s_act.rearrange("p (b n) -> p b n", b=2), H3,
                                ALU.mult).then_inc(he_ok, 1)

            def x_low(i):
                dve.wait_ge(xhi_ok, i + 1)
                v.tensor_tensor(x_lo.rearrange("p k n -> p (k n)"), bank(TB, 2), x_hi.rearrange("p k n -> p (k n)").bitcast(f32),
                                ALU.subtract).then_inc(xlo_ok, 1)

            def he_low(i):
                dve.wait_ge(hehi_ok, i + 1)
                v.tensor_tensor(he_lo.rearrange("p k n -> p (k n)"), bank(TB, 2)[:, 0:6 * P],
                                he_hi.rearrange("p k n -> p (k n)").bitcast(f32), ALU.subtract).then_inc(helo_ok, 1)

            def y_out(i):
                dve.wait_ge(fed2, 6 * (i + 1))
                reach(dve, ye_out, 16 * i)
                v.tensor_copy(y_e[:, BANK:], bank(YB + 1)).then_inc(ye_v, 1)

            def one_pass(i0, begun):
                for p in range(begun, 4):
                    split13(i0, p)
                x_low(i0)
                reach(dve, lo13_ok, begun)
                for p in range(4, KD):
                    split13(i0, p)
                gate(i0)
                x_low(i0 + 1)
                for p in range(4):
                    split13(i0 + 1, p)
                he_low(i0)

                def body(i, last=False):
                    for p in range(4, KD):
                        split13(i, p)
                    for p in range(3):
                        split2(i - 1, p)
                    gate(i)
                    x_low(i + 1)
                    for p in range(3, 6):
                        split2(i - 1, p)
                    if not last:
                        for p in range(4):
                            split13(i + 1, p)
                    y_out(i - 1)
                    he_low(i)

                body(i0 + 1)
                with dve.Fori(2, EXPERTS - 2) as e:
                    body(dve.snap(i0 + e))
                body(i0 + EXPERTS - 2, last=True)
                i = i0 + EXPERTS - 1
                for p in range(6):
                    split2(i - 1, p)
                for p in range(4):
                    split13(i, p)
                for p in range(4, KD):
                    split13(i, p)
                y_out(i - 1)
                for p in range(3):
                    split2(i, p)
                gate(i)
                he_low(i)
                for p in range(3, 6):
                    split2(i, p)
                y_out(i)

            link(v.memset(he[:, F:], 0.0))
            one_pass(0, 4)
            over = most(dve)
            with dve.If(over > threshold):
                with dve.Fori(1, ROUNDS) as r:
                    one_pass(dve.snap(r * EXPERTS), 0)
            def mix(t):
                dve.wait_ge(back_in[t][1], 16)
                dve.wait_ge(f_m1, t + 1)
                v.scalar_tensor_tensor(out=mixed[:, t], in0=back[:, t, 1], scalar=small["wts"][:, NT + t:NT + t + 1],
                                       in1=mixed[:, t], op0=ALU.mult, op1=ALU.add).then_inc(f_mix, 1)

            mix(0)
            for t in range(NT):
                if t + 1 < NT:
                    mix(t + 1)
                dve.wait_ge(f_std, t + 1)
                v.reciprocal(small["fr"][:, t:t + 1], small["fstd"][:, t:t + 1]).then_inc(f_r, 1)
                dve.wait_ge(f_r, 2 * t + 1)
                v.scalar_tensor_tensor(out=result[:, t], in0=mixed[:, t], scalar=small["fr"][:, t:t + 1], in1=gate2,
                                       op0=ALU.mult, op1=ALU.mult).then_inc(f_r, 1)
                if t >= 2:
                    dve.wait_ge(f_r, 2 * t + 2)
                    v.tensor_tensor(result[:, t], result[:, t], x2[:, t], ALU.add).then_inc(f_ok, 1)

        @block.tensor
        def _(pe):
            mm = nc.tensor.matmul
            pe.wait_ge(consts, 10)
            pe.wait_ge(par_in, 16 * 8)
            nc.tensor.transpose(bank(7)[:, 0:77], par_rows, ident[0:77, 0:77])
            for j in range(NC):
                last = nc.tensor.transpose(bank(7)[:, 128 + 32 * j:128 + 32 * j + WIDTH], dw_rows[:, j * P:(j + 1) * P],
                                           ident[0:WIDTH, 0:WIDTH])
            last.then_inc(cols_up, 1)

            def x_up(k):
                for t in range(NT):
                    if k == 0:
                        pe.wait_ge(xhat_ok, t + 1)
                    last = nc.tensor.transpose(bank(k)[:, t * P:(t + 1) * P], xhat[:, t, k * P:(k + 1) * P], ident)
                last.then_inc(xT_up, 1)

            pe.wait_ge(cols_ok, 1)
            for k in range(KD - 1):
                x_up(k)
            for b in range(4):
                pe.wait_ge(ada_summed, b + 1)
                for j in range(4):
                    last = mm(bank(7)[:, 4 * b + j:4 * b + j + 1], ada_sum[:, b % SUMS, j * P:(j + 1) * P], ones[:, 0:1],
                              start=True, stop=True)
                last.then_inc(ada_mm, 1)
            pe.wait_ge(mod1_ok, 1)
            x_up(KD - 1)

            def ada_row(r):
                pe.wait_ge(biased, r + 1)
                reach(pe, ada_taken, r - 1)
                mm(bank(6 + r % 2), ones, ada_sum[:, r % SUMS], start=True, stop=True).then_inc(ada_mm, 1)

            def product(u, rows=()):
                what, i, _ = UNITS[u]
                b, s = 2 * PAIR[what, i], u % 2
                rows = list(rows)
                pe.wait_ge(wi_hi_ok, u + 1)
                if what == "kv":
                    pe.wait_ge(wi_lo_ok, u + 1)
                    for t in range(NT):
                        for k in range(KD):
                            for n, (h, w) in enumerate(((hT_hi, wi_hi), (hT_hi, wi_lo), (hT_lo, wi_hi))):
                                last = mm(bank(b, 2)[:, t * QK:(t + 1) * QK], h[:, k, t * P:(t + 1) * P], w[:, s, k],
                                          start=k == 0 and n == 0, stop=k == KD - 1 and n == 2)
                        if t == 1 and rows:
                            ada_row(rows.pop(0))
                else:
                    for m in range(2):
                        cols = slice(m * P, (m + 1) * P)
                        for k in range(KD):
                            if u == 0:
                                pe.wait_ge(hT_v, k + 1)
                            mm(bank(b + m), wi_hi[:, s, k, cols], hT_hi[:, k], start=k == 0, stop=False)
                            mm(bank(b + m), wi_hi[:, s, k, cols], hT_lo[:, k], start=False, stop=False)
                        pe.wait_ge(wi_lo_ok, u + 1)
                        for k in range(KD):
                            last = mm(bank(b + m), wi_lo[:, s, k, cols], hT_hi[:, k], start=False, stop=k == KD - 1)
                        if m == 0 and u == NU - 1:
                            sums()
                        if m == 0 and rows:
                            ada_row(rows.pop(0))
                last.then_inc(unit_mm, 1)
                for r in rows:
                    ada_row(r)

            product(0)
            product(1)
            ada_row(0)
            product(2, (1, 2))
            pe.wait_ge(u_ok, 1)
            product(3, (3, 4))
            pe.wait_ge(u_ok, 2)
            pe.wait_ge(lrw_ok, 2)
            for k in range(KD):
                for n, (h, w) in enumerate(((hT_hi, lr_hi), (hT_hi, lr_lo), (hT_lo, lr_hi))):
                    last = mm(bank(2 * PAIR["lr"]), w[:, k], h[:, k], start=k == 0 and n == 0, stop=k == KD - 1 and n == 2)
            last.then_inc(lr_mm, 1)
            pe.wait_ge(u_ok, 3)
            product(4, (5, 6))
            pe.wait_ge(u_ok, 4)
            product(5, (7,))
            pe.wait_ge(rows_in, 96)
            pe.wait_ge(unit_ok, 2)
            for t in range(NT):
                last = mm(bank(2 * PAIR["z"], 2)[:, t * QK:(t + 1) * QK], lrT[:, t * P:(t + 1) * P], w_up, start=True, stop=True)
            last.then_inc(z_mm, 1)
            product(6)
            pe.wait_ge(soft_ok, 1)
            for t in range(NT):
                last = mm(bank(2 * PAIR["later"], 2)[:, t * QK:(t + 1) * QK], later, soft_l[:, t], start=True, stop=True)
            pe.wait_ge(ada_taken, 8)
            for t in range(NT):
                for p in range(2):
                    last = mm(bank(6)[:, p * NCH + 2 * t:p * NCH + 2 * t + 2], soft_l[:, t, p * P:(p + 1) * P], small["half"],
                              start=True, stop=True)
            last.then_inc(later_mm, 1)
            pe.wait_ge(unit_ok, 3)
            product(7)
            pe.wait_ge(unit_ok, 4)
            product(8)
            pe.wait_ge(decay_ok, 1)
            pe.wait_ge(kdec_ok, 2)
            for n in range(NCH):
                reach(pe, state_ok, 4 * (n - 1))
                for p in range(2):
                    last = mm(bank(6 + n % 2)[:, p * QK:(p + 1) * QK], k_dec[:, n // 2, n % 2, p * P:(p + 1) * P],
                              kv[:, n // 2, QK + p * QK:QK + (p + 1) * QK], start=True, stop=True)
                last.then_inc(upd_mm, 1)
            pe.wait_ge(unit_ok, 5)
            for h in range(HEADS):
                rows = slice(h % 2 * DK, (h % 2 + 1) * DK)
                for n in range(NCH):
                    pe.wait_ge(state_ok, 4 * n + 4)
                    last = mm(bank(O_BANK[h])[:, n * CHUNK:(n + 1) * CHUNK], state[rows, n, h // 2],
                              qT[rows, h // 2, n * CHUNK:(n + 1) * CHUNK], start=True, stop=True)
                last.then_inc(o_mm, 1)

            def head_sums():
                for h in range(HEADS):
                    pe.wait_ge(osq_ok, h + 1)
                    for t in range(NT):
                        last = mm(bank(6)[:, NT * h + t:NT * h + t + 1], head_sq[:, h, t * P:(t + 1) * P], ones[:, 0:1],
                                  start=True, stop=True)
                    last.then_inc(osum_mm, 1)

            def spread(h):
                pe.wait_ge(diag_ok, h + 1)
                reach(pe, ygla_ok, h - 1)
                mm(bank(6 + h % 2), ones, o_std[:, h % 2], start=True, stop=True).then_inc(spread_mm, 1)

            def sums():
                head_sums()
                for j in range(NC):
                    pe.wait_ge(tap_ok[j], WIDTH if j < NC - 1 else WIDTH - SHARED + 1)
                    last = mm(bank(7), ones, conv[:, j], start=j == 0, stop=j == NC - 1)
                last.then_inc(mean_mm, 1)
                spread(0)

            pe.wait_ge(unit_ok, 6)
            product(9)

            def y_part(t, part):
                for n, k in enumerate(GLA_FIRST):
                    if n // NC != part:
                        continue
                    if t == 0:
                        pe.wait_ge(ylo_ok, n + 1)
                        pe.wait_ge(wo_lo_ok, n + 1)
                    hi, lo = (conv_hi, conv_lo) if k < NC else (g_hi, g_lo)
                    for m, (y, w) in enumerate(((hi, wo_hi), (hi, wo_lo), (lo, wo_hi))):
                        for h in range(2):
                            last = mm(bank(2 * t + h), y[:, k % NC, t * P:(t + 1) * P], w[:, k, h * BANK:(h + 1) * BANK],
                                      start=n == 0 and m == 0, stop=n == KD - 1 and m == 2)
                return last

            pe.wait_ge(cent_ok, NC)
            spread(1)
            spread(2)
            spread(3)
            pe.wait_ge(unit_ok, 7)
            for j in range(NC):
                pe.wait_ge(csq_ok, j + 1)
                mm(bank(3), ones, o_sq[:, j % 2], start=j == 0, stop=j == NC - 1).then_inc(var_mm, 1)
            pe.wait_ge(ygla_ok, HEADS)
            for t in (0, 2, 3):
                y_part(t, 0)
            y_part(0, 1).then_inc(y_mm, 1)
            pe.wait_ge(cstd_ok, 1)
            y_part(1, 0)
            for t in range(1, NT):
                y_part(t, 1).then_inc(y_mm, 1)
            def turn_h2(t):
                pe.wait_ge(h2_ok, t + 1)
                for k in range(KD):
                    last = nc.tensor.transpose(bank(2 * t, 2)[:, k * P:(k + 1) * P], h2[:, t, k * P:(k + 1) * P], ident)
                last.then_inc(h2T_up, 1)

            def logits(t):
                pe.wait_ge(h2T_a, t + 1)
                if t == NT - 1:
                    pe.wait_ge(h2T_v, 1)
                for k in range(KD):
                    last = mm(bank(2 * t + 1)[0:EXPERTS, 0:P], w_r[:, k], h2T[:, TILE[t], k], start=k == 0, stop=k == KD - 1)
                last.then_inc(logT_mm, 1)

            pe.wait_ge(w_r_in, 16)
            turn_h2(0)
            turn_h2(1)
            turn_h2(2)
            logits(0)
            logits(1)
            logits(2)
            turn_h2(3)
            logits(3)
            for t in range(NT):
                pe.wait_ge(logT_ok, t + 1)
                nc.tensor.transpose(bank(2 * t)[:, 0:EXPERTS], logT[:, t * P:(t + 1) * P], ident[0:EXPERTS, 0:EXPERTS]).then_inc(logit_mm, 1)
            pe.wait_ge(mask_ok, 1)
            for t in range(NT):
                dst = bank(1)[:, t * EXPERTS:(t + 1) * EXPERTS]
                mm(dst, before, R["mask"][:, t], start=True, stop=t == 0)
                for s in range(t):
                    mm(dst, ones_b, R["mask"][:, s], start=False, stop=s == t - 1)
            for s in range(NT):
                last = mm(bank(1)[:, NT * EXPERTS:(NT + 1) * EXPERTS], ones_b, R["mask"][:, s], start=s == 0, stop=s == NT - 1)
            last.then_inc(rank_mm, 1)

            def turn_x(i):
                pe.wait_ge(xe_in, 16 * (i + 1))
                reach(pe, helo_ok, i - 1)
                for k in range(KD):
                    last = nc.tensor.transpose(bank(TB, 2)[:, k * P:(k + 1) * P], xe[:, k * P:(k + 1) * P], ident)
                last.then_inc(xeT_up, 1)

            def first(i):
                pe.wait_ge(xlo_ok, i + 1)
                reach(pe, he_ok, i)
                for p in range(KD):
                    pe.wait_ge(lo13_ok, KD * i + p + 1)
                    for n, (s, w) in enumerate(((x_hi, hi13), (x_hi, lo13), (x_lo, hi13))):
                        for b in range(4):
                            last = mm(bank(b)[:, 0:F2], s[:, p], w[:, p % 4, b * F2:(b + 1) * F2],
                                      start=p == 0 and n == 0, stop=p == KD - 1 and n == 2)
                    last.then_inc(fed13, 1)

            def second(i):
                reach(pe, helo_ok, i + 1)
                reach(pe, ye_a, i)
                reach(pe, ye_v, i)
                for p in range(6):
                    pe.wait_ge(lo2_ok, 6 * i + p + 1)
                    n_ = P if p < FULL else LAST
                    for n, (s, w) in enumerate(((he_hi, hi2), (he_hi, lo2), (he_lo, hi2))):
                        for b in range(2):
                            last = mm(bank(YB + b), s[0:n_, p], w[0:n_, p % 3, b * BANK:(b + 1) * BANK],
                                      start=p == 0 and n == 0, stop=p == 5 and n == 2)
                    last.then_inc(fed2, 1)

            def turn_he(i, last=False):
                pe.wait_ge(he_ok, i + 1)
                pe.wait_ge(xlo_ok, i + 1 if last else i + 2)
                for k in range(6):
                    turned = nc.tensor.transpose(bank(TB, 2)[:, k * P:(k + 1) * P], he[:, k * P:(k + 1) * P], ident)
                turned.then_inc(heT_up, 1)

            def one_pass(i0):
                turn_x(i0)
                first(i0)
                turn_x(i0 + 1)
                turn_he(i0)
                with pe.Fori(1, EXPERTS - 1) as e:
                    i = pe.snap(i0 + e)
                    first(i)
                    turn_x(i + 1)
                    second(i - 1)
                    turn_he(i)
                i = i0 + EXPERTS - 1
                second(i - 1)
                first(i)
                turn_he(i, last=True)
                second(i)

            one_pass(0)
            over = most(pe)
            with pe.If(over > threshold):
                with pe.Fori(1, ROUNDS) as r:
                    one_pass(pe.snap(r * EXPERTS))


def kernel(**inputs):
    import numpy as np
    import concourse.bacc as bacc
    from concourse.bass_utils import run_bass_kernel_spmd

    nc = bacc.Bacc("TRN2", target_bir_lowering=False, num_devices=1)
    arrays, args = {}, {}
    for name in ("x", "c", "w_ada", "b_ada", "g_pre_mix", "g_post_mix", "g_pre_ffn", "g_post_ffn", "w_in", "w_dw",
                 "b_dw", "conv_ln_g", "conv_ln_b", "w_gate_up", "b_gate", "gla_norm_g", "w_out", "w_router",
                 "b_router", "w1", "w3", "w2"):
        a = np.ascontiguousarray(inputs[name])
        arrays[f"in_{name}"] = a
        args[name] = nc.dram_tensor(f"in_{name}", a.shape, mybir.dt.from_np(a.dtype), kind="ExternalInput").ap()
    out = nc.dram_tensor("out", (1, T, D), mybir.dt.float32, kind="ExternalOutput").ap()
    build(nc, out=out, **args)
    result = run_bass_kernel_spmd(nc, [arrays], core_ids=[0])
    return result.results[0]["out"]
```
